# Optimizing a Trainium2 kernel written in Bass

```python
import math
import jax, jax.numpy as jnp
from jax import lax
import numpy as np

D_MODEL = 1024
BATCH = 1
SEQ = 512
DEPTH = 2

N_MIXERS = 2
HEAD_DIM_A = 64
DIL_GROUPS = ((128, 1), (512, 4), (2048, 16))
HEADS_PER_GROUP_A = 6
N_HEADS_A = HEADS_PER_GROUP_A * len(DIL_GROUPS)
WIDTH_A = N_HEADS_A * HEAD_DIM_A
N_BUCKETS = 32
T5_MAX_DISTANCE = 1024
N_HEADS_B = 16
QK_NOPE_DIM = 64
QK_ROPE_DIM = 32
V_HEAD_DIM = 64
Q_LORA_RANK = 256
KV_LORA_RANK = 128
WIDTH_B = N_HEADS_B * V_HEAD_DIM
IN_B = Q_LORA_RANK + KV_LORA_RANK + QK_ROPE_DIM + WIDTH_B
ROPE_THETA = 10000.0
Q_BLOCK = 128
DEPTH_A = (DEPTH + N_MIXERS - 1) // N_MIXERS
DEPTH_B = DEPTH // N_MIXERS
DEEPNORM_ALPHA = (2.0 * DEPTH) ** 0.25
DEEPNORM_BETA = (8.0 * DEPTH) ** -0.25
LN_EPS = 1e-5
RMS_EPS = 1e-6
NEG_INF = -1e30


def layernorm(x, g, b):
    xf = x.astype(jnp.float32)
    mu = xf.mean(-1, keepdims=True)
    var = jnp.square(xf - mu).mean(-1, keepdims=True)
    return ((xf - mu) * lax.rsqrt(var + LN_EPS) * g.astype(jnp.float32) + b.astype(jnp.float32)).astype(x.dtype)

def rmsnorm(x, g):
    xf = x.astype(jnp.float32)
    return (xf * lax.rsqrt(jnp.square(xf).mean(-1, keepdims=True) + RMS_EPS) * g.astype(jnp.float32)).astype(x.dtype)

def t5_bucket(rel):
    half = N_BUCKETS // 2
    max_exact = half // 2
    base = jnp.where(rel > 0, half, 0)
    n = jnp.abs(rel)
    nf = jnp.maximum(n, 1).astype(jnp.float32)
    large = max_exact + (jnp.log(nf / max_exact) / math.log(T5_MAX_DISTANCE / max_exact)
                         * (half - max_exact)).astype(jnp.int32)
    large = jnp.minimum(large, half - 1)
    return base + jnp.where(n < max_exact, n, large)

def dilated_window_attention(q, k, v, bias_table, window, dil):
    B, S, H, Dh = q.shape
    R = window // (2 * dil)
    L = S // dil
    nb = -(-L // R)
    Lp = nb * R

    def to_sub(t):
        return t.reshape(B, L, dil, H, Dh).transpose(0, 2, 3, 1, 4)

    qs = jnp.pad(to_sub(q), ((0, 0), (0, 0), (0, 0), (0, Lp - L), (0, 0))).reshape(B, dil, H, nb, R, Dh)

    def key_blocks(t):
        tp = jnp.pad(to_sub(t), ((0, 0), (0, 0), (0, 0), (R, Lp - L + R), (0, 0))).reshape(B, dil, H, nb + 2, R, Dh)
        return jnp.concatenate([tp[:, :, :, :-2], tp[:, :, :, 1:-1], tp[:, :, :, 2:]], axis=4)

    kb = key_blocks(k)
    vb = key_blocks(v)
    a = jnp.arange(R)[:, None]
    bk = jnp.arange(3 * R)[None, :]
    off = bk - R - a
    kpos = jnp.arange(nb)[:, None, None] * R + bk[None] - R
    valid = (jnp.abs(off) <= R)[None] & (kpos >= 0) & (kpos < L)
    bias = bias_table[t5_bucket(off * dil)].transpose(2, 0, 1).astype(jnp.float32)

    s = jnp.einsum('bdhnqe,bdhnke->bdhnqk', qs, kb).astype(jnp.float32) * (Dh ** -0.5) + bias[:, None]
    s = jnp.where(valid, s, NEG_INF)
    m = s.max(-1, keepdims=True)
    p = jnp.exp(s - m)
    denom = p.sum(-1, keepdims=True)
    o = jnp.einsum('bdhnqk,bdhnke->bdhnqe', p, vb.astype(jnp.float32)) / denom
    lse = (m + jnp.log(denom))[..., 0]

    def from_sub(t):
        t = t.reshape(B, dil, H, Lp, *t.shape[5:])[:, :, :, :L]
        t = jnp.moveaxis(t, 3, 1)
        return t.reshape(B, S, H, *t.shape[4:])

    return from_sub(o).astype(q.dtype), from_sub(lse)

def mixer_dilated(u, w_in, w_out, rel_bias):
    B, S, _ = u.shape
    q, k, v, gate = jnp.split(u @ w_in, 4, axis=-1)
    q = q.reshape(B, S, N_HEADS_A, HEAD_DIM_A)
    k = k.reshape(B, S, N_HEADS_A, HEAD_DIM_A)
    v = v.reshape(B, S, N_HEADS_A, HEAD_DIM_A)
    outs, lses = [], []
    for g, (window, dil) in enumerate(DIL_GROUPS):
        hs = slice(g * HEADS_PER_GROUP_A, (g + 1) * HEADS_PER_GROUP_A)
        o, l = dilated_window_attention(q[:, :, hs], k[:, :, hs], v[:, :, hs], rel_bias[:, hs], window, dil)
        outs.append(o)
        lses.append(l)
    wts = jax.nn.softmax(jnp.stack(lses, axis=0), axis=0).astype(u.dtype)
    o = jnp.concatenate([outs[g] * wts[g][..., None] for g in range(len(DIL_GROUPS))], axis=2)
    y = o.reshape(B, S, WIDTH_A) * jax.nn.silu(gate)
    return y @ w_out

def rope(x, cos, sin):
    half = x.shape[-1] // 2
    x1, x2 = x[..., :half], x[..., half:]
    return jnp.concatenate([x1 * cos - x2 * sin, x2 * cos + x1 * sin], axis=-1)

def mixer_mla(u, w_in, q_norm, w_uq, kv_norm, w_ukv, w_out):
    B, S, _ = u.shape
    cq, ckv, k_rope, gate = jnp.split(
        u @ w_in, [Q_LORA_RANK, Q_LORA_RANK + KV_LORA_RANK, Q_LORA_RANK + KV_LORA_RANK + QK_ROPE_DIM], axis=-1)
    q = (rmsnorm(cq, q_norm) @ w_uq).reshape(B, S, N_HEADS_B, QK_NOPE_DIM + QK_ROPE_DIM)
    q_nope, q_rope = q[..., :QK_NOPE_DIM], q[..., QK_NOPE_DIM:]
    kv = (rmsnorm(ckv, kv_norm) @ w_ukv).reshape(B, S, N_HEADS_B, QK_NOPE_DIM + V_HEAD_DIM)
    k_nope, v = kv[..., :QK_NOPE_DIM], kv[..., QK_NOPE_DIM:]

    pos = jnp.arange(S, dtype=jnp.float32)
    inv_freq = ROPE_THETA ** (-jnp.arange(0, QK_ROPE_DIM, 2, dtype=jnp.float32) / QK_ROPE_DIM)
    ang = pos[:, None] * inv_freq[None, :]
    cos, sin = jnp.cos(ang).astype(u.dtype), jnp.sin(ang).astype(u.dtype)
    q_rope = rope(q_rope, cos[:, None], sin[:, None])
    k_rope = rope(k_rope, cos, sin)

    scale = (QK_NOPE_DIM + QK_ROPE_DIM) ** -0.5
    nq = S // Q_BLOCK
    qn_b = q_nope.reshape(B, nq, Q_BLOCK, N_HEADS_B, QK_NOPE_DIM).transpose(1, 0, 2, 3, 4)
    qr_b = q_rope.reshape(B, nq, Q_BLOCK, N_HEADS_B, QK_ROPE_DIM).transpose(1, 0, 2, 3, 4)

    def block(args):
        qn, qr = args
        s = (jnp.einsum('bqhd,bkhd->bhqk', qn, k_nope)
             + jnp.einsum('bqhd,bkd->bhqk', qr, k_rope)).astype(jnp.float32) * scale
        p = jax.nn.softmax(s, axis=-1).astype(v.dtype)
        return jnp.einsum('bhqk,bkhd->bqhd', p, v)

    o = lax.map(block, (qn_b, qr_b))
    o = o.transpose(1, 0, 2, 3, 4).reshape(B, S, WIDTH_B)
    y = o * jax.nn.silu(gate)
    return y @ w_out

def first_inputs(seed: int = 0) -> dict:
    key = jax.random.key(seed)
    ks = jax.random.split(key, 20)
    nrm = jax.random.normal
    D = D_MODEL
    x = nrm(ks[0], (BATCH, SEQ, D), jnp.float32)
    c = nrm(ks[1], (BATCH, D), jnp.float32)
    rel_bias = 0.2 * nrm(ks[2], (N_BUCKETS, N_HEADS_A), jnp.float32)
    ada_w = 0.5 * D ** -0.5 * nrm(ks[3], (DEPTH, D, 3 * D), jnp.float32)
    ada_b = 0.02 * nrm(ks[4], (DEPTH, 3 * D), jnp.float32)
    ln_g = 1.0 + 0.05 * nrm(ks[5], (DEPTH, D), jnp.float32)
    ln_b = 0.02 * nrm(ks[6], (DEPTH, D), jnp.float32)
    a_w_in = D ** -0.5 * nrm(ks[7], (DEPTH_A, D, 4 * WIDTH_A), jnp.float32)
    a_w_in = a_w_in.at[:, :, 2 * WIDTH_A:3 * WIDTH_A].multiply(DEEPNORM_BETA)
    a_w_out = DEEPNORM_BETA * WIDTH_A ** -0.5 * nrm(ks[8], (DEPTH_A, WIDTH_A, D), jnp.float32)
    b_w_in = D ** -0.5 * nrm(ks[9], (DEPTH_B, D, IN_B), jnp.float32)
    b_q_norm = 1.0 + 0.05 * nrm(ks[10], (DEPTH_B, Q_LORA_RANK), jnp.float32)
    b_w_uq = Q_LORA_RANK ** -0.5 * nrm(ks[11], (DEPTH_B, Q_LORA_RANK, N_HEADS_B * (QK_NOPE_DIM + QK_ROPE_DIM)), jnp.float32)
    b_kv_norm = 1.0 + 0.05 * nrm(ks[12], (DEPTH_B, KV_LORA_RANK), jnp.float32)
    b_w_ukv = KV_LORA_RANK ** -0.5 * nrm(ks[13], (DEPTH_B, KV_LORA_RANK, N_HEADS_B, QK_NOPE_DIM + V_HEAD_DIM), jnp.float32)
    b_w_ukv = b_w_ukv.at[..., QK_NOPE_DIM:].multiply(DEEPNORM_BETA).reshape(
        DEPTH_B, KV_LORA_RANK, N_HEADS_B * (QK_NOPE_DIM + V_HEAD_DIM))
    b_w_out = DEEPNORM_BETA * WIDTH_B ** -0.5 * nrm(ks[14], (DEPTH_B, WIDTH_B, D), jnp.float32)
    return {"x": x, "c": c, "rel_bias": rel_bias, "ada_w": ada_w, "ada_b": ada_b,
            "ln_g": ln_g, "ln_b": ln_b, "a_w_in": a_w_in, "a_w_out": a_w_out,
            "b_w_in": b_w_in, "b_q_norm": b_q_norm, "b_w_uq": b_w_uq, "b_kv_norm": b_kv_norm,
            "b_w_ukv": b_w_ukv, "b_w_out": b_w_out}

def first_block(x, c, rel_bias, ada_w, ada_b, ln_g, ln_b, a_w_in, a_w_out,
              b_w_in, b_q_norm, b_w_uq, b_kv_norm, b_w_ukv, b_w_out):
    for i in range(DEPTH):
        mod = jax.nn.silu(c) @ ada_w[i] + ada_b[i]
        shift, scale, gate = jnp.split(mod[:, None, :], 3, axis=-1)
        u = x * (1 + scale) + shift
        j = i // N_MIXERS
        if i % N_MIXERS == 0:
            y = mixer_dilated(u, a_w_in[j], a_w_out[j], rel_bias)
        else:
            y = mixer_mla(u, b_w_in[j], b_q_norm[j], b_w_uq[j], b_kv_norm[j], b_w_ukv[j], b_w_out[j])
        x = layernorm(DEEPNORM_ALPHA * x + gate * y, ln_g[i], ln_b[i])
    return x


N_META = 16
D_RNN = D_MODEL
LRU_HEADS = 16
LRU_HEAD_DIM = D_RNN // LRU_HEADS
CONV_A = 4
LRU_C = 8.0
D_CONV = D_MODEL
CONV_B = 3
N_GROUPS = 4
EXPERTS_PER_GROUP = 8
N_EXPERTS = N_GROUPS * EXPERTS_PER_GROUP
TOP_K = 2
D_EXPERT = D_MODEL // 2
BLK = 128
N_A_LAYERS = (DEPTH + 1) // 2
N_B_LAYERS = DEPTH // 2
ALPHA = (2.0 * DEPTH) ** 0.25
BETA = (8.0 * DEPTH) ** -0.25


def layer_norm(x, g, b):
    xf = x.astype(jnp.float32)
    mu = jnp.mean(xf, axis=-1, keepdims=True)
    var = jnp.mean(jnp.square(xf - mu), axis=-1, keepdims=True)
    y = (xf - mu) * lax.rsqrt(var + LN_EPS) * g.astype(jnp.float32) + b.astype(jnp.float32)
    return y.astype(x.dtype)

def causal_depthwise_conv(x, w):
    K, C = w.shape
    return lax.conv_general_dilated(
        x, w[:, None, :].astype(x.dtype), window_strides=(1,), padding=[(K - 1, 0)],
        dimension_numbers=("NWC", "WIO", "NWC"), feature_group_count=C)

def _linear_recurrence_combine(c1, c2):
    a1, b1 = c1
    a2, b2 = c2
    return a1 * a2, a2 * b1 + b2

def rglru_mixer(h, w_in, conv_w, conv_b, w_a, b_a, w_i, b_i, lam, w_out):
    Bsz, S, _ = h.shape
    u = h @ w_in
    y_br = jax.nn.gelu(u[..., :D_RNN])
    xc = causal_depthwise_conv(u[..., D_RNN:], conv_w) + conv_b
    xh = xc.reshape(Bsz, S, LRU_HEADS, LRU_HEAD_DIM)
    r = jax.nn.sigmoid(jnp.einsum("bshd,hde->bshe", xh, w_a).reshape(Bsz, S, D_RNN) + b_a)
    gi = jax.nn.sigmoid(jnp.einsum("bshd,hde->bshe", xh, w_i).reshape(Bsz, S, D_RNN) + b_i)
    log_a = -LRU_C * r.astype(jnp.float32) * jax.nn.softplus(-lam.astype(jnp.float32))
    a = jnp.exp(log_a)
    mult = jnp.sqrt(-jnp.expm1(2.0 * log_a))
    b = mult * (gi * xc).astype(jnp.float32)
    _, hs = lax.associative_scan(_linear_recurrence_combine, (a, b), axis=1)
    return (hs.astype(h.dtype) * y_br) @ w_out

def shortconv_mixer(h, w_in, conv_w, w_out):
    u = h @ w_in
    bg = u[..., :D_CONV]
    cg = u[..., D_CONV:2 * D_CONV]
    v = u[..., 2 * D_CONV:]
    zc = causal_depthwise_conv(cg * v, conv_w)
    return (bg * zc) @ w_out

def hierarchical_moe(h, w_group, b_group, w_expert, b_expert, w_gate, w_up, w_down):
    Bsz, S, D = h.shape
    x2 = h.reshape(Bsz * S, D)
    T = x2.shape[0]
    xf = x2.astype(jnp.float32)
    glog = xf @ w_group.astype(jnp.float32) + b_group.astype(jnp.float32)
    gprob = jax.nn.softmax(glog, axis=-1)
    g = jnp.argmax(glog, axis=-1)
    pg = jnp.take_along_axis(gprob, g[:, None], axis=1)
    elog = (xf @ w_expert.astype(jnp.float32)).reshape(T, N_GROUPS, EXPERTS_PER_GROUP) + b_expert.astype(jnp.float32)
    elog_g = jnp.take_along_axis(elog, g[:, None, None], axis=1)[:, 0]
    vals, loc = lax.top_k(elog_g, TOP_K)
    gates = pg * jax.nn.softmax(vals, axis=-1)
    eid = g[:, None] * EXPERTS_PER_GROUP + loc
    A = T * TOP_K
    eid_f = eid.reshape(-1)
    tok_f = jnp.repeat(jnp.arange(T, dtype=jnp.int32), TOP_K)
    gate_f = gates.reshape(-1)
    order = jnp.argsort(eid_f)
    eid_s = eid_f[order]
    tok_s = tok_f[order]
    gate_s = gate_f[order]
    counts = jnp.bincount(eid_f, length=N_EXPERTS)
    start = jnp.cumsum(counts) - counts
    padded = (counts + BLK - 1) // BLK * BLK
    pend = jnp.cumsum(padded)
    pstart = pend - padded
    rank = jnp.arange(A, dtype=jnp.int32) - start[eid_s]
    dest = pstart[eid_s] + rank
    n_blocks = (A + N_EXPERTS * (BLK - 1) + BLK - 1) // BLK
    P = n_blocks * BLK
    slot_tok = jnp.full((P,), T, dtype=jnp.int32).at[dest].set(tok_s)
    slot_gate = jnp.zeros((P,), jnp.float32).at[dest].set(gate_s)
    block_expert = jnp.clip(jnp.searchsorted(pend, jnp.arange(n_blocks) * BLK, side="right"), 0, N_EXPERTS - 1)
    xpad = jnp.concatenate([x2, jnp.zeros((1, D), x2.dtype)], axis=0)
    xs = xpad[slot_tok].reshape(n_blocks, BLK, D)

    def expert_block(args):
        xb, e = args
        hb = jax.nn.silu(xb @ w_gate[e]) * (xb @ w_up[e])
        return hb @ w_down[e]

    ys = lax.map(expert_block, (xs, block_expert)).reshape(P, D)
    y = jnp.zeros((T + 1, D), x2.dtype).at[slot_tok].add(ys * slot_gate[:, None].astype(ys.dtype))
    return y[:T].reshape(Bsz, S, D)

def second_inputs(seed: int = 0) -> dict:
    key = jax.random.key(seed)
    ks = jax.random.split(key, 24)

    def nrm(k, shape, scale):
        return jax.random.normal(k, shape, jnp.float32) * scale

    u = jax.random.uniform(ks[10], (N_A_LAYERS, D_RNN), jnp.float32, 0.9, 0.999)
    a0 = u ** (1.0 / LRU_C)
    lru_lambda = jnp.log(a0) - jnp.log1p(-a0)
    return {
        "x": nrm(ks[0], (BATCH, SEQ, D_MODEL), 1.0),
        "meta_tokens": nrm(ks[1], (N_META, D_MODEL), 1.0),
        "lru_w_in": nrm(ks[2], (N_A_LAYERS, D_MODEL, 2 * D_RNN), D_MODEL ** -0.5),
        "lru_conv_w": nrm(ks[3], (N_A_LAYERS, CONV_A, D_RNN), CONV_A ** -0.5),
        "lru_conv_b": nrm(ks[4], (N_A_LAYERS, D_RNN), 0.01),
        "lru_w_a": nrm(ks[5], (N_A_LAYERS, LRU_HEADS, LRU_HEAD_DIM, LRU_HEAD_DIM), LRU_HEAD_DIM ** -0.5),
        "lru_b_a": nrm(ks[6], (N_A_LAYERS, D_RNN), 0.01),
        "lru_w_i": nrm(ks[7], (N_A_LAYERS, LRU_HEADS, LRU_HEAD_DIM, LRU_HEAD_DIM), LRU_HEAD_DIM ** -0.5),
        "lru_b_i": nrm(ks[8], (N_A_LAYERS, D_RNN), 0.01),
        "lru_lambda": lru_lambda,
        "lru_w_out": nrm(ks[9], (N_A_LAYERS, D_RNN, D_MODEL), BETA * D_RNN ** -0.5),
        "sc_w_in": nrm(ks[11], (N_B_LAYERS, D_MODEL, 3 * D_CONV), D_MODEL ** -0.5),
        "sc_conv_w": nrm(ks[12], (N_B_LAYERS, CONV_B, D_CONV), CONV_B ** -0.5),
        "sc_w_out": nrm(ks[13], (N_B_LAYERS, D_CONV, D_MODEL), BETA * D_CONV ** -0.5),
        "moe_w_group": nrm(ks[14], (DEPTH, D_MODEL, N_GROUPS), D_MODEL ** -0.5),
        "moe_b_group": nrm(ks[15], (DEPTH, N_GROUPS), 0.01),
        "moe_w_expert": nrm(ks[16], (DEPTH, D_MODEL, N_EXPERTS), D_MODEL ** -0.5),
        "moe_b_expert": nrm(ks[17], (DEPTH, N_GROUPS, EXPERTS_PER_GROUP), 0.01),
        "moe_w_gate": nrm(ks[18], (DEPTH, N_EXPERTS, D_MODEL, D_EXPERT), D_MODEL ** -0.5),
        "moe_w_up": nrm(ks[19], (DEPTH, N_EXPERTS, D_MODEL, D_EXPERT), D_MODEL ** -0.5),
        "moe_w_down": nrm(ks[20], (DEPTH, N_EXPERTS, D_EXPERT, D_MODEL), BETA * D_EXPERT ** -0.5),
        "ln_g": 1.0 + nrm(ks[21], (DEPTH, 2, D_MODEL), 0.02),
        "ln_b": nrm(ks[22], (DEPTH, 2, D_MODEL), 0.02),
    }

def second_block(x, meta_tokens, lru_w_in, lru_conv_w, lru_conv_b, lru_w_a, lru_b_a, lru_w_i, lru_b_i,
              lru_lambda, lru_w_out, sc_w_in, sc_conv_w, sc_w_out, moe_w_group, moe_b_group,
              moe_w_expert, moe_b_expert, moe_w_gate, moe_w_up, moe_w_down, ln_g, ln_b):
    Bsz = x.shape[0]
    meta = jnp.broadcast_to(meta_tokens.astype(x.dtype)[None], (Bsz, N_META, D_MODEL))
    h = jnp.concatenate([meta, x], axis=1)
    for i in range(DEPTH):
        j = i // N_MIXERS
        if i % N_MIXERS == 0:
            mixed = rglru_mixer(h, lru_w_in[j], lru_conv_w[j], lru_conv_b[j], lru_w_a[j], lru_b_a[j],
                                lru_w_i[j], lru_b_i[j], lru_lambda[j], lru_w_out[j])
        else:
            mixed = shortconv_mixer(h, sc_w_in[j], sc_conv_w[j], sc_w_out[j])
        h = layer_norm(ALPHA * h + mixed, ln_g[i, 0], ln_b[i, 0])
        ffn = hierarchical_moe(h, moe_w_group[i], moe_b_group[i], moe_w_expert[i], moe_b_expert[i],
                               moe_w_gate[i], moe_w_up[i], moe_w_down[i])
        h = layer_norm(ALPHA * h + ffn, ln_g[i, 1], ln_b[i, 1])
    return h[:, N_META:]


def setup_inputs(seed=0):
    out = dict(first_inputs(seed))
    for name, value in second_inputs(seed + 1).items():
        if name != "x":
            out[name + "_2"] = value
    return out


def reference(
    x, c, rel_bias, ada_w, ada_b, ln_g, ln_b, a_w_in, a_w_out, b_w_in, b_q_norm, b_w_uq,
    b_kv_norm, b_w_ukv, b_w_out, meta_tokens_2, lru_w_in_2, lru_conv_w_2, lru_conv_b_2,
    lru_w_a_2, lru_b_a_2, lru_w_i_2, lru_b_i_2, lru_lambda_2, lru_w_out_2, sc_w_in_2,
    sc_conv_w_2, sc_w_out_2, moe_w_group_2, moe_b_group_2, moe_w_expert_2, moe_b_expert_2,
    moe_w_gate_2, moe_w_up_2, moe_w_down_2, ln_g_2, ln_b_2,
):
    x = first_block(
        x, c, rel_bias, ada_w, ada_b, ln_g, ln_b, a_w_in, a_w_out, b_w_in, b_q_norm, b_w_uq,
        b_kv_norm, b_w_ukv, b_w_out,
    )
    return second_block(
        x, meta_tokens_2, lru_w_in_2, lru_conv_w_2, lru_conv_b_2, lru_w_a_2, lru_b_a_2,
        lru_w_i_2, lru_b_i_2, lru_lambda_2, lru_w_out_2, sc_w_in_2, sc_conv_w_2, sc_w_out_2,
        moe_w_group_2, moe_b_group_2, moe_w_expert_2, moe_b_expert_2, moe_w_gate_2, moe_w_up_2,
        moe_w_down_2, ln_g_2, ln_b_2,
    )


_drawn_inputs = setup_inputs


def setup_inputs(seed=0):
    import zlib

    import numpy as np

    out = dict(_drawn_inputs(seed))
    spreads = {}
    factors = {'c': 2.848,
     'rel_bias': 8.0,
     'ada_b': 8.0,
     'a_w_in': 4.845,
     'a_w_out': 6.33,
     'b_w_in': 2.958,
     'b_q_norm': 8.0,
     'b_w_uq': 8.0,
     'b_kv_norm': 8.0,
     'b_w_out': 2.967,
     'lru_conv_b_2': 3.353,
     'lru_b_a_2': 41.419,
     'lru_b_i_2': 21.352,
     'moe_b_group_2': 5.532,
     'moe_b_expert_2': 17.858}
    for name, (base, spread) in spreads.items():
        noise = np.random.default_rng([zlib.crc32(name.encode()), seed]).standard_normal(out[name].shape)
        drawn = base * np.exp(spread * noise) if base else spread * noise
        out[name] = __import__('jax').numpy.asarray(drawn.astype(out[name].dtype))
    for name, factor in factors.items():
        out[name] = (out[name] * factor).astype(out[name].dtype)
    return out
```

```python
from contextlib import ExitStack

import numpy as np

import concourse.bass as bass
from concourse import mybir

F32 = mybir.dt.float32
BF16 = mybir.dt.bfloat16
I32 = mybir.dt.int32
U32 = mybir.dt.uint32
ALU = mybir.AluOpType
ACT = mybir.ActivationFunctionType
AX = mybir.AxisListType

P = 128
D = 1024
DC = D // P
S = 512
NT = S // P
META = 16
TM = META + S
GROUPS = 3
HPG = 6
HD = 64
WA = GROUPS * HPG * HD
GW = HPG * HD
GC = GW // P
NB = 32
DILS = (1, 4, 16)
RADIUS = 64
NEG = -1e30
HB = 16
QL, KVL, ROPE = 256, 128, 32
NOPE = 64
QW = NOPE + ROPE
SCALE_B = float(QW) ** -0.5
NE = 32
NG = 4
EPG = NE // NG
FE = 512
FC = FE // P
CAP = 128
NOVER = 8
NBLK = NE + NOVER
EMPTY = 1 << 20
ALPHA = 4.0 ** 0.25
LN_EPS = 1e-5
RMS_EPS = 1e-6

SLABS = 6
SLAB = 4096


def bucket(rel):
    half, exact = NB // 2, NB // 4
    n = np.abs(rel)
    large = exact + (np.log(np.maximum(n, 1).astype(np.float32) / np.float32(exact)) / np.float32(np.log(1024 / exact))
                     * (half - exact)).astype(np.int32)
    return np.where(rel > 0, half, 0) + np.where(n < exact, n, np.minimum(large, half - 1))


def constants():
    d = 255 - np.arange(2 * 256)
    sel = np.zeros((NB + 1, GROUPS, 512), np.float32)
    for g, dil in enumerate(DILS):
        step = dil // 4 if g == 2 else 1
        ok = (np.abs(d) <= RADIUS * step) & (d % step == 0)
        if g == 2:
            ok &= np.abs(d // step) <= 31
        rel = d // step * dil
        for i in range(512):
            sel[bucket(rel[i]) if ok[i] else NB, g, i] = 1.0
    heads = np.zeros((HPG, GC, P), np.float32)
    for c in range(GC):
        for f in range(P):
            heads[2 * c + f // HD, c, f] = 1.0
    inv = np.float32(10000.0) ** (-np.arange(0, ROPE, 2, dtype=np.float32) / np.float32(ROPE))
    ang = np.arange(S, dtype=np.float32)[:, None] * inv[None, :]
    cos, sin = np.cos(ang).T, np.sin(ang).T
    rot = np.stack([np.concatenate([cos, cos]), np.concatenate([-sin, sin])], axis=1).astype(np.float32)
    return {"bucket_sel": sel, "head_sel": heads, "rotary": np.tile(rot, (4, 1, 1))}


def plan_slabs():
    out = [("ada", 0, s) for s in range(6)]
    for g in range(GROUPS):
        out += [("win_a", 0, (t, g)) for t in range(3)]
        if g == 1:
            out += [("ada", 1, s) for s in range(6)]
    out += [("win_a", 0, (3, g)) for g in range(GROUPS)]
    out += [("wout_a", 0, s) for s in range(3)]
    out += [("win_b", 0, s) for s in range(3)] + [("ukv", 0, 0), ("uq", 0, 0)]
    out += [("wout_b", 0, s) for s in range(2)]
    out += [("lru_in", 0, s) for s in (0, 2, 1, 3)] + [("lru_out", 0, s) for s in range(2)]
    out += [("expert", 0, (e, w)) for e in range(NE) for w in range(3)]
    out += [("sc_in", 0, (t, h)) for h in range(2) for t in (1, 2, 0)] + [("sc_out", 0, s) for s in range(2)]
    out += [("expert", 1, (e, w)) for e in range(NE) for w in range(3)]
    return out


STREAM = plan_slabs()
TURN = {k: n for n, k in enumerate(STREAM)}

PROWS = {}
_at = 0
for _n, _k in (("c", 8), ("ada_b", 48), ("qn", 2), ("kvn", 1), ("conv_w", 32), ("conv_b", 8), ("b_a", 8),
               ("b_i", 8), ("lam", 8)):
    PROWS[_n] = _at
    _at += _k
NROWS = _at
SC0 = P


def plan_jobs():
    j = ["params", "taps", "mod0_0"] + [f"toep{g}" for g in range(3)] + [f"mod0_{s}" for s in range(1, 6)]
    j += [f"qkv0_{i}" for i in range(10)]
    for u in range(36):
        j += FILL_A.get(u, [])
    for g in range(3):
        j += [f"negmax{g}", f"den{g}"]
    j += [f"fac_{c}" for c in range(9)]
    j += [f"outA_{t}" for t in range(NT)]
    j += [f"lat_{c}" for c in range(4)] + ["rms0", "rms1"] + ["gateb1"] + [f"vB_{t}" for t in range(NT)]
    j += [f"qr_{i}" for i in range(4)] + [f"sgB_{c}" for c in range(DC)] + ["qn_0", "kn_0", "qn_1", "kn_1"]
    for h in range(2, 8):
        j += [f"qn_{h}", f"kn_{h}"]
    j += [f"outB_{t}" for t in range(NT)]
    for c in range(DC):
        j += [f"uy_{c}", f"ux_{c}"] + ([f"ra_{c - 1}", f"ri_{c - 1}"] if c else [])
    j += ["ra_7", "ri_7"]
    j += [f"outC_{t}" for t in (4, 0, 1, 2, 3)] + ["router0", "ranks0"]
    for c in range(DC):
        j += [f"cg_{c}", f"cv_{c}", f"bg_{c}"]
    j += [f"outD_{t}" for t in range(NT)] + ["router1", "ranks1"]
    return j


FILL_A = {}
for _i in range(10):
    FILL_A.setdefault(2 + 2 * _i, []).append(f"qkv1_{_i}")
    FILL_A.setdefault(26 + _i * 4 // 10, []).append(f"qkv2_{_i}")
MOD_AT = (9, 11, 13, 15, 17, 23)
for _i in range(6):
    FILL_A[MOD_AT[_i]] = [f"mod1_{_i}"]
FILL_A[25] = ["gateb0"]
for _i in range(9):
    FILL_A.setdefault(32 + _i * 4 // 9, []).append(f"sgA_{_i}")

JOBS = plan_jobs()
JOB = {n: i for i, n in enumerate(JOBS)}
assert len(JOB) == len(JOBS)

UNITS_A = [(0, h, n) for h in range(HPG) for n in range(NT)] + [(g, h, None) for g in (1, 2) for h in range(HPG)]
NUA = len(UNITS_A)
NUB = HB * NT


def build(nc, a, out):
    with ExitStack() as ctx:
        def sb(name, shape, dt=F32):
            return ctx.enter_context(nc.sbuf_tensor(name, shape, dt))

        def sem(name):
            return ctx.enter_context(nc.semaphore(name))

        ring = sb("ring", [P, SLABS * SLAB])
        arena = sb("arena", [P, 24576])
        lnp = sb("lnp", [P, 2, D])
        gate_b = sb("gate_b", [P, D])
        ident = sb("ident", [P, P])
        ones = sb("ones", [P, P])
        before = sb("before", [P, P], BF16)
        ones_h = sb("ones_h", [P, P], BF16)
        cols = sb("cols", [P, SC0 + 24])
        csilu = sb("csilu", [P, 2, DC])
        mod = sb("mod", [P, 2, 24])
        lamc = sb("lamc", [P, 4, DC])
        half_b = sb("half_b", [P, 2, DC])
        spec = sb("spec", [P, 64])
        expert_of = arena[:, 24528:24560]
        group_of = sb("group_of", [P, NE])
        negm = sb("negm", [P, GROUPS, NT, HPG])
        den = sb("den", [P, GROUPS, NT, HPG])
        nmax = sb("nmax", [P, 8])
        dsum = sb("dsum", [P, 8])
        slots_i = sb("slots_i", [P, 10], I32)
        assign_id = sb("assign_id", [P, 10], I32)
        slot_ids = arena[:, 24448:24488].bitcast(I32)
        slot_tok = arena[:, 24488:24528].bitcast(I32)
        load_i = mod[0:1].rearrange("p l n -> p (l n)")[:, 0:NE].bitcast(I32)
        over_i = sb("over_i", [1, 16], I32)
        gates = sb("gates", [P, 2, 5])

        ps = ctx.enter_context(nc.psum_tensor("ps", [P, 8, 512], F32))

        def at(o, n):
            return arena[:, o:o + n]

        X = at(0, 5 * D).rearrange("p (t d) -> p t d", d=D)
        HT = at(5120, DC * TM).rearrange("p (c t) -> p c t", t=TM)
        R0 = 9344
        qkv_at = [0, R0 + 4608]
        oT_a = at(R0, 9 * S).rearrange("p (c t) -> p c t", t=S)
        bias0 = at(R0 + 9216, HPG * 384).rearrange("p (h j) -> p h j", j=384)
        bias12 = [at(R0 + 11520 + 768 * g, HPG * P).rearrange("p (h j) -> p h j", j=P) for g in range(2)]
        sp_a = [at(R0 + 13056 + 512 * i, 512) for i in range(3)]
        pT_a = [at(4608, 512), at(R0 + 14592, 512)]
        x_first = at(qkv_at[1], NT * D).rearrange("p (t d) -> p t d", d=D)
        q_g = [at(qkv_at[g % 2], GC * S).rearrange("p (c t) -> p c t", t=S) for g in range(GROUPS)]
        k_g = [at(qkv_at[g % 2] + 1536, GC * S).rearrange("p (c t) -> p c t", t=S) for g in range(GROUPS)]
        v_g = [at(qkv_at[g % 2] + 3072, NT * GW).rearrange("p (t f) -> p t f", f=GW) for g in range(GROUPS)]
        sg_a = at(qkv_at[1], 9 * S).rearrange("p (c t) -> p c t", t=S)
        rows_m = at(R0 + 9216, 3 * S).rearrange("p (g t) -> p g t", t=S)
        rows_d = at(R0 + 10752, 3 * S).rearrange("p (g t) -> p g t", t=S)
        rows_t = at(R0 + 12288, S)
        rows_s = at(R0 + 12800, S)
        vB = at(0, NT * D).rearrange("p (t f) -> p t f", f=D)
        sgB = at(R0, DC * S).rearrange("p (c t) -> p c t", t=S)
        qrB = at(R0 + 4096, 4 * S).rearrange("p (c t) -> p c t", t=S)
        krB = at(R0 + 6144, S)
        latB = at(R0 + 6656, 3 * S).rearrange("p (c t) -> p c t", t=S)
        qnB = [at(R0 + 8192 + 512 * i, S) for i in range(3)]
        knB = [at(R0 + 9728 + 512 * i, S) for i in range(3)]
        rot = at(R0 + 11264, 2 * S).rearrange("p (c t) -> p c t", t=S)
        tmpB = [at(R0 + 12288, S), at(R0 + 12800, S)]
        sp_b = sp_a
        pT_b = [at(4096, 512), at(R0 + 14592, 512)]
        oT_b = HT[:, :, META:TM]
        yT = at(R0, DC * TM).rearrange("p (c t) -> p c t", t=TM)
        sT = at(R0 + 4224, 2 * TM).rearrange("p (c t) -> p c t", t=TM)
        gx = at(R0 + 5280, 2 * TM).rearrange("p (c t) -> p c t", t=TM)
        root = at(R0 + 6336, 2 * TM).rearrange("p (c t) -> p c t", t=TM)
        wa_bd = at(R0 + 7392, 4 * P).rearrange("p (t i f) -> p t i f", t=2, i=2)
        upad = at(R0 + 12672, TM + 3)
        tA = at(R0 + 13204, TM)
        tB = at(R0 + 13732, TM)
        xc = at(R0 + 14260, TM)
        NC_ = S + 2
        zT = at(R0, DC * S).rearrange("p (c t) -> p c t", t=S)
        zpad = [at(R0 + 4224 + 528 * i, NC_) for i in range(2)]
        cgs = [at(R0 + 5280 + 528 * i, NC_) for i in range(2)]
        xe = [at(R0 + D * i, D) for i in range(2)]
        xeT = [at(R0 + 2048 + D * i, D).rearrange("p (c t) -> p c t", t=P) for i in range(2)]
        zg = [at(R0 + 4096 + 512 * i, 512) for i in range(2)]
        hb = [at(R0 + 5120 + 512 * i, 512).rearrange("p (c t) -> p c t", t=P) for i in range(2)]
        yo = [at(R0 + 6144 + D * i, D) for i in range(2)]
        yin = [at(R0 + 2 * D * i, 2 * D).rearrange("p (k d) -> p k d", k=2) for i in range(5)]
        rw = at(R0 + 12288, 2 * DC * 36).rearrange("p (l c n) -> p l c n", l=2, c=DC)
        rb = at(R0 + 12864, 72).rearrange("p (l n) -> p l n", l=2)
        lg = at(R0 + 12936, 5 * 40).rearrange("p (t n) -> p t n", n=40)
        RT = R0 + 13136
        elm = at(RT, 5 * NE).rearrange("p (t n) -> p t n", n=NE)
        oh1 = at(RT + 160, 5 * NE).rearrange("p (t n) -> p t n", n=NE)
        oh2 = at(RT + 320, 5 * NE).rearrange("p (t n) -> p t n", n=NE)
        adr = at(RT + 480, 5 * NE).rearrange("p (t n) -> p t n", n=NE)
        tq = at(RT + 640, 5 * NE).rearrange("p (t n) -> p t n", n=NE)
        ohb = at(RT + 800, 80).bitcast(BF16).rearrange("p (t n) -> p t n", n=NE)
        g8 = at(RT + 880, 40).rearrange("p (t n) -> p t n", n=8)
        e8 = at(RT + 920, 40).rearrange("p (t n) -> p t n", n=8)
        gi8 = at(RT + 960, 40).bitcast(U32).rearrange("p (t n) -> p t n", n=8)
        ei8 = at(RT + 1000, 40).bitcast(U32).rearrange("p (t n) -> p t n", n=8)
        sm = at(RT + 1040, 80).rearrange("p (n t) -> p n t", t=5)
        cnt = at(RT + 1120, 4 * NE).rearrange("p (n e) -> p n e", e=NE)
        slf = at(RT + 1248, 10).rearrange("p (t k) -> p t k", k=2)
        ovf = at(RT + 1258, 16)
        prow = at(R0, P)
        prow2 = at(R0 + 128, P)
        brow = at(R0 + 256, 1536).rearrange("p (g i) -> p g i", g=3)
        bsel = at(R0 + 1792, 1536).rearrange("p (g i) -> p g i", g=3)
        relb = at(R0 + 3328, 18)
        hsel = lnp[0:HPG, 0, 0:GC * P].rearrange("p (c f) -> p c f", f=P)
        meta_x = X[:, 4, :]

        def dram(name, shape, dt=F32):
            return nc.dram_tensor(name, shape, dt, kind="Internal").ap()

        bvec = dram("bias_vectors", [HPG, 3, 512])
        x1_d = dram("x1_rows", [S, D])
        h_d = [dram(f"h_rows{l}", [(TM, S)[l], D]) for l in range(2)]
        ya_d = [dram(f"assignment_rows{l}", [2 * (TM, S)[l], D]) for l in range(2)]
        tab_d = [dram(f"slot_table{l}", [P * NBLK, 1], I32) for l in range(2)]

        slab_landed = [sem(f"slab_landed{i}") for i in range(SLABS)]
        proj_done = sem("proj_done")
        proj_free = [sem(f"proj_free{i}") for i in range(2)]
        prow_set, prow_in = sem("prow_set"), sem("prow_in")
        consts_in, table_in = sem("consts_in"), sem("table_in")
        rot_in, gates_ready = sem("rot_in"), sem("gates_ready")
        x_in, meta_in, x_back, x1_out, x1_back = (sem(n) for n in ("x_in", "meta_in", "x_back", "x1_out", "x1_back"))
        pool_own, pool_set = sem("pool_own"), sem("pool_set")
        vec_own, act_own = sem("vec_own"), sem("act_own")
        csilu_ready, mod_sum = sem("csilu_ready"), sem("mod_sum")
        diag_ready, gateb_ready = sem("diag_ready"), sem("gateb_ready")
        turned = sem("turned")
        turn_copied = [sem(f"turn_copied{h}") for h in range(2)]
        bvec_ready, bvec_out, toep_in = sem("bvec_ready"), sem("bvec_out"), sem("toep_in")
        qkv_ready = sem("qkv_ready")
        scores_ready, scores_read = sem("scores_ready"), sem("scores_read")
        max_ready, probs_ready = sem("max_ready"), sem("probs_ready")
        pt_ready, pt_copied, pv_done, o_copied = (sem(n) for n in ("pt_ready", "pt_copied", "pv_done", "o_copied"))
        factors_ready, yT_ready, silu_ready = sem("factors_ready"), sem("yT_ready"), sem("silu_ready")
        var_ready, sd_ready, normed, ln_done = (sem(n) for n in ("var_ready", "sd_ready", "normed", "ln_done"))
        lnp_in = sem("lnp_in")
        lat_sq, lat_ready, rms_var, rms_sd = (sem(n) for n in ("lat_sq", "lat_ready", "rms_var", "rms_sd"))
        qr_ready, kr_ready, head_ready, vB_ready = (sem(n) for n in ("qr_ready", "kr_ready", "head_ready", "vB_ready"))
        bd_in = [sem(f"bd_in{i}") for i in range(2)]
        xc_ready, gelu_sq, gelu_in, gelu_th = (sem(n) for n in ("xc_ready", "gelu_sq", "gelu_in", "gelu_th"))
        route_ready = sem("route_ready")
        fac_in, fac_exp = sem("fac_in"), sem("fac_exp")
        u_copied, r_tanh, s_ready, i_tanh, root_ready = (sem(n) for n in ("u_copied", "r_tanh", "s_ready", "i_tanh", "root_ready"))
        lam_a, lam_b = sem("lam_a"), sem("lam_b")
        cg_copied = sem("cg_copied")
        rw_in, h_out = sem("rw_in"), sem("h_out")
        pg_in, pg_exp, onehot_ready, slots_ready, ids_out, ids_in, tok_ready = (
            sem(n) for n in ("pg_in", "pg_exp", "onehot_ready", "slots_ready", "ids_out", "ids_in", "tok_ready"))
        table_out = sem("table_out")
        xe_landed = [sem(f"xe_landed{i}") for i in range(2)]
        xe_used, xet_ready, xet_copied = sem("xe_used"), sem("xet_ready"), sem("xet_copied")
        gate_ready, up_ready, tanh_ready, hb_ready, y_ready, yo_ready = (
            sem(n) for n in ("gate_ready", "up_ready", "tanh_ready", "hb_ready", "y_ready", "yo_ready"))
        zg_ready = sem("zg_ready")
        yo_sent = [sem(f"yo_sent{i}") for i in range(2)]
        yin_in = [sem(f"yin_in{t}") for t in range(5)]
        alpha_done, scale_ready = sem("alpha_done"), sem("scale_ready")
        comb_done = sem("comb_done")
        ov = [{n: sem(f"over_{n}{l}") for n in ("w", "x", "xu", "xt", "xc", "g", "t", "z", "h", "y", "yo", "out")}
              for l in range(2)]
        out_sent = sem("out_sent")

        def slab(turn):
            o = (turn % SLABS) * SLAB
            return ring[:, o:o + SLAB]

        def bank(name):
            return 2 * (JOB[name] % 2)

        def tokens(tile):
            return slice(0, META) if tile == 4 else slice(META + P * tile, META + P * (tile + 1))

        def rows_of(tile):
            return META if tile == 4 else P

        LN_TILES = [(l, t) for l, ts in ((0, range(4)), (1, range(4)), (2, (4, 0, 1, 2, 3)), (3, (4, 0, 1, 2, 3)),
                                         (4, range(4)), (5, range(4))) for t in ts]
        LN = {k: i for i, k in enumerate(LN_TILES)}
        COMBINED = {k: i for i, k in enumerate(k for k in LN_TILES if k[0] in (3, 5))}
        TURNED = {k: i for i, k in enumerate((k, t) for k in range(6) for t in (((4,) if 2 <= k <= 4 else ()) + (0, 1, 2, 3)))}

        def taken(eng, name):
            eng.wait_ge(proj_free[JOB[name] % 2], JOB[name] // 2 + 1)

        def ht_wait(eng, k):
            for h in range(2):
                eng.wait_ge(turn_copied[h], TURNED[(k, 3)] + 1)

        def turn_bank(n, h):
            return ps[:, 4 + 2 * (n % 2) + h, :]

        def done(eng, name):
            eng.wait_ge(proj_done, JOB[name] + 1)

        def backwards(ap):
            dims = [list(x) for x in ap.ap]
            step, n = dims[-1]
            return bass.AP(ap.tensor, ap.offset + step * (n - 1), dims[:-1] + [[-step, n]])

        def spread(ap, at_dim, n):
            dims = [list(x) for x in ap.ap]
            return bass.AP(ap.tensor, ap.offset, dims[:at_dim] + [[0, n]] + dims[at_dim:])

        PARAMS = (("c", a["c"].rearrange("a (r p) -> (a r) p", p=P)),
                  ("ada_b", a["ada_b"].rearrange("l (r p) -> (l r) p", p=P)),
                  ("qn", a["b_q_norm"].rearrange("l (r p) -> (l r) p", p=P)),
                  ("kvn", a["b_kv_norm"]),
                  ("conv_w", a["lru_conv_w_2"][0].rearrange("k (r p) -> (k r) p", p=P)),
                  ("conv_b", a["lru_conv_b_2"].rearrange("l (r p) -> (l r) p", p=P)),
                  ("b_a", a["lru_b_a_2"].rearrange("l (r p) -> (l r) p", p=P)),
                  ("b_i", a["lru_b_i_2"].rearrange("l (r p) -> (l r) p", p=P)),
                  ("lam", a["lru_lambda_2"].rearrange("l (r p) -> (l r) p", p=P)))

        def load_params(eng, which):
            for name, src in which:
                eng.dma_start(prow[PROWS[name]:PROWS[name] + src.shape[0], :], src).then_inc(prow_in, 16)

        block = ctx.enter_context(nc.Block())

        def consumed(turn):
            kind, l, s = STREAM[turn]
            if kind == "expert":
                e, w = s
                return (gate_ready, up_ready, y_ready)[w], NE * l + e + 1
            last = {
                "ada": lambda: f"mod{l}_{s}",
                "win_a": lambda: f"qkv{s[1]}_{(2, 5, 9)[s[0]]}" if s[0] < 3 else f"sgA_{3 * s[1] + 2}",
                "wout_a": lambda: "outA_3",
                "win_b": lambda: ("lat_3", "sgB_3", "sgB_7")[s],
                "ukv": lambda: "kn_7", "uq": lambda: "kn_7",
                "wout_b": lambda: "outB_3",
                "lru_in": lambda: f"{'ux' if s > 1 else 'uy'}_{3 + 4 * (s % 2)}",
                "lru_out": lambda: "outC_3",
                "sc_in": lambda: f"{('bg', 'cg', 'cv')[s[0]]}_{3 + 4 * s[1]}",
                "sc_out": lambda: "outD_3",
            }[kind]()
            return proj_done, JOB[last] + 1

        def source(kind, l, s):
            def cols_(w, c0, n):
                return w[:, c0:c0 + n].rearrange("(c p) n -> p c n", p=P)

            def rows_(w, r0, n):
                return w[r0:r0 + n, :].rearrange("(c p) n -> p c n", p=P)
            if kind == "ada":
                return cols_(a["ada_w"][l], 512 * s, 512)
            if kind == "win_a":
                return cols_(a["a_w_in"][0], WA * s[0] + GW * s[1], GW)
            if kind == "wout_a":
                return rows_(a["a_w_out"][0], 512 * s, min(512, WA - 512 * s))
            if kind == "win_b":
                lo = (0, 416, 928)[s]
                return cols_(a["b_w_in"][0], lo, (416, 512, 512)[s])
            if kind == "ukv":
                return rows_(a["b_w_ukv"][0], 0, KVL)
            if kind == "uq":
                return rows_(a["b_w_uq"][0], 0, QL)
            if kind == "wout_b":
                return rows_(a["b_w_out"][0], 512 * s, 512)
            if kind == "lru_in":
                return cols_(a["lru_w_in_2"][0], 512 * s, 512)
            if kind == "lru_out":
                return rows_(a["lru_w_out_2"][0], 512 * s, 512)
            if kind == "sc_in":
                return cols_(a["sc_w_in_2"][0], D * s[0] + 512 * s[1], 512)
            return rows_(a["sc_w_out_2"][0], 512 * s, 512)

        def expert_source(l, e, w):
            t = a[("moe_w_gate_2", "moe_w_up_2", "moe_w_down_2")[w]][l]
            t = t[bass.ds(e, 1)] if not isinstance(e, int) else t[e:e + 1]
            return t.rearrange("e (c p) n -> p (e c) n", p=P)

        def shaped(turn, c, n):
            return slab(turn)[:, 0:c * n].rearrange("p (c n) -> p c n", n=n)

        def expert_slab(turn, w):
            return shaped(turn, DC, FE) if w < 2 else shaped(turn, FC, D)

        def landed(eng, turn):
            eng.wait_ge(slab_landed[turn % SLABS], 16 * (turn // SLABS + 1))

        @block.sync
        def _(sp):
            def dense(turn):
                if turn >= SLABS:
                    sp.wait_ge(*consumed(turn - SLABS))
                src = source(*STREAM[turn])
                sp.dma_start(shaped(turn, src.shape[1], src.shape[2]), src).then_inc(slab_landed[turn % SLABS], 16)

            def experts(l):
                base = TURN[("expert", l, (0, 0))]
                for pair in (0, None):
                    if pair == 0:
                        for r in range(6):
                            sp.wait_ge(*consumed(base + r - SLABS))
                            sp.dma_start(expert_slab(base + r, r % 3), expert_source(l, r // 3, r % 3))\
                              .then_inc(slab_landed[(base + r) % SLABS], 16)
                    else:
                        with sp.Fori(1, NE // 2) as i:
                            for r in range(6):
                                used = (gate_ready, up_ready, y_ready)[r % 3]
                                sp.wait_ge(used, NE * l + i * 2 + (r // 3 - 1))
                                sp.dma_start(expert_slab(base + r, r % 3), expert_source(l, i * 2 + r // 3, r % 3))\
                                  .then_inc(slab_landed[(base + r) % SLABS], 16)
                o = ov[l]
                sp.wait_ge(y_ready, NE * (l + 1))
                sp.wait_ge(route_ready, l + 1)
                n_over = sp.value_load(over_i[0:1, 8:9], min_val=0, max_val=NOVER)
                for j in range(NOVER):
                    with sp.If(n_over > j):
                        if j:
                            sp.wait_ge(o["y"], j)
                        e = sp.value_load(over_i[0:1, j:j + 1], min_val=0, max_val=NE - 1)
                        for w in range(3):
                            sp.dma_start(expert_slab(base + w, w), expert_source(l, e, w)).then_inc(o["w"], 16)
                        sp.wait_ge(o["y"], j + 1)
                    with sp.Else():
                        sp.nop()

            load_params(sp, PARAMS[:5])
            e0, e1 = TURN[("expert", 0, (0, 0))], TURN[("expert", 1, (0, 0))]
            for turn in range(e0):
                dense(turn)
            experts(0)
            for t in range(5):
                sp.wait_ge(yin_in[t], 16)
            for turn in range(e0 + 3 * NE, e1):
                dense(turn)
            experts(1)

        @block.tensor
        def _(pe):
            count = [0]

            def begin(name):
                n = count[0]
                assert JOBS[n] == name, (JOBS[n], name)
                if n >= 2:
                    pe.wait_ge(proj_free[n % 2], n // 2)
                return ps[:, 2 * (n % 2), :], ps[:, 2 * (n % 2) + 1, :]

            def end(ins):
                ins.then_inc(proj_done, 1)
                count[0] += 1

            def product(dst, pairs):
                for i, (w, m) in enumerate(pairs):
                    ins = pe.matmul(dst, w, m, start=i == 0, stop=i == len(pairs) - 1)
                return ins

            def turn_tile(k, t):
                n = TURNED[(k, t)]
                r = rows_of(t)
                src = x_first if k == 0 else X
                for h in range(2):
                    if n >= 2:
                        pe.wait_ge(turn_copied[h], n - 1)
                    b = turn_bank(n, h)
                    for c in range(4):
                        f = P * (4 * h + c)
                        ins = pe.transpose(b[:, r * c:r * c + r], src[0:r, t, f:f + P], ident[0:r, 0:r])
                    ins.then_inc(turned, 1)

            def turn_normed(k, l, t):
                pe.wait_ge(ln_done, LN[(l, t)] + 1)
                turn_tile(k, t)

            def out_and_turn(k, l, order, out_tile):
                for i, t in enumerate(order):
                    out_tile(t)
                    if i:
                        turn_normed(k, l, order[i - 1])
                turn_normed(k, l, order[-1])

            def feature_major(name, w, cols_, moving, m=P, n=DC):
                b0, b1 = begin(name)
                parts = [(b0, moving)] if isinstance(moving[0], int) else list(zip((b0, b1), moving))
                for b, mv in parts:
                    width = mv[1] - mv[0]
                    ins = product(b[0:m, 0:width], [(w[:, k, cols_], HT[:, k, mv[0]:mv[1]]) for k in range(n)])
                end(ins)

            WHOLE = (META, TM)
            BOTH = ((0, TM // 2), (TM // 2, TM))

            def token_major(name, tile, y, parts):
                b0, b1 = begin(name)
                r = rows_of(tile)
                for h, b in enumerate((b0, b1)):
                    ins = product(b[0:r, :], [(y(k), w[:, kk, 512 * h:512 * h + 512]) for k, (w, kk) in enumerate(parts)])
                end(ins)

            def modulation(l, s):
                acc = slab(TURN[("ada", l, s)])[:, 0:512]
                pe.wait_ge(mod_sum, 6 * l + s + 1)
                b0, _ = begin(f"mod{l}_{s}")
                for m in range(4):
                    ins = pe.matmul(b0[:, m:m + 1], acc[:, P * m:P * (m + 1)], ones[:, 0:1], start=True, stop=True)
                end(ins)

            def gate_rows(l):
                pe.wait_ge(diag_ready, l + 1)
                b0, b1 = begin(f"gateb{l}")
                product(b0, [(ones[:], gate_b[:, 0:512])])
                end(product(b1, [(ones[:], gate_b[:, 512:1024])]))

            pe.wait_ge(pool_set, 3)
            pe.wait_ge(prow_in, 16 * 10)
            b0, _ = begin("params")
            end(pe.transpose(b0[:, 0:NROWS], prow[0:NROWS, :], ident[0:NROWS, 0:NROWS]))
            b0, _ = begin("taps")
            end(pe.transpose(b0[:, 0:24], prow2[0:24, :], ident[0:24, 0:24]))
            modulation(0, 0)
            pe.wait_ge(consts_in, 48)
            pe.wait_ge(prow_set, 1)
            for g in range(3):
                b0, _ = begin(f"toep{g}")
                end(product(b0[0:HPG, :], [(relb[0:NB + 1, HPG * g:HPG * (g + 1)], bsel[0:NB + 1, g, :])]))
            for s in range(1, 6):
                modulation(0, s)
            pe.wait_ge(x_in, 16)
            for t in range(NT):
                turn_tile(0, t)

            def qkv(g, i):
                if g == 0 and i == 0:
                    ht_wait(pe, 0)
                t = 0 if i < 3 else 1 if i < 6 else 2
                turn = TURN[("win_a", 0, (t, g))]
                landed(pe, turn)
                w = shaped(turn, DC, GW)
                if t < 2:
                    c = i - 3 * t
                    feature_major(f"qkv{g}_{i}", w, slice(P * c, P * (c + 1)), WHOLE)
                else:
                    n = i - 6
                    b0, _ = begin(f"qkv{g}_{i}")
                    view = HT[:, :, META:TM] if g == 0 else None
                    lhs = [(HT[:, k, META + P * n:META + P * (n + 1)] if g == 0 else
                            HT[:, k, META + n:TM:4]) for k in range(DC)]
                    end(product(b0[:, 0:GW], [(lhs[k], w[:, k, :]) for k in range(DC)]))

            def sg_a_job(c):
                turn = TURN[("win_a", 0, (3, c // 3))]
                landed(pe, turn)
                feature_major(f"sgA_{c}", shaped(turn, DC, GW), slice(P * (c % 3), P * (c % 3 + 1)), WHOLE)

            def scores_a(u):
                g, h, n = UNITS_A[u]
                if h == 0 and (n or 0) == 0:
                    taken(pe, f"qkv{g}_8")
                    taken(pe, f"qkv{g}_9")
                if u >= 2:
                    pe.wait_ge(scores_read, u - 1)
                b = ps[:, 4 + u % 2, :]
                lo, c = 64 * (h % 2), h // 2
                q, k = q_g[g][lo:lo + 64, c, :], k_g[g][lo:lo + 64, c, :]
                if g == 0:
                    k0, k1 = max(0, n - 1), min(NT, n + 2)
                    ins = pe.matmul(b[:, 0:P * (k1 - k0)], q[:, P * n:P * (n + 1)], k[:, P * k0:P * k1], start=True, stop=True)
                else:
                    for n in range(NT):
                        t = slice(P * n, P * (n + 1))
                        ins = pe.matmul(b[:, t], q[:, t], k[:, t], start=True, stop=True)
                ins.then_inc(scores_ready, 1)

            def width_a(u):
                g, _, n = UNITS_A[u]
                return 512 if g else P * (min(NT, n + 2) - max(0, n - 1))

            def turn_probs(u, sp, width):
                pe.wait_ge(probs_ready, u + 1)
                if u >= 2:
                    pe.wait_ge(pt_copied, u - 1)
                b = ps[:, (6, 1)[u % 2], :]
                for i in range(width // P):
                    ins = pe.transpose(b[:, P * i:P * (i + 1)], sp[u % 3][:, P * i:P * (i + 1)], ident[:])
                ins.then_inc(pt_ready, 1)

            def pv_a(u):
                g, h, n = UNITS_A[u]
                pe.wait_ge(pt_copied, u + 1)
                pair = (3 * g + h // 2)
                first = h % 2 == 0 and (n or 0) == 0
                if first and pair >= 2:
                    pe.wait_ge(o_copied, pair - 1)
                o = ps[64 * (h % 2):64 * (h % 2) + 64, (7, 3)[pair % 2], :]
                pT = pT_a[u % 2]
                hs = slice(HD * h, HD * (h + 1))
                if g == 0:
                    k0, k1 = max(0, n - 1), min(NT, n + 2)
                    ins = product(o[:, P * n:P * (n + 1)], [(v_g[g][:, k, hs], pT[:, P * (k - k0):P * (k - k0 + 1)]) for k in range(k0, k1)])
                else:
                    for n in range(NT):
                        t = slice(P * n, P * (n + 1))
                        ins = pe.matmul(o[:, t], v_g[g][:, n, hs], pT[:, t], start=True, stop=True)
                ins.then_inc(pv_done, 1)

            for i in range(10):
                qkv(0, i)
            for u in range(NUA + 2):
                if u < NUA:
                    scores_a(u)
                for name in FILL_A.get(u, []):
                    if name[:3] == "qkv":
                        qkv(int(name[3]), int(name[5:]))
                    elif name[:3] == "mod":
                        modulation(1, int(name[5:]))
                    elif name == "gateb0":
                        gate_rows(0)
                    else:
                        sg_a_job(int(name[4:]))
                if 1 <= u <= NUA:
                    turn_probs(u - 1, sp_a, width_a(u - 1))
                if u >= 2:
                    pv_a(u - 2)

            pe.wait_ge(probs_ready, NUA)
            for g in range(3):
                for name, src in (("negmax", negm), ("den", den)):
                    b0, _ = begin(f"{name}{g}")
                    for n in range(NT):
                        ins = pe.transpose(b0[0:HPG, P * n:P * (n + 1)], src[:, g, n, :], ident[:])
                    end(ins)
            pe.wait_ge(factors_ready, 1)
            for c in range(9):
                b0, _ = begin(f"fac_{c}")
                end(product(b0, [(hsel[:, c % 3, :], rows_m[0:HPG, c // 3, :])]))
            turns = [TURN[("wout_a", 0, s)] for s in range(3)]
            for t in turns:
                landed(pe, t)
            parts = [(shaped(turns[k // 4], 4 if k < 8 else 1, D), k % 4) for k in range(9)]
            taken(pe, "fac_7")
            taken(pe, "fac_8")
            pe.wait_ge(pt_copied, NUA)
            pe.wait_ge(o_copied, 9)
            out_and_turn(1, 0, range(NT), lambda t: token_major(f"outA_{t}", t, lambda k: oT_a[:, k, P * t:P * (t + 1)], parts))

            ht_wait(pe, 1)
            t0 = TURN[("win_b", 0, 0)]
            landed(pe, t0)
            w = shaped(t0, DC, 416)
            for c in range(4):
                feature_major(f"lat_{c}", w, slice(P * c, P * c + (P if c < 3 else ROPE)), WHOLE, m=P if c < 3 else ROPE)
            pe.wait_ge(lat_sq, 3)
            b0, _ = begin("rms0")
            end(product(b0, [(ones[:], sgB[:, 0, :]), (ones[:], sgB[:, 1, :])]))
            b0, _ = begin("rms1")
            end(product(b0, [(ones[:], sgB[:, 2, :])]))
            gate_rows(1)
            tkv, tq_ = TURN[("ukv", 0, 0)], TURN[("uq", 0, 0)]
            landed(pe, tkv)
            landed(pe, tq_)
            wkv = slab(tkv)[:, 0:2048]
            wv = wkv.rearrange("p (h x f) -> p h x f", h=HB, x=2)
            wq = shaped(tq_, 2, HB * QW)
            pe.wait_ge(lat_ready, 3)
            for t in range(NT):
                b0, b1 = begin(f"vB_{t}")
                for h, b in enumerate((b0, b1)):
                    ins = pe.matmul(b, latB[:, 2, P * t:P * (t + 1)], wv[:, 8 * h:8 * h + 8, 1, :], start=True, stop=True)
                end(ins)
            for i in range(4):
                b0, _ = begin(f"qr_{i}")
                for r in range(4):
                    o = QW * (4 * i + r) + NOPE
                    ins = product(b0[32 * r:32 * r + 32, :], [(wq[:, k, o:o + ROPE], latB[:, k, :]) for k in range(2)])
                end(ins)
            for c in range(DC):
                turn = TURN[("win_b", 0, 1 + c // 4)]
                landed(pe, turn)
                feature_major(f"sgB_{c}", shaped(turn, DC, 512), slice(P * (c % 4), P * (c % 4 + 1)), WHOLE)

            def qn_kn(hp):
                b0, _ = begin(f"qn_{hp}")
                for r in range(2):
                    o = QW * (2 * hp + r)
                    ins = product(b0[64 * r:64 * r + 64, :], [(wq[:, k, o:o + NOPE], latB[:, k, :]) for k in range(2)])
                end(ins)
                b0, _ = begin(f"kn_{hp}")
                for r in range(2):
                    ins = product(b0[64 * r:64 * r + 64, :], [(wv[:, 2 * hp + r, 0, :], latB[:, 2, :])])
                end(ins)

            def scores_b(u):
                h, t = u // NT, u % NT
                U = NUA + u
                if t == 0:
                    if h == 0:
                        pe.wait_ge(qr_ready, 4)
                        pe.wait_ge(kr_ready, 4)
                        taken(pe, "vB_2")
                        taken(pe, "vB_3")
                    if h % 2 == 0:
                        taken(pe, f"qn_{h // 2}")
                        taken(pe, f"kn_{h // 2}")
                pe.wait_ge(scores_read, U - 1)
                b = ps[:, 4 + U % 2, :]
                lo, hp, r = 64 * (h % 2), (h // 2) % 3, 32 * (h % 4)
                tt = slice(P * t, P * (t + 1))
                pe.matmul(b, qnB[hp][lo:lo + 64, tt], knB[hp][lo:lo + 64, :], start=True, stop=False)
                pe.matmul(b, qrB[r:r + 32, h // 4, tt], krB[r:r + 32, :], start=False, stop=True)\
                  .then_inc(scores_ready, 1)

            def pv_b(u):
                h, t = u // NT, u % NT
                U = NUA + u
                pe.wait_ge(pt_copied, U + 1)
                pair = h // 2 + 9
                if h % 2 == 0 and t == 0:
                    pe.wait_ge(o_copied, pair - 1)
                o = ps[64 * (h % 2):64 * (h % 2) + 64, (7, 3)[pair % 2], :]
                product(o[:, P * t:P * (t + 1)], [(vB[:, k, HD * h:HD * (h + 1)], pT_b[U % 2][:, P * k:P * (k + 1)]) for k in range(NT)])\
                    .then_inc(pv_done, 1)

            qn_kn(0)
            qn_kn(1)
            pe.wait_ge(proj_free[0], (JOB["kn_1"] + 2) // 2)
            pe.wait_ge(proj_free[1], (JOB["kn_1"] + 1) // 2)
            for u in range(NUB + 3):
                if u < NUB:
                    scores_b(u)
                if u % 8 == 4 and u // 8 + 2 < 8:
                    qn_kn(u // 8 + 2)
                if 2 <= u < NUB + 2:
                    turn_probs(NUA + u - 2, sp_b, 512)
                if u >= 3:
                    pv_b(u - 3)
            pe.wait_ge(pt_copied, NUA + NUB)
            pe.wait_ge(o_copied, 17)
            turns = [TURN[("wout_b", 0, s)] for s in range(2)]
            for t in turns:
                landed(pe, t)
            pe.wait_ge(meta_in, 16)
            turn_tile(2, 4)
            out_and_turn(2, 1, range(NT), lambda t: token_major(f"outB_{t}", t, lambda k: oT_b[:, k, P * t:P * (t + 1)],
                                                                [(shaped(turns[k // 4], 4, D), k % 4) for k in range(DC)]))

            ht_wait(pe, 2)

            def lru_gates(c):
                pe.wait_ge(bd_in[c % 2], 16 * 4 * (c // 2 + 1))
                pe.wait_ge(xc_ready, c + 1)
                for i, name in enumerate(("ra", "ri")):
                    b0, b1 = begin(f"{name}_{c}")
                    for h, b in enumerate((b0, b1)):
                        ins = pe.matmul(b[:, 0:264], wa_bd[:, c % 2, i, :], xc[:, 264 * h:264 * h + 264], start=True, stop=True)
                    end(ins)

            for c in range(DC):
                for s, name in ((c // 4, "uy"), (2 + c // 4, "ux")):
                    turn = TURN[("lru_in", 0, s)]
                    landed(pe, turn)
                    feature_major(f"{name}_{c}", shaped(turn, DC, 512), slice(P * (c % 4), P * (c % 4 + 1)), BOTH)
                if c:
                    lru_gates(c - 1)
            lru_gates(7)
            turns = [TURN[("lru_out", 0, s)] for s in range(2)]
            for t in turns:
                landed(pe, t)
            pe.wait_ge(yT_ready, DC)
            out_and_turn(3, 2, (4, 0, 1, 2, 3), lambda t: token_major(f"outC_{t}", t, lambda k: yT[:, k, tokens(t)],
                                                                      [(shaped(turns[k // 4], 4, D), k % 4) for k in range(DC)]))

            def route(l):
                tiles = range(5 if l == 0 else 4)
                ht_wait(pe, (3, 5)[l])
                pe.wait_ge(rw_in, 16 * 8)
                b0, _ = begin(f"router{l}")
                for t in tiles:
                    ins = product(b0[0:rows_of(t), 36 * t:36 * t + 36], [(HT[:, k, tokens(t)], rw[:, l, k, :]) for k in range(DC)])
                end(ins)
                pe.wait_ge(onehot_ready, l + 1)
                b0, _ = begin(f"ranks{l}")
                for t in tiles:
                    product(b0[:, NE * t:NE * (t + 1)], [(before[:], ohb[:, t, :])] + [(ones_h[:], ohb[:, s, :]) for s in range(t)])
                end(product(b0[:, 160:192], [(ones_h[:], ohb[:, s, :]) for s in tiles]))

            def turn_slots(E, par):
                pe.wait_ge(xe_landed[par], (E - par) * 8 + 16)
                pe.wait_ge(xet_copied, E)
                for c in range(DC):
                    ins = pe.transpose(ps[:, c // 4, P * (c % 4):P * (c % 4 + 1)], xe[par][:, P * c:P * (c + 1)], ident[:])
                ins.then_inc(xe_used, 1)

            def up_down(w, src, dst):
                for f in range(FC):
                    ins = product(dst[:, P * f:P * (f + 1)], [(w[:, k, P * f:P * (f + 1)], src[:, k, :]) for k in range(DC)])
                return ins

            def down(w, par):
                for h in range(2):
                    ins = product(ps[:, 6 + h, :], [(hb[par][:, k, :], w[:, k, 512 * h:512 * h + 512]) for k in range(FC)])
                return ins

            def expert(l, e, par, base, with_next=True):
                E = NE * l + e
                turn = [base + 3 * par + w for w in range(3)]
                def wait_slab(w):
                    pe.wait_ge(slab_landed[turn[w] % SLABS], (e - par) * 8 + 16 * (turn[w] // SLABS + 1))
                wait_slab(0)
                pe.wait_ge(xet_copied, E + 1)
                if not (isinstance(E, int) and E < 2):
                    pe.wait_ge(hb_ready, E - 1)
                g, u = ps[:, 2 + 2 * par, :], ps[:, 3 + 2 * par, :]
                up_down(expert_slab(turn[0], 0), xeT[par], g).then_inc(gate_ready, 1)
                wait_slab(1)
                up_down(expert_slab(turn[1], 1), xeT[par], u).then_inc(up_ready, 1)
                if with_next:
                    turn_slots(E + 1, 1 - par)
                wait_slab(2)
                pe.wait_ge(hb_ready, E + 1)
                pe.wait_ge(yo_ready, E)
                down(expert_slab(turn[2], 2), par).then_inc(y_ready, 1)

            def over_blocks(l):
                o, base = ov[l], TURN[("expert", l, (0, 0))]
                pe.wait_ge(route_ready, l + 1)
                n_over = pe.value_load(over_i[0:1, 8:9], min_val=0, max_val=NOVER)
                for j in range(NOVER):
                    with pe.If(n_over > j):
                        pe.wait_ge(o["x"], 16 * (j + 1))
                        for c in range(DC):
                            ins = pe.transpose(ps[:, c // 4, P * (c % 4):P * (c % 4 + 1)], xe[0][:, P * c:P * (c + 1)], ident[:])
                        ins.then_inc(o["xt"], 1)
                        pe.wait_ge(o["xc"], j + 1)
                        pe.wait_ge(o["w"], 48 * (j + 1))
                        up_down(expert_slab(base, 0), xeT[0], ps[:, 2, :]).then_inc(o["g"], 1)
                        up_down(expert_slab(base + 1, 1), xeT[0], ps[:, 3, :]).then_inc(o["g"], 1)
                        pe.wait_ge(o["h"], j + 1)
                        down(expert_slab(base + 2, 2), 0).then_inc(o["y"], 1)
                        pe.wait_ge(o["yo"], j + 1)
                    with pe.Else():
                        pe.nop()

            def experts(l):
                base = TURN[("expert", l, (0, 0))]
                pe.wait_ge(proj_free[0], (count[0] + 1) // 2)
                pe.wait_ge(proj_free[1], count[0] // 2)
                turn_slots(NE * l, 0)
                expert(l, 0, 0, base)
                expert(l, 1, 1, base)
                with pe.Fori(1, NE // 2 - 1) as i:
                    expert(l, i * 2, 0, base)
                    expert(l, i * 2 + 1, 1, base)
                expert(l, NE - 2, 0, base)
                expert(l, NE - 1, 1, base, with_next=False)
                pe.wait_ge(yo_ready, NE * (l + 1))
                over_blocks(l)

            route(0)
            experts(0)

            for t in (4, 0, 1, 2, 3):
                turn_normed(4, 3, t)
            ht_wait(pe, 4)
            HALVES = ((META - 2, META - 2 + 257), (META - 2 + 257, TM))
            for c in range(DC):
                for t, name in ((1, "cg"), (2, "cv"), (0, "bg")):
                    turn = TURN[("sc_in", 0, (t, c // 4))]
                    landed(pe, turn)
                    feature_major(f"{name}_{c}", shaped(turn, DC, 512), slice(P * (c % 4), P * (c % 4 + 1)),
                                  HALVES if t else WHOLE)
            turns = [TURN[("sc_out", 0, s)] for s in range(2)]
            for t in turns:
                landed(pe, t)
            taken(pe, "bg_6")
            taken(pe, "bg_7")
            out_and_turn(5, 4, range(NT), lambda t: token_major(f"outD_{t}", t, lambda k: zT[:, k, P * t:P * (t + 1)],
                                                                [(shaped(turns[k // 4], 4, D), k % 4) for k in range(DC)]))
            route(1)
            experts(1)
            assert count[0] == len(JOBS)

        GELU_C = float(np.sqrt(2.0 / np.pi))
        ztmp = at(R0 + 13056, D)
        O_LAST = {}
        for u, (g, h, n) in enumerate(UNITS_A):
            O_LAST[3 * g + h // 2] = u
        for p_ in range(8):
            O_LAST[9 + p_] = NUA + 8 * p_ + 7
        O_AT = {u: p_ for p_, u in O_LAST.items()}

        def halves(ap2):
            return ap2.rearrange("p (a b) -> p a b", a=2)

        def job_bank(name, n=512):
            return ps[:, bank(name), 0:n]

        def job_pair(name, n=512):
            return ps[:, bank(name):bank(name) + 2, 0:n]

        def col(name, i=0):
            return cols[:, PROWS[name] + i:PROWS[name] + i + 1]

        def by_residue(ap2):
            return ap2.rearrange("p (l j) -> p j l", j=4)

        def tiles4(ap2):
            return ap2.rearrange("p (j l) -> p j l", j=4)

        @block.scalar
        def _(act):
            own = [0]

            def mark(ins):
                own[0] += 1
                ins.then_inc(act_own, 1)

            def settle():
                act.wait_ge(act_own, own[0])

            def free(ins, name):
                ins.then_inc(proj_free[JOB[name] % 2], 1)

            load_params(act, PARAMS[5:])
            act.dma_start(prow2[0:24, :], a["sc_conv_w_2"][0].rearrange("k (r p) -> (k r) p", p=P)).then_inc(prow_in, 16)
            act.dma_start(bsel[0:NB + 1, :, :], a["bucket_sel"]).then_inc(consts_in, 16)
            act.dma_start(hsel, a["head_sel"]).then_inc(consts_in, 16)
            act.dma_start(relb[0:NB, :], a["rel_bias"]).then_inc(consts_in, 16)
            act.dma_start(x_first, a["x"][0].rearrange("(t p) d -> p t d", p=P)).then_inc(x_in, 16)

            taken(act, "params")
            act.activation(csilu[:, 0, :], cols[:, PROWS["c"]:PROWS["c"] + DC], ACT.Tanh, scale=0.5).then_inc(lam_a, 1)
            act.wait_ge(lam_b, 1)
            mark(act.activation(lamc[:, 1, :], lamc[:, 0, :], ACT.Exp, scale=-1.0))
            settle()
            act.activation(lamc[:, 2, :], lamc[:, 1, :], ACT.Ln, bias=1.0).then_inc(lam_a, 1)

            def turn_copy(k, t):
                n = TURNED[(k, t)]
                r = rows_of(t)
                act.wait_ge(turned, 2 * n + 1)
                src = turn_bank(n, 0)
                if k >= 2:
                    ins = act.activation(HT[:, 0:4, tokens(t)], src[:, 0:4 * r].rearrange("p (c t) -> p c t", t=r), ACT.Copy)
                else:
                    for c in range(4):
                        ins = act.activation(HT[:, c, tokens(t)], src[:, P * c:P * (c + 1)], ACT.Identity,
                                             bias=mod[:, k, c:c + 1], scale=mod[:, k, 8 + c:9 + c])
                        if c < 3:
                            mark(ins)
                ins.then_inc(turn_copied[0], 1)

            def normed_and_turned(k, l, order):
                for i, t in enumerate(order):
                    deviation(l, t)
                    if i:
                        turn_copy(k, order[i - 1])
                turn_copy(k, order[-1])

            def deviation(l, t):
                n = LN[(l, t)]
                act.wait_ge(var_ready, n + 1)
                r, o = rows_of(t), 32 * (n % 2)
                act.activation(spec[0:r, o + 15:o + 16], spec[0:r, o + 14:o + 15], ACT.Sqrt).then_inc(sd_ready, 1)
                if l in (3, 5):
                    m = COMBINED[(l, t)]
                    act.wait_ge(scale_ready, m + 1)
                    act.activation(X[0:r, t, :], X[0:r, t, :], ACT.Identity, scale=spec[0:r, o + 16:o + 17],
                                   bias=spec[0:r, o + 17:o + 18]).then_inc(normed, 1)

            taken(act, "mod0_4")
            taken(act, "mod0_5")
            for t in range(NT):
                turn_copy(0, t)

            def qkv_out(g, i):
                name = f"qkv{g}_{i}"
                done(act, name)
                if i == 0 and g == 2:
                    act.wait_ge(pv_done, 24)
                if i < 6:
                    dst = (q_g if i < 3 else k_g)[g][:, i % 3, :]
                    src = job_bank(name)
                    if g:
                        dst, src = tiles4(dst), by_residue(src)
                    free(act.activation(dst, src, ACT.Copy), name)
                else:
                    free(act.activation(v_g[g][:, i - 6, :], job_bank(name, GW), ACT.Copy), name)

            def silu_tanh(name, dst, n=512):
                done(act, name)
                act.activation(dst, job_bank(name, n), ACT.Tanh, scale=0.5).then_inc(silu_ready, 1)

            def pt_copy(U, pT):
                act.wait_ge(pt_ready, U + 1)
                if U >= 2:
                    act.wait_ge(pv_done, U - 1)
                w = 512 if U >= NUA or UNITS_A[U][0] else P * (min(NT, UNITS_A[U][2] + 2) - max(0, UNITS_A[U][2] - 1))
                act.activation(pT[U % 2][:, 0:w], ps[:, (6, 1)[U % 2], 0:w], ACT.Copy).then_inc(pt_copied, 1)

            for i in range(10):
                qkv_out(0, i)
            for u in range(NUA + 1):
                if u < NUA:
                    g, h, n = UNITS_A[u]
                    act.wait_ge(max_ready, u + 1)
                    sp = sp_a[u % 3]
                    if g == 0:
                        w = P * (min(NT, n + 2) - max(0, n - 1))
                        act.activation(sp[:, 0:w], sp[:, 0:w], ACT.Exp, bias=negm[:, 0, n, h:h + 1],
                                       accum_out=den[:, 0, n, h:h + 1]).then_inc(probs_ready, 1)
                    else:
                        for n in range(NT):
                            t = slice(P * n, P * (n + 1))
                            ins = act.activation(sp[:, t], sp[:, t], ACT.Exp, bias=negm[:, g, n, h:h + 1],
                                                 accum_out=den[:, g, n, h:h + 1])
                            if n < NT - 1:
                                mark(ins)
                        ins.then_inc(probs_ready, 1)
                for name in FILL_A.get(u, []):
                    if name[:3] == "qkv":
                        qkv_out(int(name[3]), int(name[5:]))
                    elif name[:3] == "sgA":
                        if name == "sgA_0":
                            act.wait_ge(pv_done, 30)
                        silu_tanh(name, sg_a[:, int(name[4:]), :])
                if u >= 1:
                    pt_copy(u - 1, pT_a)
            act.wait_ge(fac_in, 1)
            act.activation(at(R0 + 9216, 3 * S)[0:HPG, :], at(R0 + 9216, 3 * S)[0:HPG, :], ACT.Exp).then_inc(fac_exp, 1)

            normed_and_turned(1, 0, range(NT))

            for c in range(3):
                done(act, f"lat_{c}")
                act.activation(sgB[:, c, :], job_bank(f"lat_{c}"), ACT.Square).then_inc(lat_sq, 1)
            act.wait_ge(kr_ready, 1)
            for r in range(1, 4):
                act.activation(krB[32 * r:32 * r + 32, :], krB[0:32, :], ACT.Copy).then_inc(kr_ready, 1)
            for i in range(2):
                taken(act, f"rms{i}")
                act.activation(tmpB[i], tmpB[i], ACT.Sqrt).then_inc(rms_sd, 1)
            act.wait_ge(x1_out, 64)
            for t in range(NT):
                done(act, f"vB_{t}")
                free(act.activation(halves(vB[:, t, :]), job_pair(f"vB_{t}"), ACT.Copy), f"vB_{t}")
            for c in range(DC):
                silu_tanh(f"sgB_{c}", sgB[:, c, :])

            def qn_kn_out(hp):
                for name, dst in ((f"qn_{hp}", qnB[hp % 3]), (f"kn_{hp}", knB[hp % 3])):
                    done(act, name)
                    if hp >= 3:
                        act.wait_ge(scores_ready, NUA + 8 * (hp - 2))
                    free(act.activation(dst, job_bank(name), ACT.Copy), name)

            qn_kn_out(0)
            qn_kn_out(1)
            for u in range(NUB + 2):
                if u < NUB:
                    U = NUA + u
                    act.wait_ge(max_ready, U + 1)
                    act.wait_ge(pt_ready, U - 2)
                    act.activation(sp_b[U % 3], ps[:, 4 + U % 2, :], ACT.Exp, bias=nmax[:, 4 + U % 4:5 + U % 4],
                                   scale=SCALE_B, accum_out=dsum[:, U % 4:U % 4 + 1]).then_inc(scores_read, 1)
                if u % 8 == 4 and u // 8 + 2 < 8:
                    qn_kn_out(u // 8 + 2)
                if u >= 2:
                    pt_copy(NUA + u - 2, pT_b)
            turn_copy(2, 4)
            normed_and_turned(2, 1, range(NT))

            def lru_decay(c):
                if c >= 2:
                    act.wait_ge(yT_ready, c - 1)
                for name, dst, hbias in ((f"ra_{c}", sT, 0), (f"ri_{c}", gx, 1)):
                    done(act, name)
                    free(act.activation(halves(dst[:, c % 2, :]), job_pair(name, 264), ACT.Tanh, scale=0.5,
                                        bias=half_b[:, hbias, c:c + 1]), name)
                taken(act, f"ra_{c}")
                act.activation(sT[:, c % 2, :], sT[:, c % 2, :], ACT.Tanh, scale=lamc[:, 0, c:c + 1], bias=lamc[:, 0, c:c + 1])\
                   .then_inc(s_ready, 1)
                act.wait_ge(s_ready, c + 1)
                act.activation(root[:, c % 2, :], sT[:, c % 2, :], ACT.Sqrt, scale=-1.0).then_inc(root_ready, 1)

            for c in range(DC):
                done(act, f"uy_{c}")
                if c:
                    taken(act, f"uy_{c - 1}")
                act.activation(halves(tA), job_pair(f"uy_{c}", 264), ACT.Square).then_inc(gelu_sq, 1)
                act.wait_ge(gelu_in, c + 1)
                act.activation(tB, tB, ACT.Tanh, scale=GELU_C).then_inc(gelu_th, 1)
                done(act, f"ux_{c}")
                if c:
                    act.wait_ge(xc_ready, c)
                free(act.activation(halves(upad[:, 3:TM + 3]), job_pair(f"ux_{c}", 264), ACT.Copy), f"ux_{c}")
                if c:
                    lru_decay(c - 1)
            lru_decay(7)
            normed_and_turned(3, 2, (4, 0, 1, 2, 3))

            def xet_copy(E, par, first=False):
                act.wait_ge(xe_used, E + 1)
                if not first:
                    act.wait_ge(up_ready, E - 1)
                act.activation(xeT[par], ps[:, 0:2, :].rearrange("p a (b c) -> p (a b) c", c=P), ACT.Copy).then_inc(xet_copied, 1)

            def expert(l, e, par, with_next=True):
                E = NE * l + e
                early = isinstance(E, int) and E < 2
                act.wait_ge(gate_ready, E + 1)
                if not early:
                    act.wait_ge(hb_ready, E - 1)
                act.activation(zg[par], ps[:, 2 + 2 * par, :], ACT.Tanh, scale=0.5).then_inc(tanh_ready, 1)
                if with_next:
                    xet_copy(E + 1, 1 - par, first=isinstance(E, int) and E + 1 < 2)
                act.wait_ge(y_ready, E + 1)
                if not early:
                    act.wait_ge(yo_sent[par], (E - par) * 8)
                act.activation(halves(yo[par]), ps[:, 6:8, :], ACT.Copy).then_inc(yo_ready, 1)

            def experts(l):
                xet_copy(NE * l, 0, first=l == 0)
                expert(l, 0, 0)
                expert(l, 1, 1)
                with act.Fori(1, NE // 2 - 1) as i:
                    expert(l, i * 2, 0)
                    expert(l, i * 2 + 1, 1)
                expert(l, NE - 2, 0)
                expert(l, NE - 1, 1, with_next=False)
                o = ov[l]
                act.wait_ge(route_ready, l + 1)
                n_over = act.value_load(over_i[0:1, 8:9], min_val=0, max_val=NOVER)
                for j in range(NOVER):
                    with act.If(n_over > j):
                        act.wait_ge(o["xt"], j + 1)
                        act.activation(xeT[0], ps[:, 0:2, :].rearrange("p a (b c) -> p (a b) c", c=P), ACT.Copy).then_inc(o["xc"], 1)
                        act.wait_ge(o["g"], 2 * j + 1)
                        act.activation(zg[0], ps[:, 2, :], ACT.Tanh, scale=0.5).then_inc(o["t"], 1)
                        act.wait_ge(o["y"], j + 1)
                        if j == 0:
                            act.wait_ge(yo_sent[0], 8 * NE * (l + 1))
                        else:
                            act.wait_ge(o["out"], 16 * j)
                        act.activation(halves(yo[0]), ps[:, 6:8, :], ACT.Copy).then_inc(o["yo"], 1)
                    with act.Else():
                        act.nop()

            def route(l):
                act.wait_ge(pg_in, l + 1)
                mark(act.activation(adr[:, :, 0:NG], adr[:, :, 0:NG], ACT.Exp))
                act.activation(sm[:, 5, :], sm[:, 4, :], ACT.Exp).then_inc(pg_exp, 1)

            route(0)
            experts(0)
            normed_and_turned(4, 3, (4, 0, 1, 2, 3))
            for c in range(DC):
                done(act, f"cg_{c}")
                if c >= 2:
                    taken(act, f"cv_{c - 2}")
                free(act.activation(halves(cgs[c % 2]), job_pair(f"cg_{c}", 257), ACT.Copy), f"cg_{c}")
            normed_and_turned(5, 4, range(NT))
            route(1)
            experts(1)
            for t in range(NT):
                deviation(5, t)

        @block.vector
        def _(vec):
            own = [0]

            def mark(ins):
                own[0] += 1
                ins.then_inc(vec_own, 1)

            def settle():
                vec.wait_ge(vec_own, own[0])

            def step(ins):
                mark(ins)
                settle()

            def free(ins, name):
                ins.then_inc(proj_free[JOB[name] % 2], 1)

            done(vec, "params")
            free(vec.tensor_copy(cols[:, 0:NROWS], job_bank("params", NROWS)), "params")
            done(vec, "taps")
            free(vec.tensor_copy(cols[:, SC0:SC0 + 24], job_bank("taps", 24)), "taps")
            taken(vec, "params")
            taken(vec, "taps")
            lam = cols[:, PROWS["lam"]:PROWS["lam"] + DC]
            vec.scalar_tensor_tensor(lamc[:, 0, :], lam, -1.0, lam, ALU.mult, ALU.max).then_inc(lam_b, 1)
            mark(vec.tensor_scalar(lamc[:, 3, :], lam, -1.0, 0.0, ALU.mult, ALU.max))
            for i, n in enumerate(("b_a", "b_i")):
                mark(vec.tensor_scalar(half_b[:, i, :], cols[:, PROWS[n]:PROWS[n] + DC], 0.5, None, ALU.mult))
            vec.wait_ge(lam_a, 1)
            step(vec.scalar_tensor_tensor(csilu[:, 0, :], csilu[:, 0, :], 1.0, cols[:, PROWS["c"]:PROWS["c"] + DC], ALU.add, ALU.mult))
            vec.tensor_scalar(csilu[:, 1, :], csilu[:, 0, :], 0.5, None, ALU.mult).then_inc(csilu_ready, 1)
            vec.wait_ge(lam_a, 2)
            step(vec.tensor_tensor(lamc[:, 0, :], lamc[:, 3, :], lamc[:, 2, :], ALU.add))
            step(vec.tensor_scalar(lamc[:, 0, :], lamc[:, 0, :], -2.0, None, ALU.mult))

            def modulation_sum(l, s):
                turn = TURN[("ada", l, s)]
                w = shaped(turn, DC, 512)
                landed(vec, turn)
                step(vec.tensor_scalar(w[:, 0, :], w[:, 0, :], csilu[:, 1, 0:1], None, ALU.mult))
                for k in range(1, DC):
                    ins = vec.scalar_tensor_tensor(w[:, 0, :], w[:, k, :], csilu[:, 1, k:k + 1], w[:, 0, :], ALU.mult, ALU.add)
                    if k < DC - 1:
                        step(ins)
                ins.then_inc(mod_sum, 1)

            def modulation(l, s):
                name = f"mod{l}_{s}"
                done(vec, name)
                o = PROWS["ada_b"] + 24 * l + 4 * s
                free(vec.scalar_tensor_tensor(mod[:, l, 4 * s:4 * s + 4], job_bank(name, 4), 1.0 if s in (2, 3) else 0.0,
                                              cols[:, o:o + 4], ALU.add, ALU.add), name)

            def turn_copy(k, t):
                n = TURNED[(k, t)]
                r = rows_of(t)
                vec.wait_ge(turned, 2 * n + 2)
                src = turn_bank(n, 1)
                if k >= 2:
                    ins = vec.tensor_copy(HT[:, 4:8, tokens(t)], src[:, 0:4 * r].rearrange("p (c t) -> p c t", t=r))
                else:
                    for c in range(4):
                        ins = vec.tensor_scalar(HT[:, 4 + c, tokens(t)], src[:, P * c:P * (c + 1)], mod[:, k, 12 + c:13 + c],
                                                mod[:, k, 4 + c:5 + c], ALU.mult, ALU.add)
                        if c < 3:
                            mark(ins)
                ins.then_inc(turn_copied[1], 1)

            def finish_and_turn(k, order, finish):
                for i, t in enumerate(order):
                    finish(t)
                    if i:
                        turn_copy(k, order[i - 1])
                affine_last(k - 1, order[-1])
                turn_copy(k, order[-1])

            def affine_last(l, t):
                n = LN[(l, t)]
                x = X[:, t, :]
                vec.wait_ge(normed, n + 1)
                vec.wait_ge(lnp_in, 32 * (l + 1))
                step(vec.tensor_tensor(x, x, lnp[:, 0, :], ALU.mult))
                vec.wait_ge(ln_done, n)
                vec.tensor_tensor(x, x, lnp[:, 1, :], ALU.add).then_inc(ln_done, 1)

            def gate_diagonals(l):
                for c in range(DC):
                    ins = vec.tensor_scalar(gate_b[:, P * c:P * (c + 1)], ident[:], mod[:, l, 16 + c:17 + c], None, ALU.mult)
                    if c < DC - 1:
                        mark(ins)
                ins.then_inc(diag_ready, 1)

            def gate_copy(l):
                done(vec, f"gateb{l}")
                free(vec.tensor_copy(halves(gate_b[:]), job_pair(f"gateb{l}")), f"gateb{l}")

            vec.wait_ge(csilu_ready, 1)
            for s in range(6):
                modulation_sum(0, s)
                if s:
                    modulation(0, s - 1)
                if s == 1:
                    for g in range(3):
                        done(vec, f"toep{g}")
                        free(vec.tensor_copy(brow[0:HPG, g, :], job_bank(f"toep{g}")[0:HPG, :]), f"toep{g}")
            modulation(0, 5)
            taken(vec, "mod0_4")
            taken(vec, "mod0_5")
            for t in range(NT):
                turn_copy(0, t)
            vec.wait_ge(pool_set, 3)
            gate_diagonals(0)

            def scores_max_a(u):
                g, h, n = UNITS_A[u]
                vec.wait_ge(scores_ready, u + 1)
                if u == 0:
                    vec.wait_ge(toep_in, 16 * 3)
                if u >= 3:
                    vec.wait_ge(pt_ready, u - 2)
                b, sp = ps[:, 4 + u % 2, :], sp_a[u % 3]
                if g == 0:
                    k0, k1 = max(0, n - 1), min(NT, n + 2)
                    w = P * (k1 - k0)
                    o = P * (k0 - n + 1)
                    vec.scalar_tensor_tensor(sp[:, 0:w], b[:, 0:w], HD ** -0.5, backwards(bias0[:, h, 384 - o - w:384 - o]), ALU.mult, ALU.add)\
                       .then_inc(scores_read, 1)
                    vec.wait_ge(scores_read, u + 1)
                    vec.tensor_reduce(negm[:, 0, n, h:h + 1], sp[:, 0:w], AX.X, ALU.max, negate=True).then_inc(max_ready, 1)
                else:
                    vec.scalar_tensor_tensor(tiles4(sp), tiles4(b), HD ** -0.5, spread(backwards(bias12[g - 1][:, h, :]), 1, NT),
                                             ALU.mult, ALU.add).then_inc(scores_read, 1)
                    vec.wait_ge(scores_read, u + 1)
                    vec.tensor_reduce(negm[:, g, :, h], tiles4(sp), AX.X, ALU.max, negate=True).then_inc(max_ready, 1)

            def o_copy_a(pair):
                vec.wait_ge(pv_done, O_LAST[pair] + 1)
                g = pair // 3
                src, dst = ps[:, (7, 3)[pair % 2], :], oT_a[:, pair, :]
                if g:
                    src, dst = tiles4(src), by_residue(dst)
                vec.tensor_copy(dst, src).then_inc(o_copied, 1)

            def silu_times(name, dst, k):
                vec.wait_ge(silu_ready, k + 1)
                free(vec.scalar_tensor_tensor(dst, dst, 1.0, job_bank(name), ALU.add, ALU.mult), name)

            for u in range(NUA + 2):
                if u < NUA:
                    scores_max_a(u)
                if u + 1 in MOD_AT:
                    modulation_sum(1, MOD_AT.index(u + 1))
                for name in FILL_A.get(u, []):
                    if name[:3] == "sgA":
                        c = int(name[4:])
                        silu_times(name, sg_a[:, c, :], c)
                    elif name[:3] == "mod":
                        modulation(1, int(name[5:]))
                    elif name == "gateb0":
                        gate_copy(0)
                if u >= 3 and (u - 3) in O_AT:
                    o_copy_a(O_AT[u - 3])
            for u in range(NUA - 1, NUA + 2):
                if u in O_AT and u >= NUA - 1:
                    o_copy_a(O_AT[u])

            for g in range(3):
                for name, dst in (("negmax", rows_m), ("den", rows_d)):
                    done(vec, f"{name}{g}")
                    src, d = job_bank(f"{name}{g}")[0:HPG, :], dst[0:HPG, g, :]
                    if g:
                        src, d = tiles4(src), by_residue(d)
                    free(vec.tensor_copy(d, src), f"{name}{g}")
            taken(vec, "negmax2")
            taken(vec, "den2")
            m_, d_, t_, s_ = rows_m[0:HPG], rows_d[0:HPG], rows_t[0:HPG, :], rows_s[0:HPG, :]
            step(vec.tensor_tensor(t_, m_[:, 0, :], m_[:, 1, :], ALU.min))
            step(vec.tensor_tensor(t_, t_, m_[:, 2, :], ALU.min))
            vec.tensor_tensor(m_, spread(t_, 1, 3), m_, ALU.subtract).then_inc(fac_in, 1)
            vec.wait_ge(fac_exp, 1)
            step(vec.tensor_tensor(d_, d_, m_, ALU.mult))
            step(vec.tensor_tensor(s_, d_[:, 0, :], d_[:, 1, :], ALU.add))
            step(vec.tensor_tensor(s_, s_, d_[:, 2, :], ALU.add))
            step(vec.reciprocal(s_, s_))
            vec.tensor_tensor(m_, m_, spread(s_, 1, 3), ALU.mult).then_inc(factors_ready, 1)
            taken(vec, "sgA_7")
            taken(vec, "sgA_8")
            vec.wait_ge(o_copied, 9)
            for c in range(9):
                mark(vec.scalar_tensor_tensor(oT_a[:, c, :], oT_a[:, c, :], 0.5, sg_a[:, c, :], ALU.mult, ALU.mult))
            settle()
            for c in range(9):
                done(vec, f"fac_{c}")
                free(vec.tensor_tensor(oT_a[:, c, :], oT_a[:, c, :], job_bank(f"fac_{c}"), ALU.mult), f"fac_{c}")
            def normalise(l, t):
                n = LN[(l, t)]
                r, o = rows_of(t), 32 * (n % 2)
                x = X[0:r, t, :]
                for h in range(2):
                    mark(vec.bn_stats(spec[0:r, o + 6 * h:o + 6 * h + 6], x[:, 512 * h:512 * h + 512]))
                settle()
                step(vec.bn_aggr(spec[0:r, o + 12:o + 14], spec[0:r, o:o + 12]))
                vec.tensor_scalar(spec[0:r, o + 14:o + 15], spec[0:r, o + 13:o + 14], LN_EPS, None, ALU.add).then_inc(var_ready, 1)
                vec.wait_ge(sd_ready, n + 1)
                step(vec.reciprocal(spec[0:r, o + 16:o + 17], spec[0:r, o + 15:o + 16]))
                if l in (3, 5):
                    vec.scalar_tensor_tensor(spec[0:r, o + 17:o + 18], spec[0:r, o + 12:o + 13], -1.0, spec[0:r, o + 16:o + 17],
                                             ALU.mult, ALU.mult).then_inc(scale_ready, 1)
                    return
                vec.tensor_scalar(x, x, spec[0:r, o + 12:o + 13], spec[0:r, o + 16:o + 17], ALU.subtract, ALU.mult)\
                   .then_inc(normed, 1)

            def gated_residual(l, t, name):
                done(vec, name)
                free(vec.tensor_tensor(halves(ztmp), job_pair(name), halves(gate_b[:]), ALU.mult), name)
                taken(vec, name)
                step(vec.scalar_tensor_tensor(X[:, t, :], X[:, t, :], ALPHA, ztmp, ALU.mult, ALU.add))
                normalise(l, t)

            def residual(l, t, name):
                r = rows_of(t)
                done(vec, name)
                free(vec.scalar_tensor_tensor(halves(X[0:r, t, :]), halves(X[0:r, t, :]), ALPHA, job_pair(name)[0:r],
                                              ALU.mult, ALU.add), name)
                taken(vec, name)
                normalise(l, t)

            taken(vec, "gateb0")
            vec.wait_ge(x_back, 16)
            finish_and_turn(1, range(NT), lambda t: gated_residual(0, t, f"outA_{t}"))
            gate_diagonals(1)

            for c in range(3):
                name = f"lat_{c}"
                done(vec, name)
                vec.wait_ge(lat_sq, c + 1)
                free(vec.tensor_copy(latB[:, c, :], job_bank(name)), name)
            SWAP = [(i + 16) % 32 for i in range(32)]
            vec.wait_ge(rot_in, 16)
            done(vec, "lat_3")
            free(vec.tensor_copy(tmpB[0][0:32, :], job_bank("lat_3")[0:32, :]), "lat_3")
            taken(vec, "lat_3")
            step(vec.stream_shuffle(tmpB[1][0:32, :], tmpB[0][0:32, :], SWAP))
            mark(vec.tensor_tensor(tmpB[0][0:32, :], tmpB[0][0:32, :], rot[0:32, 0, :], ALU.mult))
            step(vec.tensor_tensor(tmpB[1][0:32, :], tmpB[1][0:32, :], rot[0:32, 1, :], ALU.mult))
            vec.tensor_tensor(krB[0:32, :], tmpB[0][0:32, :], tmpB[1][0:32, :], ALU.add).then_inc(kr_ready, 1)
            vec.wait_ge(kr_ready, 1)
            for i, width in enumerate((QL, KVL)):
                done(vec, f"rms{i}")
                free(vec.tensor_scalar(tmpB[i], job_bank(f"rms{i}"), 1.0 / width, RMS_EPS, ALU.mult, ALU.add), f"rms{i}")
            gate_copy(1)
            vec.wait_ge(rms_sd, 2)
            for i in range(2):
                mark(vec.reciprocal(tmpB[i], tmpB[i]))
            settle()
            for c, (gain, i) in enumerate(((col("qn", 0), 0), (col("qn", 1), 0), (col("kvn"), 1))):
                vec.scalar_tensor_tensor(latB[:, c, :], latB[:, c, :], gain, tmpB[i], ALU.mult, ALU.mult).then_inc(lat_ready, 1)
            vec.wait_ge(lat_ready, 3)
            for i in range(4):
                name = f"qr_{i}"
                done(vec, name)
                mark(vec.stream_shuffle(tmpB[1], job_bank(name), SWAP))
                free(vec.tensor_tensor(tmpB[0], job_bank(name), rot[:, 0, :], ALU.mult), name)
                taken(vec, name)
                settle()
                step(vec.tensor_tensor(tmpB[1], tmpB[1], rot[:, 1, :], ALU.mult))
                vec.tensor_tensor(qrB[:, i, :], tmpB[0], tmpB[1], ALU.add).then_inc(qr_ready, 1)
                vec.wait_ge(qr_ready, i + 1)
            for c in range(DC):
                silu_times(f"sgB_{c}", sgB[:, c, :], 9 + c)
            taken(vec, "sgB_6")
            taken(vec, "sgB_7")

            def scores_max_b(U):
                vec.wait_ge(scores_ready, U + 1)
                step(vec.tensor_reduce(nmax[:, U % 4:U % 4 + 1], ps[:, 4 + U % 2, :], AX.X, ALU.max, negate=True))
                vec.tensor_scalar(nmax[:, 4 + U % 4:5 + U % 4], nmax[:, U % 4:U % 4 + 1], SCALE_B, None, ALU.mult).then_inc(max_ready, 1)

            def probs_b(U):
                vec.wait_ge(scores_read, U + 1)
                step(vec.reciprocal(dsum[:, 4 + U % 4:5 + U % 4], dsum[:, U % 4:U % 4 + 1]))
                vec.tensor_scalar(sp_b[U % 3], sp_b[U % 3], dsum[:, 4 + U % 4:5 + U % 4], None, ALU.mult).then_inc(probs_ready, 1)

            def o_copy_b(pair):
                vec.wait_ge(pv_done, O_LAST[pair] + 1)
                vec.scalar_tensor_tensor(oT_b[:, pair - 9, :], ps[:, (7, 3)[pair % 2], :], 0.5, sgB[:, pair - 9, :],
                                         ALU.mult, ALU.mult).then_inc(o_copied, 1)

            for u in range(NUB + 1):
                if u < NUB:
                    scores_max_b(NUA + u)
                if u >= 1:
                    probs_b(NUA + u - 1)
                if u >= 12 and (u - 12) % 8 == 0 and (u - 12) // 8 < 7:
                    o_copy_b(9 + (u - 12) // 8)
            o_copy_b(16)
            vec.wait_ge(x1_back, 16)
            turn_copy(2, 4)
            finish_and_turn(2, range(NT), lambda t: gated_residual(1, t, f"outB_{t}"))

            mark(vec.memset(upad[:, 0:3], 0.0))
            settle()

            def lru_scan(c):
                taken(vec, f"ri_{c}")
                step(vec.scalar_tensor_tensor(gx[:, c % 2, :], gx[:, c % 2, :], 1.0, xc, ALU.add, ALU.mult))
                vec.wait_ge(s_ready, c + 1)
                step(vec.tensor_scalar(xc, sT[:, c % 2, :], -1.0, 1.0, ALU.mult, ALU.add))
                step(vec.reciprocal(xc, xc))
                mark(vec.tensor_tensor(gx[:, c % 2, :], gx[:, c % 2, :], xc, ALU.mult))
                vec.wait_ge(root_ready, c + 1)
                step(vec.scalar_tensor_tensor(sT[:, c % 2, :], sT[:, c % 2, :], 1.0, xc, ALU.add, ALU.mult))
                step(vec.tensor_tensor(gx[:, c % 2, :], gx[:, c % 2, :], root[:, c % 2, :], ALU.mult))
                step(vec.tensor_tensor_scan(sT[:, c % 2, :], sT[:, c % 2, :], gx[:, c % 2, :], 0.0, ALU.mult, ALU.add))
                vec.scalar_tensor_tensor(yT[:, c, :], sT[:, c % 2, :], 0.5, yT[:, c, :], ALU.mult, ALU.mult).then_inc(yT_ready, 1)

            for c in range(DC):
                name = f"uy_{c}"
                done(vec, name)
                vec.wait_ge(gelu_sq, c + 1)
                step(vec.tensor_scalar(tA, tA, 0.044715, 1.0, ALU.mult, ALU.add))
                vec.tensor_tensor(halves(tB), halves(tA), job_pair(name, 264), ALU.mult).then_inc(gelu_in, 1)
                vec.wait_ge(gelu_th, c + 1)
                free(vec.scalar_tensor_tensor(halves(yT[:, c, :]), halves(tB), 1.0, job_pair(name, 264), ALU.add, ALU.mult), name)
                if c:
                    lru_scan(c - 1)
                taken(vec, f"ux_{c}")
                step(vec.tensor_scalar(xc, upad[:, 0:TM], col("conv_w", c), col("conv_b", c), ALU.mult, ALU.add))
                for k in range(1, 4):
                    ins = vec.scalar_tensor_tensor(xc, upad[:, k:TM + k], col("conv_w", 8 * k + c), xc, ALU.mult, ALU.add)
                    if k < 3:
                        step(ins)
                ins.then_inc(xc_ready, 1)
                vec.wait_ge(xc_ready, c + 1)
            lru_scan(7)
            finish_and_turn(3, (4, 0, 1, 2, 3), lambda t: residual(2, t, f"outC_{t}"))

            def route(l):
                tiles = range(5 if l == 0 else 4)
                mark(vec.memset(lg, 0.0))
                mark(vec.memset(ohb, 0.0))
                mark(vec.memset(cnt[:, 3, :], 0.0))
                settle()
                step(vec.memset(lg[:, :, NG:8], NEG))
                name = f"router{l}"
                done(vec, name)
                b = job_bank(name)
                parts = [(P, 0, 4)] + ([(META, 4, 1)] if l == 0 else [])
                for r, t0, nt in parts:
                    src = b[0:r, 36 * t0:36 * (t0 + nt)].rearrange("p (t n) -> p t n", n=36)
                    mark(vec.tensor_tensor(lg[0:r, t0:t0 + nt, 0:NG], src[:, :, 0:NG], spread(rb[0:r, l, 0:NG], 1, nt), ALU.add))
                    ins = vec.tensor_tensor(lg[0:r, t0:t0 + nt, 8:40], src[:, :, NG:36], spread(rb[0:r, l, NG:36], 1, nt), ALU.add)
                    if t0 + nt < len(tiles):
                        mark(ins)
                free(ins, name)
                taken(vec, name)
                settle()
                for t in range(5):
                    mark(vec.max(g8[:, t, :], lg[:, t, 0:8]))
                settle()
                for t in range(5):
                    mark(vec.max_index(gi8[:, t, :], g8[:, t, :], lg[:, t, 0:8]))
                mark(vec.tensor_tensor(adr[:, :, 0:NG], lg[:, :, 0:NG], spread(g8[:, :, 0], 2, NG), ALU.subtract))
                settle()
                step(vec.tensor_copy(sm[:, 1, :], gi8[:, :, 0]))
                for t in range(5):
                    mark(vec.tensor_scalar(tq[:, t, :], group_of[:], sm[:, 1, t:t + 1], None, ALU.is_equal))
                settle()
                step(vec.tensor_tensor(elm, lg[:, :, 8:40], tq, ALU.mult))
                step(vec.tensor_scalar(tq, tq, 1.0, -NEG, ALU.subtract, ALU.mult))
                step(vec.tensor_tensor(elm, elm, tq, ALU.add))
                for t in range(5):
                    mark(vec.max(e8[:, t, :], elm[:, t, :]))
                settle()
                for t in range(5):
                    mark(vec.max_index(ei8[:, t, :], e8[:, t, :], elm[:, t, :]))
                vec.tensor_tensor(sm[:, 4, :], e8[:, :, 1], e8[:, :, 0], ALU.subtract).then_inc(pg_in, 1)
                settle()
                for k in range(2):
                    mark(vec.tensor_copy(sm[:, 2 + k, :], ei8[:, :, k]))
                settle()
                for t in range(5):
                    mark(vec.tensor_scalar(oh1[:, t, :], expert_of[:], sm[:, 2, t:t + 1], None, ALU.is_equal))
                    mark(vec.tensor_scalar(oh2[:, t, :], expert_of[:], sm[:, 3, t:t + 1], None, ALU.is_equal))
                settle()
                if l == 0:
                    mark(vec.tensor_tensor(ohb[0:META, 4, :], oh1[0:META, 4, :], oh2[0:META, 4, :], ALU.add))
                vec.tensor_tensor(ohb[:, 0:4, :], oh1[:, 0:4, :], oh2[:, 0:4, :], ALU.add).then_inc(onehot_ready, 1)
                vec.wait_ge(pg_exp, l + 1)
                step(vec.tensor_reduce(sm[:, 6, :], adr[:, :, 0:NG], AX.X, ALU.add))
                step(vec.scalar_tensor_tensor(sm[:, 7, :], sm[:, 5, :], 1.0, sm[:, 6, :], ALU.add, ALU.mult))
                step(vec.reciprocal(gates[:, 0, :], sm[:, 7, :]))
                mark(vec.tensor_tensor(gates[:, 1, :], gates[:, 0, :], sm[:, 5, :], ALU.mult))
                name = f"ranks{l}"
                done(vec, name)
                b = job_bank(name)
                nt = 5 if l == 0 else 4
                c = b[:, 0:NE * nt].rearrange("p (t n) -> p t n", n=NE)
                A, T_ = adr[:, 0:nt, :], tq[:, 0:nt, :]
                mark(vec.tensor_copy(cnt[:, 0, :], b[:, 160:192]))
                mark(vec.tensor_copy(load_i, b[0:1, 160:192]))
                step(vec.tensor_scalar(T_, c, float(CAP), None, ALU.is_ge))
                for k in range(2, 5):
                    step(vec.scalar_tensor_tensor(T_, c, float(CAP * k), T_, ALU.is_ge, ALU.add))
                step(vec.scalar_tensor_tensor(A, c, float(NBLK), spread(expert_of[:], 1, nt), ALU.mult, ALU.add))
                step(vec.scalar_tensor_tensor(A, T_, 1.0 - CAP * NBLK, A, ALU.mult, ALU.add))
                step(vec.tensor_scalar(cnt[:, 1, :], cnt[:, 0, :], float(CAP), None, ALU.is_gt))
                for k in range(2, 5):
                    step(vec.scalar_tensor_tensor(cnt[:, 1, :], cnt[:, 0, :], float(CAP * k), cnt[:, 1, :], ALU.is_gt, ALU.add))
                step(vec.tensor_tensor_scan(cnt[:, 2, :], cnt[:, 1, :], cnt[:, 3, :], 0.0, ALU.add, ALU.add))
                step(vec.tensor_tensor(cnt[:, 0, :], cnt[:, 2, :], cnt[:, 1, :], ALU.subtract))
                step(vec.scalar_tensor_tensor(cnt[:, 0, :], cnt[:, 0, :], float(NE - 1), expert_of[:], ALU.add, ALU.subtract))
                free(vec.scalar_tensor_tensor(T_, c, float(CAP), spread(cnt[:, 0, :], 1, nt), ALU.is_ge, ALU.mult), name)
                taken(vec, name)
                step(vec.tensor_tensor(A, A, T_, ALU.add))
                for k, oh in enumerate((oh1, oh2)):
                    mark(vec.tensor_tensor(oh[:, 0:nt, :], oh[:, 0:nt, :], A, ALU.mult))
                settle()
                for k, oh in enumerate((oh1, oh2)):
                    mark(vec.tensor_reduce(slf[:, 0:nt, k], oh[:, 0:nt, :], AX.X, ALU.add))
                settle()
                vec.tensor_copy(slots_i[:, 0:2 * nt], slf[:, 0:nt, :].rearrange("p t k -> p (t k)")).then_inc(slots_ready, 1)
                ovt = at(RT + 480, NOVER * NE)[0:1, :].rearrange("p (j e) -> p j e", e=NE)
                step(vec.tensor_tensor(ovt, spread(cnt[0:1, 2, :], 1, NOVER), spread(expert_of[0:1, 0:NOVER], 2, NE), ALU.is_le))
                mark(vec.tensor_copy(ovf[0:1, 8:9], cnt[0:1, 2, NE - 1:NE]))
                step(vec.tensor_reduce(ovf[0:1, 0:8], ovt, AX.X, ALU.add))
                step(vec.tensor_scalar(ovf[0:1, 0:8], ovf[0:1, 0:8], float(NE - 1), None, ALU.min))
                vec.tensor_copy(over_i[0:1, 0:9], ovf[0:1, 0:9]).then_inc(route_ready, 1)
                vec.wait_ge(ids_in, 16 * (l + 1))
                vec.tensor_scalar(slot_tok[:], slot_ids[:], 1, None, ALU.arith_shift_right).then_inc(tok_ready, 1)

            def expert(l, e, par):
                E = NE * l + e
                vec.wait_ge(tanh_ready, E + 1)
                vec.scalar_tensor_tensor(zg[par], zg[par], 1.0, ps[:, 2 + 2 * par, :], ALU.add, ALU.mult).then_inc(zg_ready, 1)
                vec.wait_ge(zg_ready, E + 1)
                vec.wait_ge(up_ready, E + 1)
                if not (isinstance(E, int) and E < 2):
                    vec.wait_ge(y_ready, E - 1)
                vec.scalar_tensor_tensor(hb[par], zg[par].rearrange("p (c t) -> p c t", t=P), 0.5,
                                         ps[:, 3 + 2 * par, :].rearrange("p (c t) -> p c t", t=P), ALU.mult, ALU.mult)\
                   .then_inc(hb_ready, 1)

            def experts(l):
                expert(l, 0, 0)
                expert(l, 1, 1)
                alpha(l)
                with vec.Fori(1, NE // 2) as i:
                    expert(l, i * 2, 0)
                    expert(l, i * 2 + 1, 1)
                o = ov[l]
                n_over = vec.value_load(over_i[0:1, 8:9], min_val=0, max_val=NOVER)
                vec.wait_ge(y_ready, NE * (l + 1))
                for j in range(NOVER):
                    with vec.If(n_over > j):
                        vec.wait_ge(o["t"], j + 1)
                        vec.scalar_tensor_tensor(zg[0], zg[0], 1.0, ps[:, 2, :], ALU.add, ALU.mult).then_inc(o["z"], 1)
                        vec.wait_ge(o["z"], j + 1)
                        vec.wait_ge(o["g"], 2 * j + 2)
                        vec.scalar_tensor_tensor(hb[0], zg[0].rearrange("p (c t) -> p c t", t=P), 0.5,
                                                 ps[:, 3, :].rearrange("p (c t) -> p c t", t=P), ALU.mult, ALU.mult)\
                           .then_inc(o["h"], 1)
                    with vec.Else():
                        vec.nop()

            def alpha(l):
                vec.wait_ge(h_out, 16 * (5 if l == 0 else 9))
                for t in range(5 if l == 0 else 4):
                    r = rows_of(t)
                    vec.tensor_scalar(X[0:r, t, :], X[0:r, t, :], ALPHA, None, ALU.mult).then_inc(alpha_done, 1)

            def combine(l, t):
                n = COMBINED[(3 + 2 * l, t)]
                r = rows_of(t)
                x, y = X[0:r, t, :], yin[t][0:r]
                vec.wait_ge(alpha_done, 5 if l == 0 else 9)
                vec.wait_ge(yin_in[t], 16 * (l + 1))
                step(vec.scalar_tensor_tensor(x, y[:, 0, :], gates[0:r, 0, t:t + 1], x, ALU.mult, ALU.add))
                vec.scalar_tensor_tensor(x, y[:, 1, :], gates[0:r, 1, t:t + 1], x, ALU.mult, ALU.add).then_inc(comb_done, 1)
                vec.wait_ge(comb_done, n + 1)
                normalise(3 + 2 * l, t)

            route(0)
            experts(0)
            finish_and_turn(4, (4, 0, 1, 2, 3), lambda t: combine(0, t))

            for c in range(DC):
                z = zpad[c % 2]
                taken(vec, f"cg_{c}")
                done(vec, f"cv_{c}")
                free(vec.tensor_tensor(halves(z), halves(cgs[c % 2]), job_pair(f"cv_{c}", 257), ALU.mult), f"cv_{c}")
                taken(vec, f"cv_{c}")
                y = zT[:, c, :]
                tap = lambda k: cols[:, SC0 + 8 * k + c:SC0 + 8 * k + c + 1]
                step(vec.tensor_scalar(y, z[:, 0:S], tap(0), None, ALU.mult))
                for k in (1, 2):
                    step(vec.scalar_tensor_tensor(y, z[:, k:S + k], tap(k), y, ALU.mult, ALU.add))
                done(vec, f"bg_{c}")
                free(vec.tensor_tensor(y, y, job_bank(f"bg_{c}"), ALU.mult), f"bg_{c}")
            finish_and_turn(5, range(NT), lambda t: residual(4, t, f"outD_{t}"))
            route(1)
            experts(1)
            for t in range(NT):
                combine(1, t)
            affine_last(5, 3)

        @block.gpsimd
        def _(pool):
            own = [0]

            def mark(ins):
                own[0] += 1
                ins.then_inc(pool_own, 1)

            def settle():
                pool.wait_ge(pool_own, own[0])

            mark(pool.memset(ident[:], 0.0))
            mark(pool.memset(before[:], 1.0))
            mark(pool.memset(ones[:], 1.0))
            settle()
            pool.affine_select(out=ident[:], in_=ident[:], compare_op=ALU.not_equal, fill=1.0, base=0,
                               pattern=[[-1, P]], channel_multiplier=1).then_inc(pool_set, 1)
            pool.memset(ones_h[:], 1.0).then_inc(pool_set, 1)
            pool.affine_select(out=before[:], in_=before[:], compare_op=ALU.is_gt, fill=0.0, base=0,
                               pattern=[[1, P]], channel_multiplier=-1).then_inc(pool_set, 1)
            pool.wait_ge(pool_set, 3)
            pool.memset(relb[NB:NB + 1, :], NEG).then_inc(prow_set, 1)
            pool.wait_ge(prow_set, 1)
            mark(pool.memset(slot_ids, EMPTY))
            mark(pool.iota(expert_of[:], pattern=[[1, NE]], base=0, channel_multiplier=0, allow_small_or_imprecise_dtypes=True))
            mark(pool.iota(group_of[:], pattern=[[1, NG], [0, EPG]], base=0, channel_multiplier=0, allow_small_or_imprecise_dtypes=True))
            mark(pool.iota(assign_id[:], pattern=[[2 * P, 5], [1, 2]], base=0, channel_multiplier=2))
            settle()
            for l in range(2):
                pool.dma_start(tab_d[l].rearrange("(p b) o -> p (b o)", b=NBLK), slot_ids).then_inc(table_in, 16)

            taken(pool, "toep1")
            taken(pool, "toep2")
            pool.dma_start(bvec, brow[0:HPG, :, :]).then_inc(bvec_out, 16)
            pool.wait_ge(bvec_out, 16)
            pool.dma_start(bias0, bass.AP(bvec.tensor, 0, [[1, P], [1536, HPG], [1, 384]])).then_inc(toep_in, 16)
            for g in (1, 2):
                pool.dma_start(bias12[g - 1], bass.AP(bvec.tensor, 512 * g + P, [[1, P], [1536, HPG], [1, P]])).then_inc(toep_in, 16)

            LNP = [(a["ln_g"][0], a["ln_b"][0]), (a["ln_g"][1], a["ln_b"][1])] + [
                (a["ln_g_2"][l, i], a["ln_b_2"][l, i]) for l in range(2) for i in range(2)]

            def load_lnp(l):
                for i in range(2):
                    v = LNP[l][i]
                    pool.dma_start(lnp[:, i, :], bass.AP(v.tensor, v.offset, [[0, P], [1, D]])).then_inc(lnp_in, 16)

            def affine(l, t):
                n = LN[(l, t)]
                if t == NT - 1:
                    pool.wait_ge(ln_done, n + 1)
                    return
                r = rows_of(t)
                x = X[0:r, t, :]
                pool.wait_ge(normed, n + 1)
                mark(pool.tensor_tensor(x, x, lnp[0:r, 0, :], ALU.mult))
                settle()
                pool.tensor_tensor(x, x, lnp[0:r, 1, :], ALU.add).then_inc(ln_done, 1)
                pool.wait_ge(ln_done, n + 1)

            done(pool, "fac_8")
            load_lnp(0)
            pool.wait_ge(pv_done, NUA)
            pool.dma_start(X[:, 0:NT, :], a["x"][0].rearrange("(t p) d -> p t d", p=P)).then_inc(x_back, 16)
            pool.wait_ge(factors_ready, 1)
            pool.wait_ge(lnp_in, 32)
            for t in range(NT):
                affine(0, t)
                pool.dma_start(x1_d[P * t:P * (t + 1), :], X[:, t, :]).then_inc(x1_out, 16)
            pool.dma_start(rot, a["rotary"]).then_inc(rot_in, 16)
            load_lnp(1)
            pool.wait_ge(pv_done, NUA + NUB)
            pool.wait_ge(x1_out, 64)
            pool.dma_start(X[:, 0:NT, :], x1_d.rearrange("(t p) d -> p t d", p=P)).then_inc(x1_back, 16)
            pool.dma_start(meta_x[0:META, :], a["meta_tokens_2"]).then_inc(meta_in, 16)

            def load_bd(c):
                if c >= 2:
                    done(pool, f"ri_{c - 2}")
                for i, w in enumerate((a["lru_w_a_2"], a["lru_w_i_2"])):
                    for h in range(2):
                        s = slice(64 * h, 64 * h + 64)
                        pool.dma_start(wa_bd[s, c % 2, i, s], w[0, 2 * c + h]).then_inc(bd_in[c % 2], 16)

            mark(pool.memset(wa_bd, 0.0))
            settle()
            load_bd(0)
            load_bd(1)
            pool.wait_ge(lnp_in, 64)
            for t in range(NT):
                affine(1, t)
            load_lnp(2)
            for c in range(2, DC):
                load_bd(c)
            pool.wait_ge(yT_ready, DC)
            for l in range(2):
                pool.dma_start(rw[:, l, :, 0:NG], a["moe_w_group_2"][l].rearrange("(c p) n -> p c n", p=P)).then_inc(rw_in, 16)
                pool.dma_start(rw[:, l, :, NG:36], a["moe_w_expert_2"][l].rearrange("(c p) n -> p c n", p=P)).then_inc(rw_in, 16)
                vg, ve = a["moe_b_group_2"][l], a["moe_b_expert_2"][l]
                pool.dma_start(rb[:, l, 0:NG], bass.AP(vg.tensor, vg.offset, [[0, P], [1, NG]])).then_inc(rw_in, 16)
                pool.dma_start(rb[:, l, NG:36], bass.AP(ve.tensor, ve.offset, [[0, P], [1, NE]])).then_inc(rw_in, 16)

            def rows_out(l, t):
                r0 = P * t
                pool.dma_start(h_d[l][r0:r0 + rows_of(t), :], X[0:rows_of(t), t, :]).then_inc(h_out, 16)

            def by_load(e, rows):
                load = pool.value_load(load_i[0:1, e:e + 1], min_val=0, max_val=TM)
                with pool.If(load > CAP // 2):
                    rows(CAP)
                with pool.Else():
                    rows(CAP // 2)

            def gather(l, e):
                E = NE * l + e
                if E >= 2:
                    pool.wait_ge(xe_used, E - 1)
                def rows(n):
                    pool.indirect_dma_start(out=xe[e % 2][0:n], out_offset=None, in_=h_d[l],
                                            in_offset=bass.IndirectOffsetOnAxis(ap=slot_tok[0:n, e:e + 1], axis=0),
                                            bounds_check=(TM if l == 0 else S) - 1, oob_is_err=False).then_inc(xe_landed[e % 2], 16)
                by_load(e, rows)

            def scatter(l, e):
                pool.wait_ge(yo_ready, NE * l + e + 1)
                def rows(n):
                    pool.indirect_dma_start(out=ya_d[l], out_offset=bass.IndirectOffsetOnAxis(ap=slot_ids[0:n, e:e + 1], axis=0),
                                            in_=yo[e % 2][0:n], in_offset=None, bounds_check=2 * (TM if l == 0 else S) - 1,
                                            oob_is_err=False).then_inc(yo_sent[e % 2], 16)
                by_load(e, rows)

            def experts(l):
                tiles = range(5 if l == 0 else 4)
                pool.wait_ge(table_in, 32)
                pool.wait_ge(slots_ready, l + 1)
                for t in tiles:
                    for k in range(2):
                        r, i = rows_of(t), 2 * t + k
                        pool.indirect_dma_start(out=tab_d[l], out_offset=bass.IndirectOffsetOnAxis(ap=slots_i[0:r, i:i + 1], axis=0),
                                                in_=assign_id[0:r, i:i + 1], in_offset=None).then_inc(ids_out, 16)
                pool.wait_ge(ids_out, 16 * (10 if l == 0 else 18))
                pool.dma_start(slot_ids[:], tab_d[l].rearrange("(p b) o -> p (b o)", b=NBLK)).then_inc(ids_in, 16)
                pool.wait_ge(tok_ready, l + 1)
                pool.wait_ge(h_out, 16 * (5 if l == 0 else 9))
                pool.wait_ge(route_ready, l + 1)
                gather(l, 0)
                for e in range(NE):
                    if e + 1 < NE:
                        gather(l, e + 1)
                    scatter(l, e)
                for par in range(2):
                    pool.wait_ge(yo_sent[par], 8 * NE * (l + 1))
                o = ov[l]
                pool.wait_ge(route_ready, l + 1)
                n_over = pool.value_load(over_i[0:1, 8:9], min_val=0, max_val=NOVER)
                for j in range(NOVER):
                    with pool.If(n_over > j):
                        b = NE + j
                        pool.indirect_dma_start(out=xe[0], out_offset=None, in_=h_d[l],
                                                in_offset=bass.IndirectOffsetOnAxis(ap=slot_tok[:, b:b + 1], axis=0),
                                                bounds_check=(TM if l == 0 else S) - 1, oob_is_err=False).then_inc(o["x"], 16)
                        pool.wait_ge(o["yo"], j + 1)
                        pool.indirect_dma_start(out=ya_d[l], out_offset=bass.IndirectOffsetOnAxis(ap=slot_ids[:, b:b + 1], axis=0),
                                                in_=yo[0], in_offset=None, bounds_check=2 * (TM if l == 0 else S) - 1,
                                                oob_is_err=False).then_inc(o["out"], 16)
                        pool.wait_ge(o["out"], 16 * (j + 1))
                    with pool.Else():
                        pool.nop()

            def combined(l, order):
                for t in order:
                    r = rows_of(t)
                    pool.dma_start(yin[t][0:r], ya_d[l][2 * P * t:2 * P * t + 2 * r, :].rearrange("(p k) d -> p k d", k=2))\
                        .then_inc(yin_in[t], 16)
                pool.wait_ge(lnp_in, 32 * (4 + 2 * l))
                for t in order:
                    affine(3 + 2 * l, t)
                    if l == 1:
                        pool.dma_start(out[0, P * t:P * (t + 1), :], X[:, t, :]).then_inc(out_sent, 16)

            pool.wait_ge(lnp_in, 96)
            for t in (4, 0, 1, 2, 3):
                affine(2, t)
                rows_out(0, t)
            load_lnp(3)
            experts(0)
            combined(0, (4, 0, 1, 2, 3))
            load_lnp(4)
            pool.wait_ge(lnp_in, 32 * 5)
            for t in range(NT):
                affine(4, t)
                rows_out(1, t)
            load_lnp(5)
            experts(1)
            combined(1, (0, 1, 2, 3))
            pool.wait_ge(out_sent, 64)


_INS = ["x", "c", "rel_bias", "ada_w", "ada_b", "ln_g", "ln_b", "a_w_in", "a_w_out", "b_w_in", "b_q_norm", "b_w_uq",
        "b_kv_norm", "b_w_ukv", "b_w_out", "meta_tokens_2", "lru_w_in_2", "lru_conv_w_2", "lru_conv_b_2", "lru_w_a_2",
        "lru_b_a_2", "lru_w_i_2", "lru_b_i_2", "lru_lambda_2", "lru_w_out_2", "sc_w_in_2", "sc_conv_w_2", "sc_w_out_2",
        "moe_w_group_2", "moe_b_group_2", "moe_w_expert_2", "moe_b_expert_2", "moe_w_gate_2", "moe_w_up_2",
        "moe_w_down_2", "ln_g_2", "ln_b_2"]


def kernel(**inputs):
    import numpy as _np
    import concourse.bacc as _bacc
    from concourse import mybir as _mybir
    from concourse.bass_utils import run_bass_kernel_spmd as _run

    nc = _bacc.Bacc("TRN2", target_bir_lowering=False, num_devices=1)
    arrays, aps = {}, {}
    given = {n: inputs[n] for n in _INS}
    given.update(constants())
    for name, value in given.items():
        v = _np.ascontiguousarray(value)
        arrays[f"in_{name}_dram"] = v
        aps[name] = nc.dram_tensor(f"in_{name}_dram", v.shape, _mybir.dt.from_np(v.dtype), kind="ExternalInput").ap()
    out = nc.dram_tensor("out_0_dram", (1, S, D), F32, kind="ExternalOutput").ap()
    build(nc, aps, out)
    r = _run(nc, [arrays], core_ids=[0])
    return r.results[0]["out_0_dram"]
```

```python
from contextlib import ExitStack

import numpy as np

import concourse.bass as bass
from concourse import mybir

F32 = mybir.dt.float32
BF16 = mybir.dt.bfloat16
I32 = mybir.dt.int32
U32 = mybir.dt.uint32
ALU = mybir.AluOpType
ACT = mybir.ActivationFunctionType
AX = mybir.AxisListType

P = 128
D = 1024
DC = D // P
S = 512
NT = S // P
META = 16
TM = META + S
GROUPS = 3
HPG = 6
HD = 64
WA = GROUPS * HPG * HD
GW = HPG * HD
GC = GW // P
NB = 32
DILS = (1, 4, 16)
RADIUS = 64
NEG = -1e30
HB = 16
QL, KVL, ROPE = 256, 128, 32
NOPE = 64
QW = NOPE + ROPE
SCALE_B = float(QW) ** -0.5
NE = 32
NG = 4
EPG = NE // NG
FE = 512
FC = FE // P
CAP = 128
NOVER = 8
NBLK = NE + NOVER
EMPTY = 1 << 20
ALPHA = 4.0 ** 0.25
LN_EPS = 1e-5
RMS_EPS = 1e-6

SLABS = 6
SLAB = 4096


def bucket(rel):
    half, exact = NB // 2, NB // 4
    n = np.abs(rel)
    large = exact + (np.log(np.maximum(n, 1).astype(np.float32) / np.float32(exact)) / np.float32(np.log(1024 / exact))
                     * (half - exact)).astype(np.int32)
    return np.where(rel > 0, half, 0) + np.where(n < exact, n, np.minimum(large, half - 1))


def constants():
    d = 255 - np.arange(2 * 256)
    sel = np.zeros((NB + 1, GROUPS, 512), np.float32)
    for g, dil in enumerate(DILS):
        step = dil // 4 if g == 2 else 1
        ok = (np.abs(d) <= RADIUS * step) & (d % step == 0)
        if g == 2:
            ok &= np.abs(d // step) <= 31
        rel = d // step * dil
        for i in range(512):
            sel[bucket(rel[i]) if ok[i] else NB, g, i] = 1.0
    heads = np.zeros((HPG, GC, P), np.float32)
    for c in range(GC):
        for f in range(P):
            heads[2 * c + f // HD, c, f] = 1.0
    inv = np.float32(10000.0) ** (-np.arange(0, ROPE, 2, dtype=np.float32) / np.float32(ROPE))
    ang = np.arange(S, dtype=np.float32)[:, None] * inv[None, :]
    cos, sin = np.cos(ang).T, np.sin(ang).T
    rot = np.stack([np.concatenate([cos, cos]), np.concatenate([-sin, sin])], axis=1).astype(np.float32)
    return {"bucket_sel": sel, "head_sel": heads, "rotary": np.tile(rot, (4, 1, 1))}


LATE_MODS = [(0, 4), (0, 5)] + [(1, s) for s in range(6)]
MOD_AT = (3, 7, 11, 15, 27, 28, 29, 31)


def plan_slabs():
    out = [("ada", 0, s) for s in range(4)]
    for g in range(GROUPS):
        out += [("win_a", 0, (t, g)) for t in range(3)]
        if g == 1:
            out += [("ada", l, s) for l, s in LATE_MODS[:4]]
        if g == 2:
            out += [("ada", l, s) for l, s in LATE_MODS[4:]]
    out += [("win_a", 0, (3, g)) for g in range(GROUPS)]
    out += [("wout_a", 0, s) for s in range(3)]
    out += [("win_b", 0, s) for s in range(3)] + [("ukv", 0, 0), ("uq", 0, 0)]
    out += [("wout_b", 0, s) for s in range(2)]
    out += [("lru_in", 0, s) for s in (0, 2, 1, 3)] + [("lru_out", 0, s) for s in range(2)]
    out += [("expert", 0, (e, w)) for e in range(NE) for w in range(3)]
    out += [("sc_in", 0, (t, h)) for h in range(2) for t in (1, 2, 0)] + [("sc_out", 0, s) for s in range(2)]
    out += [("expert", 1, (e, w)) for e in range(NE) for w in range(3)]
    return out


STREAM = plan_slabs()
TURN = {k: n for n, k in enumerate(STREAM)}

PROWS = {}
_at = 0
for _n, _k in (("c", 8), ("ada_b", 48), ("qn", 2), ("kvn", 1), ("conv_w", 32), ("conv_b", 8), ("b_a", 8),
               ("b_i", 8), ("lam", 8)):
    PROWS[_n] = _at
    _at += _k
NROWS = _at
SC0 = P


def with_router(out, l, order):
    j = []
    for i, t in enumerate(order):
        j += [f"{out}_{t}"] + ([f"router{l}_{order[i - 2]}"] if i > 1 else [])
    return j + [f"router{l}_{t}" for t in order[-2:]] + [f"ranks{l}", f"table{l}"]


def plan_jobs():
    j = ["params", "taps", "mod0_0"] + [f"toep{g}" for g in range(3)] + [f"mod0_{s}" for s in range(1, 4)]
    j += [f"qkv0_{i}" for i in range(10)]
    for u in range(36):
        j += FILL_A.get(u, [])
    j += ["negmax2", "den2", "sgA_7", "sgA_8"]
    j += [f"fac_{c}" for c in range(9)]
    j += [f"outA_{t}" for t in range(NT)]
    j += [f"lat_{c}" for c in range(4)] + ["rms0", "rms1"] + ["gateb1", "sgB_0", "sgB_1"] + [f"vB_{t}" for t in range(NT)]
    for h in range(3):
        j += [f"qn_{h}", f"kn_{h}"]
    j += [f"sgB_{c}" for c in range(2, DC)]
    for h in range(3, HB):
        j += [f"qn_{h}", f"kn_{h}"]
    j += [f"outB_{t}" for t in range(NT)]
    for c in range(DC):
        j += [f"uy_{c}", f"ux_{c}"] + ([f"ra_{c - 1}", f"ri_{c - 1}"] if c else [])
    j += ["ra_7", "ri_7"]
    j += with_router("outC", 0, (4, 0, 1, 2, 3))
    for c in range(DC):
        j += [f"cg_{c}", f"cv_{c}", f"bg_{c}"]
    j += with_router("outD", 1, (0, 1, 2, 3))
    return j


FILL_A = {}
for _i in range(10):
    FILL_A.setdefault(2 + 2 * _i, []).append(f"qkv1_{_i}")
    FILL_A.setdefault(26 + _i * 4 // 10, []).append(f"qkv2_{_i}")
for _i, (_l, _s) in enumerate(LATE_MODS):
    FILL_A.setdefault(MOD_AT[_i], []).append(f"mod{_l}_{_s}")
FILL_A[25] = ["gateb0"]
for _i in range(7):
    FILL_A.setdefault(32 + _i * 4 // 7, []).append(f"sgA_{_i}")

for _g in range(2):
    FILL_A[33 + _g] += [f"negmax{_g}", f"den{_g}"]

JOBS = plan_jobs()
JOB = {n: i for i, n in enumerate(JOBS)}
assert len(JOB) == len(JOBS)

UNITS_A = [(0, h, n) for h in range(HPG) for n in range(NT)] + [(g, h, None) for g in (1, 2) for h in range(HPG)]
NUA = len(UNITS_A)
NUB = HB * NT


def build(nc, a, out):
    with ExitStack() as ctx:
        def sb(name, shape, dt=F32):
            return ctx.enter_context(nc.sbuf_tensor(name, shape, dt))

        def sem(name):
            return ctx.enter_context(nc.semaphore(name))

        ring = sb("ring", [P, SLABS * SLAB])
        arena = sb("arena", [P, 24576])
        lnp = sb("lnp", [P, 2, D])
        gate_b = sb("gate_b", [P, D])
        ident = sb("ident", [P, P])
        ones = sb("ones", [P, P])
        before = sb("before", [P, P], BF16)
        ones_h = sb("ones_h", [P, P], BF16)
        cols = sb("cols", [P, SC0 + 24])
        csilu = sb("csilu", [P, 2, DC])
        mod = sb("mod", [P, 2, 24])
        lamc = sb("lamc", [P, 4, DC])
        half_b = sb("half_b", [P, 2, DC])
        spec = sb("spec", [P, 64])
        expert_of = arena[:, 24528:24560]
        group_of = sb("group_of", [P, NE])
        negm = sb("negm", [P, GROUPS, NT, HPG])
        den = sb("den", [P, GROUPS, NT, HPG])
        nmax = sb("nmax", [P, 8])
        dsum = sb("dsum", [P, 8])
        slot_ids = arena[:, 24448:24488].bitcast(I32)
        slot_tok = arena[:, 24488:24528].bitcast(I32)
        load_i = mod[0:1].rearrange("p l n -> p (l n)")[:, 0:NE].bitcast(I32)
        over_i = sb("over_i", [1, 16], I32)
        gates = sb("gates", [P, 2, 5])

        ps = ctx.enter_context(nc.psum_tensor("ps", [P, 8, 512], F32))

        def at(o, n):
            return arena[:, o:o + n]

        X = at(0, 5 * D).rearrange("p (t d) -> p t d", d=D)
        HT = at(5120, DC * TM).rearrange("p (c t) -> p c t", t=TM)
        R0 = 9344
        qkv_at = [0, R0 + 4608]
        oT_a = at(R0, 9 * S).rearrange("p (c t) -> p c t", t=S)
        bias0 = at(R0 + 9216, HPG * 384).rearrange("p (h j) -> p h j", j=384)
        bias12 = [at(R0 + 11520 + 768 * g, HPG * P).rearrange("p (h j) -> p h j", j=P) for g in range(2)]
        scores_sb = [at(R0 + 13056 + 512 * i, 512) for i in range(3)]
        pt_a = [at(4608, 512), at(R0 + 14592, 512)]
        x_first = at(qkv_at[1], NT * D).rearrange("p (t d) -> p t d", d=D)
        q_g = [at(qkv_at[g % 2], GC * S).rearrange("p (c t) -> p c t", t=S) for g in range(GROUPS)]
        k_g = [at(qkv_at[g % 2] + 1536, GC * S).rearrange("p (c t) -> p c t", t=S) for g in range(GROUPS)]
        v_g = [at(qkv_at[g % 2] + 3072, NT * GW).rearrange("p (t f) -> p t f", f=GW) for g in range(GROUPS)]
        sg_a = at(qkv_at[1], 9 * S).rearrange("p (c t) -> p c t", t=S)
        rows_m = at(R0 + 9216, 3 * S).rearrange("p (g t) -> p g t", t=S)
        rows_d = at(R0 + 10752, 3 * S).rearrange("p (g t) -> p g t", t=S)
        rows_t = at(R0 + 12288, S)
        rows_s = at(R0 + 12800, S)
        vB = at(0, NT * D).rearrange("p (t f) -> p t f", f=D)
        sgB = at(R0, DC * S).rearrange("p (c t) -> p c t", t=S)
        qB = [at(R0 + 4096 + 512 * i, S) for i in range(4)]
        kB = [at(R0 + 8192 + 512 * i, S) for i in range(4)]
        q_swap = at(R0 + 10240, S)
        krB = at(R0 + 6144, S)
        latB = at(R0 + 6656, 3 * S).rearrange("p (c t) -> p c t", t=S)
        rot = at(R0 + 11264, 2 * S).rearrange("p (c t) -> p c t", t=S)
        tmp_b = [at(R0 + 12288, S), at(R0 + 12800, S)]
        pt_b = [at(4096, 512), at(R0 + 14592, 512)]
        oT_b = HT[:, :, META:TM]
        yT = at(R0, DC * TM).rearrange("p (c t) -> p c t", t=TM)
        sT = at(R0 + 4224, 2 * TM).rearrange("p (c t) -> p c t", t=TM)
        gx = at(R0 + 5280, 2 * TM).rearrange("p (c t) -> p c t", t=TM)
        root = at(R0 + 6336, 2 * TM).rearrange("p (c t) -> p c t", t=TM)
        wa_bd = at(R0 + 7392, 4 * P).rearrange("p (t i f) -> p t i f", t=2, i=2)
        upad = at(R0 + 12672, TM + 3)
        tA = at(R0 + 13204, TM)
        tB = at(R0 + 13732, TM)
        xcs = [at(R0 + 8192 + TM * i, TM) for i in range(2)]
        NC_ = S + 2
        zT = at(R0, DC * S).rearrange("p (c t) -> p c t", t=S)
        zpad = [at(R0 + 4224 + 528 * i, NC_) for i in range(2)]
        cgs = [at(R0 + 5280 + 528 * i, NC_) for i in range(2)]
        xe = [at(R0 + D * i, D) for i in range(2)]
        xeT = [at(R0 + 2048 + D * i, D).rearrange("p (c t) -> p c t", t=P) for i in range(2)]
        zg = [at(R0 + 4096 + 512 * i, 512) for i in range(2)]
        hb = [at(R0 + 5120 + 512 * i, 512).rearrange("p (c t) -> p c t", t=P) for i in range(2)]
        yo = [at(R0 + 6144 + D * i, D) for i in range(2)]
        yin = [at(R0 + 2 * D * i, 2 * D).rearrange("p (k d) -> p k d", k=2) for i in range(5)]
        rw = at(R0 + 12288, 2 * DC * 36).rearrange("p (l c n) -> p l c n", l=2, c=DC)
        rb = at(R0 + 12864, 72).rearrange("p (l n) -> p l n", l=2)
        lg = at(R0 + 12936, 5 * 40).rearrange("p (t n) -> p t n", n=40)
        RT = R0 + 13136
        elm = at(RT, 5 * NE).rearrange("p (t n) -> p t n", n=NE)
        oh1 = at(RT + 160, 5 * NE).rearrange("p (t n) -> p t n", n=NE)
        oh2 = at(RT + 320, 5 * NE).rearrange("p (t n) -> p t n", n=NE)
        adr = at(RT + 480, 5 * NE).rearrange("p (t n) -> p t n", n=NE)
        tq = at(RT + 640, 5 * NE).rearrange("p (t n) -> p t n", n=NE)
        ohb = at(RT + 800, 80).bitcast(BF16).rearrange("p (t n) -> p t n", n=NE)
        g8 = at(RT + 880, 40).rearrange("p (t n) -> p t n", n=8)
        e8 = at(RT + 920, 40).rearrange("p (t n) -> p t n", n=8)
        gi8 = at(RT + 960, 40).bitcast(U32).rearrange("p (t n) -> p t n", n=8)
        ei8 = at(RT + 1000, 40).bitcast(U32).rearrange("p (t n) -> p t n", n=8)
        sm = at(RT + 1040, 80).rearrange("p (n t) -> p n t", t=5)
        cnt = at(RT + 1120, 4 * NE).rearrange("p (n e) -> p n e", e=NE)
        row_of = at(R0 + 8192, 10).rearrange("p (t k) -> p t k", k=2)
        block_of = at(R0 + 8208, 10).rearrange("p (t k) -> p t k", k=2)
        picked = at(R0 + 8224, 2 * 5 * NE).rearrange("p (k t n) -> p k t n", k=2, n=NE)
        blk = at(R0 + 8544, 5 * NE).rearrange("p (t n) -> p t n", n=NE)
        emptied = at(R0 + 8704, NBLK)
        row_hot = at(R0 + 8960, 10 * CAP).rearrange("p (i r) -> p i r", r=CAP)
        block_hot = at(R0 + 10240, 10 * NBLK).rearrange("p (i b) -> p i b", b=NBLK)
        column_no = at(R0 + 10656, CAP)
        assign_no = at(R0 + 10784, 10)
        ovf = at(RT + 1258, 16)
        prow = at(R0, P)
        prow2 = at(R0 + 128, P)
        brow = at(R0 + 256, 1536).rearrange("p (g i) -> p g i", g=3)
        bsel = at(R0 + 1792, 1536).rearrange("p (g i) -> p g i", g=3)
        relb = at(R0 + 3328, 18)
        hsel = lnp[0:HPG, 0, 0:GC * P].rearrange("p (c f) -> p c f", f=P)
        meta_x = X[:, 4, :]

        def dram(name, shape, dt=F32):
            return nc.dram_tensor(name, shape, dt, kind="Internal").ap()

        bvec = dram("bias_vectors", [HPG, 3, 512])
        x1_d = dram("x1_rows", [S, D])
        h_d = [dram(f"h_rows{l}", [(TM, S)[l], D]) for l in range(2)]
        ya_d = [dram(f"assignment_rows{l}", [2 * (TM, S)[l], D]) for l in range(2)]

        slab_landed = [sem(f"slab_landed{i}") for i in range(SLABS)]
        proj_done = sem("proj_done")
        proj_free = [sem(f"proj_free{i}") for i in range(2)]
        prow_set, prow_in = sem("prow_set"), sem("prow_in")
        consts_in, numbers_set, hot_ready = sem("consts_in"), sem("numbers_set"), sem("hot_ready")
        rot_in = sem("rot_in")
        x_in, meta_in, x_back, x1_out, x1_back = (sem(n) for n in ("x_in", "meta_in", "x_back", "x1_out", "x1_back"))
        pool_own, pool_set = sem("pool_own"), sem("pool_set")
        vec_own, act_own = sem("vec_own"), sem("act_own")
        csilu_ready, mod_sum = sem("csilu_ready"), sem("mod_sum")
        diag_ready = sem("diag_ready")
        turned = sem("turned")
        turn_copied = [sem(f"turn_copied{h}") for h in range(2)]
        bvec_out, toep_in = sem("bvec_out"), sem("toep_in")
        scores_ready, scores_read = sem("scores_ready"), sem("scores_read")
        max_ready, probs_ready = sem("max_ready"), sem("probs_ready")
        pt_ready, pt_copied, pv_done, o_copied = (sem(n) for n in ("pt_ready", "pt_copied", "pv_done", "o_copied"))
        factors_ready, yT_ready, silu_ready = sem("factors_ready"), sem("yT_ready"), sem("silu_ready")
        var_ready, sd_ready, normed, ln_done = (sem(n) for n in ("var_ready", "sd_ready", "normed", "ln_done"))
        lnp_in = sem("lnp_in")
        lat_sq, lat_ready, rms_sd = (sem(n) for n in ("lat_sq", "lat_ready", "rms_sd"))
        q_swapped, qr_ready, kr_ready = (sem(n) for n in ("q_swapped", "qr_ready", "kr_ready"))
        bd_in = [sem(f"bd_in{i}") for i in range(2)]
        xc_ready, gelu_sq, gelu_in, gelu_th = (sem(n) for n in ("xc_ready", "gelu_sq", "gelu_in", "gelu_th"))
        route_ready = sem("route_ready")
        fac_in, fac_exp = sem("fac_in"), sem("fac_exp")
        s_ready, root_ready = sem("s_ready"), sem("root_ready")
        lam_a, lam_b = sem("lam_a"), sem("lam_b")
        rw_in, h_out = sem("rw_in"), sem("h_out")
        pg_in, pg_exp, onehot_ready, tok_ready = (sem(n) for n in ("pg_in", "pg_exp", "onehot_ready", "tok_ready"))
        xe_landed = [sem(f"xe_landed{i}") for i in range(2)]
        xe_used, xet_copied = sem("xe_used"), sem("xet_copied")
        gate_ready, up_ready, tanh_ready, hb_ready, y_ready, yo_ready = (
            sem(n) for n in ("gate_ready", "up_ready", "tanh_ready", "hb_ready", "y_ready", "yo_ready"))
        zg_ready = sem("zg_ready")
        yo_sent = [sem(f"yo_sent{i}") for i in range(2)]
        yin_in = [sem(f"yin_in{t}") for t in range(5)]
        alpha_done, scale_ready = sem("alpha_done"), sem("scale_ready")
        comb_done = sem("comb_done")
        ov = [{n: sem(f"over_{n}{l}") for n in ("w", "x", "xu", "xt", "xc", "g", "t", "z", "h", "y", "yo", "out")}
              for l in range(2)]
        out_sent = sem("out_sent")

        def slab(turn):
            o = (turn % SLABS) * SLAB
            return ring[:, o:o + SLAB]

        def bank(name):
            return 2 * (JOB[name] % 2)

        def tokens(tile):
            return slice(0, META) if tile == 4 else slice(META + P * tile, META + P * (tile + 1))

        def rows_of(tile):
            return META if tile == 4 else P

        LN_TILES = [(l, t) for l, ts in ((0, range(4)), (1, range(4)), (2, (4, 0, 1, 2, 3)), (3, (4, 0, 1, 2, 3)),
                                         (4, range(4)), (5, range(4))) for t in ts]
        LN = {k: i for i, k in enumerate(LN_TILES)}
        COMBINED = {k: i for i, k in enumerate(k for k in LN_TILES if k[0] in (3, 5))}
        TURNED = {k: i for i, k in enumerate((k, t) for k in range(6) for t in (((4,) if 2 <= k <= 4 else ()) + (0, 1, 2, 3)))}

        def taken(eng, name):
            eng.wait_ge(proj_free[JOB[name] % 2], JOB[name] // 2 + 1)

        def ht_wait(eng, k):
            for h in range(2):
                eng.wait_ge(turn_copied[h], TURNED[(k, 3)] + 1)

        def turn_bank(n, h):
            return ps[:, 4 + 2 * (n % 2) + h, :]

        def done(eng, name):
            eng.wait_ge(proj_done, JOB[name] + 1)

        def backwards(ap):
            dims = [list(x) for x in ap.ap]
            step, n = dims[-1]
            return bass.AP(ap.tensor, ap.offset + step * (n - 1), dims[:-1] + [[-step, n]])

        def spread(ap, at_dim, n):
            dims = [list(x) for x in ap.ap]
            return bass.AP(ap.tensor, ap.offset, dims[:at_dim] + [[0, n]] + dims[at_dim:])

        PARAMS = (("c", a["c"].rearrange("a (r p) -> (a r) p", p=P)),
                  ("ada_b", a["ada_b"].rearrange("l (r p) -> (l r) p", p=P)),
                  ("qn", a["b_q_norm"].rearrange("l (r p) -> (l r) p", p=P)),
                  ("kvn", a["b_kv_norm"]),
                  ("conv_w", a["lru_conv_w_2"][0].rearrange("k (r p) -> (k r) p", p=P)),
                  ("conv_b", a["lru_conv_b_2"].rearrange("l (r p) -> (l r) p", p=P)),
                  ("b_a", a["lru_b_a_2"].rearrange("l (r p) -> (l r) p", p=P)),
                  ("b_i", a["lru_b_i_2"].rearrange("l (r p) -> (l r) p", p=P)),
                  ("lam", a["lru_lambda_2"].rearrange("l (r p) -> (l r) p", p=P)))

        def load_params(eng, which):
            for name, src in which:
                eng.dma_start(prow[PROWS[name]:PROWS[name] + src.shape[0], :], src).then_inc(prow_in, 16)

        block = ctx.enter_context(nc.Block())

        def consumed(turn):
            kind, l, s = STREAM[turn]
            if kind == "expert":
                e, w = s
                return (gate_ready, up_ready, y_ready)[w], NE * l + e + 1
            last = {
                "ada": lambda: f"mod{l}_{s}",
                "win_a": lambda: f"qkv{s[1]}_{(2, 5, 9)[s[0]]}" if s[0] < 3 else f"sgA_{3 * s[1] + 2}",
                "wout_a": lambda: "outA_3",
                "win_b": lambda: ("lat_3", "sgB_3", "sgB_7")[s],
                "ukv": lambda: "kn_15", "uq": lambda: "kn_15",
                "wout_b": lambda: "outB_3",
                "lru_in": lambda: f"{'ux' if s > 1 else 'uy'}_{3 + 4 * (s % 2)}",
                "lru_out": lambda: "outC_3",
                "sc_in": lambda: f"{('bg', 'cg', 'cv')[s[0]]}_{3 + 4 * s[1]}",
                "sc_out": lambda: "outD_3",
            }[kind]()
            return proj_done, JOB[last] + 1

        def source(kind, l, s):
            def cols_(w, c0, n):
                return w[:, c0:c0 + n].rearrange("(c p) n -> p c n", p=P)

            def rows_(w, r0, n):
                return w[r0:r0 + n, :].rearrange("(c p) n -> p c n", p=P)
            if kind == "ada":
                return cols_(a["ada_w"][l], 512 * s, 512)
            if kind == "win_a":
                return cols_(a["a_w_in"][0], WA * s[0] + GW * s[1], GW)
            if kind == "wout_a":
                return rows_(a["a_w_out"][0], 512 * s, min(512, WA - 512 * s))
            if kind == "win_b":
                lo = (0, 416, 928)[s]
                return cols_(a["b_w_in"][0], lo, (416, 512, 512)[s])
            if kind == "ukv":
                return rows_(a["b_w_ukv"][0], 0, KVL)
            if kind == "uq":
                return rows_(a["b_w_uq"][0], 0, QL)
            if kind == "wout_b":
                return rows_(a["b_w_out"][0], 512 * s, 512)
            if kind == "lru_in":
                return cols_(a["lru_w_in_2"][0], 512 * s, 512)
            if kind == "lru_out":
                return rows_(a["lru_w_out_2"][0], 512 * s, 512)
            if kind == "sc_in":
                return cols_(a["sc_w_in_2"][0], D * s[0] + 512 * s[1], 512)
            return rows_(a["sc_w_out_2"][0], 512 * s, 512)

        def expert_source(l, e, w):
            t = a[("moe_w_gate_2", "moe_w_up_2", "moe_w_down_2")[w]][l]
            t = t[bass.ds(e, 1)] if not isinstance(e, int) else t[e:e + 1]
            return t.rearrange("e (c p) n -> p (e c) n", p=P)

        def shaped(turn, c, n):
            return slab(turn)[:, 0:c * n].rearrange("p (c n) -> p c n", n=n)

        def expert_slab(turn, w):
            return shaped(turn, DC, FE) if w < 2 else shaped(turn, FC, D)

        def landed(eng, turn):
            eng.wait_ge(slab_landed[turn % SLABS], 16 * (turn // SLABS + 1))

        @block.sync
        def _(sp):
            def dense(turn):
                if turn >= SLABS:
                    sp.wait_ge(*consumed(turn - SLABS))
                src = source(*STREAM[turn])
                sp.dma_start(shaped(turn, src.shape[1], src.shape[2]), src).then_inc(slab_landed[turn % SLABS], 16)

            def experts(l):
                base = TURN[("expert", l, (0, 0))]
                for pair in (0, None):
                    if pair == 0:
                        for r in range(6):
                            sp.wait_ge(*consumed(base + r - SLABS))
                            sp.dma_start(expert_slab(base + r, r % 3), expert_source(l, r // 3, r % 3))\
                              .then_inc(slab_landed[(base + r) % SLABS], 16)
                    else:
                        with sp.Fori(1, NE // 2) as i:
                            for r in range(6):
                                used = (gate_ready, up_ready, y_ready)[r % 3]
                                sp.wait_ge(used, NE * l + i * 2 + (r // 3 - 1))
                                sp.dma_start(expert_slab(base + r, r % 3), expert_source(l, i * 2 + r // 3, r % 3))\
                                  .then_inc(slab_landed[(base + r) % SLABS], 16)
                o = ov[l]
                sp.wait_ge(y_ready, NE * (l + 1))
                sp.wait_ge(route_ready, l + 1)
                n_over = sp.value_load(over_i[0:1, 8:9], min_val=0, max_val=NOVER)
                for j in range(NOVER):
                    with sp.If(n_over > j):
                        if j:
                            sp.wait_ge(o["y"], j)
                        e = sp.value_load(over_i[0:1, j:j + 1], min_val=0, max_val=NE - 1)
                        for w in range(3):
                            sp.dma_start(expert_slab(base + w, w), expert_source(l, e, w)).then_inc(o["w"], 16)
                        sp.wait_ge(o["y"], j + 1)
                    with sp.Else():
                        sp.nop()

            load_params(sp, PARAMS[:5])
            e0, e1 = TURN[("expert", 0, (0, 0))], TURN[("expert", 1, (0, 0))]
            for turn in range(e0):
                dense(turn)
            experts(0)
            for t in range(5):
                sp.wait_ge(yin_in[t], 16)
            for turn in range(e0 + 3 * NE, e1):
                dense(turn)
            experts(1)

        @block.tensor
        def _(pe):
            count = [0]

            def begin(name, ahead=0):
                n = count[0] + ahead
                assert JOBS[n] == name, (JOBS[n], name)
                if n >= 2:
                    pe.wait_ge(proj_free[n % 2], n // 2)
                return ps[:, 2 * (n % 2), :], ps[:, 2 * (n % 2) + 1, :]

            def end(ins):
                ins.then_inc(proj_done, 1)
                count[0] += 1

            def product(dst, pairs):
                for i, (w, m) in enumerate(pairs):
                    ins = pe.matmul(dst, w, m, start=i == 0, stop=i == len(pairs) - 1)
                return ins

            def turn_tile(k, t):
                n = TURNED[(k, t)]
                r = rows_of(t)
                src = x_first if k == 0 else X
                for h in range(2):
                    if n >= 2:
                        pe.wait_ge(turn_copied[h], n - 1)
                    b = turn_bank(n, h)
                    for c in range(4):
                        f = P * (4 * h + c)
                        ins = pe.transpose(b[:, r * c:r * c + r], src[0:r, t, f:f + P], ident[0:r, 0:r])
                    ins.then_inc(turned, 1)

            def turn_normed(k, l, t):
                pe.wait_ge(ln_done, LN[(l, t)] + 1)
                turn_tile(k, t)

            def out_and_turn(k, l, order, out_tile, router=None, early=(), hold=False):
                for i, t in enumerate(order):
                    out_tile(t)
                    if i == 2 and hold:
                        turn_normed(k, l, order[0])
                    if i > hold:
                        turn_normed(k, l, order[i - 1])
                    if router and i > 1:
                        router(order[i - 2])
                if early:
                    start_early(early, k)
                turn_normed(k, l, order[-1])
                if router:
                    router(order[-2])
                    router(order[-1])

            def router(l):
                def tile(t):
                    n = TURNED[((3, 5)[l], t)]
                    for h in range(2):
                        pe.wait_ge(turn_copied[h], n + 1)
                    pe.wait_ge(rw_in, 16 * 8)
                    b0, _ = begin(f"router{l}_{t}")
                    end(product(b0[0:rows_of(t), 0:36], [(HT[:, k, tokens(t)], rw[:, l, k, :]) for k in range(DC)]))
                return tile

            started = {}
            SPLIT = META + 3 * P

            def chunk(banks, w, cols_, moving, m, lo, hi):
                for b, (s0, s1) in [(banks[0], moving)] if isinstance(moving[0], int) else zip(banks, moving):
                    c0, c1 = max(s0, lo), min(s1, hi)
                    if c0 < c1:
                        ins = product(b[0:m, c0 - s0:c1 - s0], [(w[:, k, cols_], HT[:, k, c0:c1]) for k in range(DC)])
                return ins

            def start_early(jobs, k):
                for h in range(2):
                    pe.wait_ge(turn_copied[h], TURNED[(k, 2)] + 1)
                for i, (name, turn, w, cols_, moving) in enumerate(jobs):
                    landed(pe, turn)
                    started[name] = begin(name, i)
                    chunk(started[name], w, cols_, moving, P, 0, SPLIT)

            def feature_major(name, w, cols_, moving, m=P):
                lo = SPLIT if name in started else 0
                banks = started.pop(name) if name in started else begin(name)
                end(chunk(banks, w, cols_, moving, m, lo, TM))

            WHOLE = (META, TM)
            BOTH = ((0, TM // 2), (TM // 2, TM))

            def out_products(banks, tile, y, parts, ks):
                r = rows_of(tile)
                for h, b in enumerate(banks):
                    for k in ks:
                        w, kk = parts[k]
                        ins = pe.matmul(b[0:r, :], y(k), w[:, kk, 512 * h:512 * h + 512], start=k == 0, stop=k == len(parts) - 1)
                return ins

            def start_out(name, ahead, tile, y, parts):
                started[name] = begin(name, ahead)
                out_products(started[name], tile, y, parts, range(len(parts) - 1))

            def token_major(name, tile, y, parts):
                ks = range(len(parts) - 1 if name in started else 0, len(parts))
                banks = started.pop(name) if name in started else begin(name)
                end(out_products(banks, tile, y, parts, ks))

            def modulation(l, s):
                acc = slab(TURN[("ada", l, s)])[:, 0:512]
                pe.wait_ge(mod_sum, 6 * l + s + 1)
                b0, _ = begin(f"mod{l}_{s}")
                for m in range(4):
                    ins = pe.matmul(b0[:, m:m + 1], acc[:, P * m:P * (m + 1)], ones[:, 0:1], start=True, stop=True)
                end(ins)

            def gate_rows(l):
                pe.wait_ge(diag_ready, l + 1)
                b0, b1 = begin(f"gateb{l}")
                product(b0, [(ones[:], gate_b[:, 0:512])])
                end(product(b1, [(ones[:], gate_b[:, 512:1024])]))

            pe.wait_ge(pool_set, 3)
            pe.wait_ge(prow_in, 16 * 10)
            b0, _ = begin("params")
            end(pe.transpose(b0[:, 0:NROWS], prow[0:NROWS, :], ident[0:NROWS, 0:NROWS]))
            b0, _ = begin("taps")
            end(pe.transpose(b0[:, 0:24], prow2[0:24, :], ident[0:24, 0:24]))
            modulation(0, 0)
            pe.wait_ge(consts_in, 48)
            pe.wait_ge(prow_set, 1)
            for g in range(3):
                b0, _ = begin(f"toep{g}")
                end(product(b0[0:HPG, :], [(relb[0:NB + 1, HPG * g:HPG * (g + 1)], bsel[0:NB + 1, g, :])]))
            for s in range(1, 4):
                modulation(0, s)
            pe.wait_ge(x_in, 16)
            for t in range(NT):
                turn_tile(0, t)

            def qkv(g, i):
                if g == 0 and i == 0:
                    ht_wait(pe, 0)
                t = 0 if i < 3 else 1 if i < 6 else 2
                turn = TURN[("win_a", 0, (t, g))]
                landed(pe, turn)
                w = shaped(turn, DC, GW)
                if t < 2:
                    c = i - 3 * t
                    feature_major(f"qkv{g}_{i}", w, slice(P * c, P * (c + 1)), WHOLE)
                else:
                    n = i - 6
                    b0, _ = begin(f"qkv{g}_{i}")
                    lhs = [(HT[:, k, META + P * n:META + P * (n + 1)] if g == 0 else
                            HT[:, k, META + n:TM:4]) for k in range(DC)]
                    end(product(b0[:, 0:GW], [(lhs[k], w[:, k, :]) for k in range(DC)]))

            def sg_a_job(c):
                turn = TURN[("win_a", 0, (3, c // 3))]
                landed(pe, turn)
                feature_major(f"sgA_{c}", shaped(turn, DC, GW), slice(P * (c % 3), P * (c % 3 + 1)), WHOLE)

            def rows_job(name):
                g = int(name[-1])
                pe.wait_ge(probs_ready, (24, 30, 36)[g])
                b0, _ = begin(name)
                for n in range(NT):
                    ins = pe.transpose(b0[0:HPG, P * n:P * (n + 1)], (negm if name[0] == "n" else den)[:, g, n, :], ident[:])
                end(ins)

            def scores_a(u):
                g, h, n = UNITS_A[u]
                if h == 0 and (n or 0) == 0:
                    taken(pe, f"qkv{g}_8")
                    taken(pe, f"qkv{g}_9")
                if u >= 2:
                    pe.wait_ge(scores_read, u - 1)
                b = ps[:, 4 + u % 2, :]
                lo, c = 64 * (h % 2), h // 2
                q, k = q_g[g][lo:lo + 64, c, :], k_g[g][lo:lo + 64, c, :]
                if g == 0:
                    k0, k1 = max(0, n - 1), min(NT, n + 2)
                    ins = pe.matmul(b[:, 0:P * (k1 - k0)], q[:, P * n:P * (n + 1)], k[:, P * k0:P * k1], start=True, stop=True)
                else:
                    for n in range(NT):
                        t = slice(P * n, P * (n + 1))
                        ins = pe.matmul(b[:, t], q[:, t], k[:, t], start=True, stop=True)
                ins.then_inc(scores_ready, 1)

            def width_a(u):
                g, _, n = UNITS_A[u]
                return 512 if g else P * (min(NT, n + 2) - max(0, n - 1))

            def turn_probs(u, sp, width):
                pe.wait_ge(probs_ready, u + 1)
                if u >= 2:
                    pe.wait_ge(pt_copied, u - 1)
                b = ps[:, (6, 1)[u % 2], :]
                for i in range(width // P):
                    ins = pe.transpose(b[:, P * i:P * (i + 1)], sp[u % 3][:, P * i:P * (i + 1)], ident[:])
                ins.then_inc(pt_ready, 1)

            def pv_a(u):
                g, h, n = UNITS_A[u]
                pe.wait_ge(pt_copied, u + 1)
                pair = (3 * g + h // 2)
                first = h % 2 == 0 and (n or 0) == 0
                if first and pair >= 2:
                    pe.wait_ge(o_copied, pair - 1)
                o = ps[64 * (h % 2):64 * (h % 2) + 64, (7, 3)[pair % 2], :]
                pT = pt_a[u % 2]
                hs = slice(HD * h, HD * (h + 1))
                if g == 0:
                    k0, k1 = max(0, n - 1), min(NT, n + 2)
                    ins = product(o[:, P * n:P * (n + 1)], [(v_g[g][:, k, hs], pT[:, P * (k - k0):P * (k - k0 + 1)]) for k in range(k0, k1)])
                else:
                    for n in range(NT):
                        t = slice(P * n, P * (n + 1))
                        ins = pe.matmul(o[:, t], v_g[g][:, n, hs], pT[:, t], start=True, stop=True)
                ins.then_inc(pv_done, 1)

            for i in range(10):
                qkv(0, i)
            for u in range(NUA + 2):
                if u < NUA:
                    scores_a(u)
                for name in FILL_A.get(u, []):
                    if name[:3] == "qkv":
                        qkv(int(name[3]), int(name[5:]))
                    elif name[:3] == "mod":
                        modulation(int(name[3]), int(name[5:]))
                    elif name == "gateb0":
                        gate_rows(0)
                    elif name[:-1] in ("negmax", "den"):
                        rows_job(name)
                    else:
                        sg_a_job(int(name[4:]))
                if 1 <= u <= NUA:
                    turn_probs(u - 1, scores_sb, width_a(u - 1))
                if u >= 2:
                    pv_a(u - 2)

            rows_job("negmax2")
            rows_job("den2")
            sg_a_job(7)
            sg_a_job(8)
            pe.wait_ge(factors_ready, 1)
            for c in range(9):
                b0, _ = begin(f"fac_{c}")
                end(product(b0, [(hsel[:, c % 3, :], rows_m[0:HPG, c // 3, :])]))
            turns = [TURN[("wout_a", 0, s)] for s in range(3)]
            for t in turns:
                landed(pe, t)
            parts = [(shaped(turns[k // 4], 4 if k < 8 else 1, D), k % 4) for k in range(9)]
            taken(pe, "fac_7")
            taken(pe, "fac_8")
            pe.wait_ge(pt_copied, NUA)
            pe.wait_ge(o_copied, 9)
            t0 = TURN[("win_b", 0, 0)]
            w = shaped(t0, DC, 416)
            out_and_turn(1, 0, range(NT), lambda t: token_major(f"outA_{t}", t, lambda k: oT_a[:, k, P * t:P * (t + 1)], parts),
                         early=[(f"lat_{c}", t0, w, slice(P * c, P * (c + 1)), WHOLE) for c in range(2)])

            ht_wait(pe, 1)
            for c in range(4):
                feature_major(f"lat_{c}", w, slice(P * c, P * c + (P if c < 3 else ROPE)), WHOLE, m=P if c < 3 else ROPE)
            pe.wait_ge(lat_sq, 3)
            b0, _ = begin("rms0")
            end(product(b0, [(ones[:], sgB[:, 0, :]), (ones[:], sgB[:, 1, :])]))
            b0, _ = begin("rms1")
            end(product(b0, [(ones[:], sgB[:, 2, :])]))
            gate_rows(1)

            def sg_b_job(c):
                turn = TURN[("win_b", 0, 1 + c // 4)]
                landed(pe, turn)
                feature_major(f"sgB_{c}", shaped(turn, DC, 512), slice(P * (c % 4), P * (c % 4 + 1)), WHOLE)

            for c in range(2):
                sg_b_job(c)
            tkv, tq_ = TURN[("ukv", 0, 0)], TURN[("uq", 0, 0)]
            landed(pe, tkv)
            landed(pe, tq_)
            wkv = slab(tkv)[:, 0:2048]
            wv = wkv.rearrange("p (h x f) -> p h x f", h=HB, x=2)
            wq = shaped(tq_, 2, HB * QW)
            pe.wait_ge(lat_ready, 3)
            for t in range(NT):
                b0, b1 = begin(f"vB_{t}")
                for h, b in enumerate((b0, b1)):
                    ins = pe.matmul(b, latB[:, 2, P * t:P * (t + 1)], wv[:, 8 * h:8 * h + 8, 1, :], start=True, stop=True)
                end(ins)
            def qn_kn(h):
                b0, _ = begin(f"qn_{h}")
                end(product(b0[0:QW, :], [(wq[:, k, QW * h:QW * (h + 1)], latB[:, k, :]) for k in range(2)]))
                b0, _ = begin(f"kn_{h}")
                end(product(b0[0:NOPE, :], [(wv[:, h, 0, :], latB[:, 2, :])]))

            for h in range(3):
                qn_kn(h)
            for c in range(2, DC):
                sg_b_job(c)

            def scores_b(u):
                h, t = u // NT, u % NT
                U = NUA + u
                if t == 0:
                    if h == 0:
                        pe.wait_ge(kr_ready, 5)
                        taken(pe, "vB_2")
                        taken(pe, "vB_3")
                    pe.wait_ge(qr_ready, h + 1)
                    taken(pe, f"kn_{h}")
                pe.wait_ge(scores_read, U - 1)
                b = ps[:, 4 + U % 2, :]
                pe.matmul(b, qB[h % 4][0:QW, P * t:P * (t + 1)], kB[h % 4][0:QW, :], start=True, stop=True)\
                  .then_inc(scores_ready, 1)

            def pv_b(u):
                h, t = u // NT, u % NT
                U = NUA + u
                pe.wait_ge(pt_copied, U + 1)
                pair = h // 2 + 9
                if h % 2 == 0 and t == 0:
                    pe.wait_ge(o_copied, pair - 1)
                o = ps[64 * (h % 2):64 * (h % 2) + 64, (7, 3)[pair % 2], :]
                product(o[:, P * t:P * (t + 1)], [(vB[:, k, HD * h:HD * (h + 1)], pt_b[U % 2][:, P * k:P * (k + 1)]) for k in range(NT)])\
                    .then_inc(pv_done, 1)

            taken(pe, "vB_2")
            taken(pe, "vB_3")
            for u in range(NUB + 3):
                if u < NUB:
                    scores_b(u)
                if u % 4 == 2 and u // 4 + 3 < HB:
                    qn_kn(u // 4 + 3)
                if 2 <= u < NUB + 2:
                    turn_probs(NUA + u - 2, scores_sb, 512)
                if u >= 3:
                    pv_b(u - 3)
            pe.wait_ge(pt_copied, NUA + NUB)
            pe.wait_ge(o_copied, 16)
            turns = [TURN[("wout_b", 0, s)] for s in range(2)]
            for t in turns:
                landed(pe, t)
            parts_b = [(shaped(turns[k // 4], 4, D), k % 4) for k in range(DC)]
            start_out("outB_0", 0, 0, lambda k: oT_b[:, k, 0:P], parts_b)
            pe.wait_ge(o_copied, 17)
            pe.wait_ge(meta_in, 16)
            turn_tile(2, 4)
            out_and_turn(2, 1, range(NT), lambda t: token_major(f"outB_{t}", t, lambda k: oT_b[:, k, P * t:P * (t + 1)],
                                                                [(shaped(turns[k // 4], 4, D), k % 4) for k in range(DC)]),
                         early=[(f"{n}_0", t, shaped(t, DC, 512), slice(0, P), BOTH)
                                for n, t in (("uy", TURN[("lru_in", 0, 0)]), ("ux", TURN[("lru_in", 0, 2)]))])

            ht_wait(pe, 2)

            def lru_gates(c):
                pe.wait_ge(bd_in[c % 2], 16 * 4 * (c // 2 + 1))
                pe.wait_ge(xc_ready, c + 1)
                for i, name in enumerate(("ra", "ri")):
                    b0, b1 = begin(f"{name}_{c}")
                    for h, b in enumerate((b0, b1)):
                        ins = pe.matmul(b[:, 0:264], wa_bd[:, c % 2, i, :], xcs[c % 2][:, 264 * h:264 * h + 264], start=True, stop=True)
                    end(ins)

            for c in range(DC):
                for s, name in ((c // 4, "uy"), (2 + c // 4, "ux")):
                    turn = TURN[("lru_in", 0, s)]
                    landed(pe, turn)
                    feature_major(f"{name}_{c}", shaped(turn, DC, 512), slice(P * (c % 4), P * (c % 4 + 1)), BOTH)
                if c:
                    lru_gates(c - 1)
            lru_gates(7)
            turns = [TURN[("lru_out", 0, s)] for s in range(2)]
            for t in turns:
                landed(pe, t)
            pe.wait_ge(yT_ready, DC - 1)
            parts_c = [(shaped(turns[k // 4], 4, D), k % 4) for k in range(DC)]
            start_out("outC_4", 0, 4, lambda k: yT[:, k, tokens(4)], parts_c)
            start_out("outC_0", 1, 0, lambda k: yT[:, k, tokens(0)], parts_c)
            pe.wait_ge(yT_ready, DC)
            out_and_turn(3, 2, (4, 0, 1, 2, 3), lambda t: token_major(f"outC_{t}", t, lambda k: yT[:, k, tokens(t)],
                                                                      [(shaped(turns[k // 4], 4, D), k % 4) for k in range(DC)]),
                         router(0), hold=True)

            def route(l):
                tiles = range(5 if l == 0 else 4)
                pe.wait_ge(onehot_ready, l + 1)
                b0, _ = begin(f"ranks{l}")
                for t in tiles:
                    product(b0[:, NE * t:NE * (t + 1)], [(before[:], ohb[:, t, :])] + [(ones_h[:], ohb[:, s, :]) for s in range(t)])
                end(product(b0[:, 160:192], [(ones_h[:], ohb[:, s, :]) for s in tiles]))
                b0, _ = begin(f"table{l}")
                n = 2 * len(tiles)
                for i in range(n):
                    r = rows_of(i // 2)
                    pe.wait_ge(hot_ready, (0, 10)[l] + i + 1)
                    ins = pe.matmul(b0[:, 0:NBLK], row_hot[0:r, i, :], block_hot[0:r, i, :], start=i == 0, stop=i == n - 1)
                end(ins)

            def turn_slots(E, par):
                pe.wait_ge(xe_landed[par], (E - par) * 8 + 16)
                pe.wait_ge(xet_copied, E)
                for c in range(DC):
                    ins = pe.transpose(ps[:, c // 4, P * (c % 4):P * (c % 4 + 1)], xe[par][:, P * c:P * (c + 1)], ident[:])
                ins.then_inc(xe_used, 1)

            def up_down(w, src, dst):
                for f in range(FC):
                    ins = product(dst[:, P * f:P * (f + 1)], [(w[:, k, P * f:P * (f + 1)], src[:, k, :]) for k in range(DC)])
                return ins

            def down(w, par):
                for h in range(2):
                    ins = product(ps[:, 6 + h, :], [(hb[par][:, k, :], w[:, k, 512 * h:512 * h + 512]) for k in range(FC)])
                return ins

            def expert(l, e, par, base, with_next=True):
                E = NE * l + e
                turn = [base + 3 * par + w for w in range(3)]
                def wait_slab(w):
                    pe.wait_ge(slab_landed[turn[w] % SLABS], (e - par) * 8 + 16 * (turn[w] // SLABS + 1))
                wait_slab(0)
                pe.wait_ge(xet_copied, E + 1)
                if not (isinstance(E, int) and E < 2):
                    pe.wait_ge(hb_ready, E * 2 - 2)
                g, u = ps[:, 2 + 2 * par, :], ps[:, 3 + 2 * par, :]
                up_down(expert_slab(turn[0], 0), xeT[par], g).then_inc(gate_ready, 1)
                wait_slab(1)
                up_down(expert_slab(turn[1], 1), xeT[par], u).then_inc(up_ready, 1)
                if with_next:
                    turn_slots(E + 1, 1 - par)
                wait_slab(2)
                pe.wait_ge(yo_ready, E)
                w = expert_slab(turn[2], 2)
                for k in range(FC):
                    if k % 2 == 0:
                        pe.wait_ge(hb_ready, E * 2 + 1 + k // 2)
                    for h in range(2):
                        ins = pe.matmul(ps[:, 6 + h, :], hb[par][:, k, :], w[:, k, 512 * h:512 * h + 512], start=k == 0, stop=k == FC - 1)
                ins.then_inc(y_ready, 1)

            def over_blocks(l):
                o, base = ov[l], TURN[("expert", l, (0, 0))]
                pe.wait_ge(route_ready, l + 1)
                n_over = pe.value_load(over_i[0:1, 8:9], min_val=0, max_val=NOVER)
                for j in range(NOVER):
                    with pe.If(n_over > j):
                        pe.wait_ge(o["x"], 16 * (j + 1))
                        for c in range(DC):
                            ins = pe.transpose(ps[:, c // 4, P * (c % 4):P * (c % 4 + 1)], xe[0][:, P * c:P * (c + 1)], ident[:])
                        ins.then_inc(o["xt"], 1)
                        pe.wait_ge(o["xc"], j + 1)
                        pe.wait_ge(o["w"], 48 * (j + 1))
                        up_down(expert_slab(base, 0), xeT[0], ps[:, 2, :]).then_inc(o["g"], 1)
                        up_down(expert_slab(base + 1, 1), xeT[0], ps[:, 3, :]).then_inc(o["g"], 1)
                        pe.wait_ge(o["h"], j + 1)
                        down(expert_slab(base + 2, 2), 0).then_inc(o["y"], 1)
                        pe.wait_ge(o["yo"], j + 1)
                    with pe.Else():
                        pe.nop()

            def experts(l):
                base = TURN[("expert", l, (0, 0))]
                pe.wait_ge(proj_free[0], (count[0] + 1) // 2)
                pe.wait_ge(proj_free[1], count[0] // 2)
                turn_slots(NE * l, 0)
                expert(l, 0, 0, base)
                expert(l, 1, 1, base)
                with pe.Fori(1, NE // 2 - 1) as i:
                    expert(l, i * 2, 0, base)
                    expert(l, i * 2 + 1, 1, base)
                expert(l, NE - 2, 0, base)
                expert(l, NE - 1, 1, base, with_next=False)
                pe.wait_ge(yo_ready, NE * (l + 1))
                over_blocks(l)

            route(0)
            experts(0)

            HALVES = ((META - 2, META - 2 + 257), (META - 2 + 257, TM))
            for t in (4, 0, 1, 2):
                turn_normed(4, 3, t)
            start_early([(f"{n}_0", t, shaped(t, DC, 512), slice(0, P), HALVES)
                         for n, t in (("cg", TURN[("sc_in", 0, (1, 0))]), ("cv", TURN[("sc_in", 0, (2, 0))]))], 4)
            turn_normed(4, 3, 3)
            ht_wait(pe, 4)
            for c in range(DC):
                for t, name in ((1, "cg"), (2, "cv"), (0, "bg")):
                    turn = TURN[("sc_in", 0, (t, c // 4))]
                    landed(pe, turn)
                    feature_major(f"{name}_{c}", shaped(turn, DC, 512), slice(P * (c % 4), P * (c % 4 + 1)),
                                  HALVES if t else WHOLE)
            turns = [TURN[("sc_out", 0, s)] for s in range(2)]
            for t in turns:
                landed(pe, t)
            taken(pe, "bg_6")
            taken(pe, "bg_7")
            out_and_turn(5, 4, range(NT), lambda t: token_major(f"outD_{t}", t, lambda k: zT[:, k, P * t:P * (t + 1)],
                                                                [(shaped(turns[k // 4], 4, D), k % 4) for k in range(DC)]),
                         router(1))
            route(1)
            experts(1)
            assert count[0] == len(JOBS)

        GELU_C = float(np.sqrt(2.0 / np.pi))
        ztmp = at(R0 + 13056, D)
        O_LAST = {}
        for u, (g, h, n) in enumerate(UNITS_A):
            O_LAST[3 * g + h // 2] = u
        for p_ in range(8):
            O_LAST[9 + p_] = NUA + 8 * p_ + 7
        O_AT = {u: p_ for p_, u in O_LAST.items()}

        def halves(ap2):
            return ap2.rearrange("p (a b) -> p a b", a=2)

        def job_bank(name, n=512):
            return ps[:, bank(name), 0:n]

        def job_pair(name, n=512):
            return ps[:, bank(name):bank(name) + 2, 0:n]

        def col(name, i=0):
            return cols[:, PROWS[name] + i:PROWS[name] + i + 1]

        def by_residue(ap2):
            return ap2.rearrange("p (l j) -> p j l", j=4)

        def tiles4(ap2):
            return ap2.rearrange("p (j l) -> p j l", j=4)

        @block.scalar
        def _(act):
            own = [0]

            def mark(ins):
                own[0] += 1
                ins.then_inc(act_own, 1)

            def settle():
                act.wait_ge(act_own, own[0])

            def free(ins, name):
                ins.then_inc(proj_free[JOB[name] % 2], 1)

            load_params(act, PARAMS[5:])
            act.dma_start(prow2[0:24, :], a["sc_conv_w_2"][0].rearrange("k (r p) -> (k r) p", p=P)).then_inc(prow_in, 16)
            act.dma_start(bsel[0:NB + 1, :, :], a["bucket_sel"]).then_inc(consts_in, 16)
            act.dma_start(hsel, a["head_sel"]).then_inc(consts_in, 16)
            act.dma_start(relb[0:NB, :], a["rel_bias"]).then_inc(consts_in, 16)
            act.dma_start(x_first, a["x"][0].rearrange("(t p) d -> p t d", p=P)).then_inc(x_in, 16)

            taken(act, "params")
            act.activation(csilu[:, 0, :], cols[:, PROWS["c"]:PROWS["c"] + DC], ACT.Tanh, scale=0.5).then_inc(lam_a, 1)
            act.wait_ge(lam_b, 1)
            mark(act.activation(lamc[:, 1, :], lamc[:, 0, :], ACT.Exp, scale=-1.0))
            settle()
            act.activation(lamc[:, 2, :], lamc[:, 1, :], ACT.Ln, bias=1.0).then_inc(lam_a, 1)

            def turn_copy(k, t):
                n = TURNED[(k, t)]
                r = rows_of(t)
                act.wait_ge(turned, 2 * n + 1)
                src = turn_bank(n, 0)
                if k >= 2:
                    ins = act.activation(HT[:, 0:4, tokens(t)], src[:, 0:4 * r].rearrange("p (c t) -> p c t", t=r), ACT.Copy)
                else:
                    for c in range(4):
                        ins = act.activation(HT[:, c, tokens(t)], src[:, P * c:P * (c + 1)], ACT.Identity,
                                             bias=mod[:, k, c:c + 1], scale=mod[:, k, 8 + c:9 + c])
                        if c < 3:
                            mark(ins)
                ins.then_inc(turn_copied[0], 1)

            def normed_and_turned(k, l, order, lag=1):
                for i, t in enumerate(order):
                    deviation(l, t)
                    if i >= lag:
                        turn_copy(k, order[i - lag])
                for t in order[-lag:]:
                    turn_copy(k, t)

            def deviation(l, t):
                n = LN[(l, t)]
                act.wait_ge(var_ready, n + 1)
                r, o = rows_of(t), 32 * (n % 2)
                act.activation(spec[0:r, o + 15:o + 16], spec[0:r, o + 14:o + 15], ACT.Sqrt).then_inc(sd_ready, 1)
                if l in (3, 5):
                    m = COMBINED[(l, t)]
                    act.wait_ge(scale_ready, m + 1)
                    act.activation(X[0:r, t, :], X[0:r, t, :], ACT.Identity, scale=spec[0:r, o + 16:o + 17],
                                   bias=spec[0:r, o + 17:o + 18]).then_inc(normed, 1)

            taken(act, "mod0_2")
            taken(act, "mod0_3")
            for t in range(NT):
                turn_copy(0, t)

            def qkv_out(g, i):
                name = f"qkv{g}_{i}"
                done(act, name)
                if i == 0 and g == 2:
                    act.wait_ge(pv_done, 24)
                if i < 6:
                    dst = (q_g if i < 3 else k_g)[g][:, i % 3, :]
                    src = job_bank(name)
                    if g:
                        dst, src = tiles4(dst), by_residue(src)
                    free(act.activation(dst, src, ACT.Copy), name)
                else:
                    free(act.activation(v_g[g][:, i - 6, :], job_bank(name, GW), ACT.Copy), name)

            def silu_tanh(name, dst, n=512):
                done(act, name)
                act.activation(dst, job_bank(name, n), ACT.Tanh, scale=0.5).then_inc(silu_ready, 1)

            def pt_copy(U, pT):
                act.wait_ge(pt_ready, U + 1)
                if U >= 2:
                    act.wait_ge(pv_done, U - 1)
                w = 512 if U >= NUA or UNITS_A[U][0] else P * (min(NT, UNITS_A[U][2] + 2) - max(0, UNITS_A[U][2] - 1))
                act.activation(pT[U % 2][:, 0:w], ps[:, (6, 1)[U % 2], 0:w], ACT.Copy).then_inc(pt_copied, 1)

            for i in range(10):
                qkv_out(0, i)
            for u in range(NUA + 1):
                if u < NUA:
                    g, h, n = UNITS_A[u]
                    act.wait_ge(max_ready, u + 1)
                    sp = scores_sb[u % 3]
                    if g == 0:
                        w = P * (min(NT, n + 2) - max(0, n - 1))
                        act.activation(sp[:, 0:w], sp[:, 0:w], ACT.Exp, bias=negm[:, 0, n, h:h + 1],
                                       accum_out=den[:, 0, n, h:h + 1]).then_inc(probs_ready, 1)
                    else:
                        for n in range(NT):
                            t = slice(P * n, P * (n + 1))
                            ins = act.activation(sp[:, t], sp[:, t], ACT.Exp, bias=negm[:, g, n, h:h + 1],
                                                 accum_out=den[:, g, n, h:h + 1])
                            if n < NT - 1:
                                mark(ins)
                        ins.then_inc(probs_ready, 1)
                for name in FILL_A.get(u, []):
                    if name[:3] == "qkv":
                        qkv_out(int(name[3]), int(name[5:]))
                    elif name[:3] == "sgA":
                        if name == "sgA_0":
                            act.wait_ge(pv_done, 30)
                        silu_tanh(name, sg_a[:, int(name[4:]), :])
                if u >= 1:
                    pt_copy(u - 1, pt_a)
            act.wait_ge(fac_in, 1)
            act.activation(at(R0 + 9216, 3 * S)[0:HPG, :], at(R0 + 9216, 3 * S)[0:HPG, :], ACT.Exp).then_inc(fac_exp, 1)
            for c in (7, 8):
                silu_tanh(f"sgA_{c}", sg_a[:, c, :])

            normed_and_turned(1, 0, range(NT))

            for c in range(3):
                done(act, f"lat_{c}")
                act.activation(sgB[:, c, :], job_bank(f"lat_{c}"), ACT.Square).then_inc(lat_sq, 1)
            act.wait_ge(kr_ready, 1)
            for i in range(4):
                act.activation(kB[i][NOPE:QW, :], krB[0:ROPE, :], ACT.Copy).then_inc(kr_ready, 1)
            for i in range(2):
                taken(act, f"rms{i}")
                act.activation(tmp_b[i], tmp_b[i], ACT.Sqrt).then_inc(rms_sd, 1)
            for c in range(2):
                silu_tanh(f"sgB_{c}", sgB[:, c, :])
            act.wait_ge(x1_out, 64)
            for t in range(NT):
                done(act, f"vB_{t}")
                free(act.activation(halves(vB[:, t, :]), job_pair(f"vB_{t}"), ACT.Copy), f"vB_{t}")
            def qn_kn_out(h):
                for name, dst, n in ((f"qn_{h}", qB[h % 4], QW), (f"kn_{h}", kB[h % 4], NOPE)):
                    done(act, name)
                    if h >= 4:
                        act.wait_ge(scores_ready, NUA + NT * (h - 3))
                    free(act.activation(dst[0:n, :], job_bank(name)[0:n, :], ACT.Copy), name)

            for h in range(3):
                qn_kn_out(h)
            for c in range(2, DC):
                silu_tanh(f"sgB_{c}", sgB[:, c, :])
            for u in range(NUB + 2):
                if u < NUB:
                    U = NUA + u
                    act.wait_ge(max_ready, U + 1)
                    act.wait_ge(pt_ready, U - 2)
                    act.activation(scores_sb[U % 3], ps[:, 4 + U % 2, :], ACT.Exp, bias=nmax[:, 4 + U % 4:5 + U % 4],
                                   scale=SCALE_B, accum_out=dsum[:, U % 4:U % 4 + 1]).then_inc(scores_read, 1)
                if u % 4 == 2 and u // 4 + 3 < HB:
                    qn_kn_out(u // 4 + 3)
                if u >= 2:
                    pt_copy(NUA + u - 2, pt_b)
            turn_copy(2, 4)
            normed_and_turned(2, 1, range(NT))

            def lru_decay(c):
                if c >= 2:
                    act.wait_ge(yT_ready, c - 1)
                for name, dst, hbias in ((f"ra_{c}", sT, 0), (f"ri_{c}", gx, 1)):
                    done(act, name)
                    free(act.activation(halves(dst[:, c % 2, :]), job_pair(name, 264), ACT.Tanh, scale=0.5,
                                        bias=half_b[:, hbias, c:c + 1]), name)
                taken(act, f"ra_{c}")
                mark(act.activation(root[:, c % 2, :], sT[:, c % 2, :], ACT.Tanh, scale=lamc[:, 0, c:c + 1], bias=lamc[:, 0, c:c + 1]))
                settle()
                act.activation(sT[:, c % 2, :], sT[:, c % 2, :], ACT.Exp, scale=lamc[:, 1, c:c + 1], bias=lamc[:, 1, c:c + 1])\
                   .then_inc(s_ready, 1)
                act.activation(root[:, c % 2, :], root[:, c % 2, :], ACT.Sqrt, scale=-1.0).then_inc(root_ready, 1)

            for c in range(DC):
                done(act, f"uy_{c}")
                if c:
                    taken(act, f"uy_{c - 1}")
                act.activation(halves(tA), job_pair(f"uy_{c}", 264), ACT.Square).then_inc(gelu_sq, 1)
                act.wait_ge(gelu_in, c + 1)
                act.activation(tB, tB, ACT.Tanh, scale=GELU_C).then_inc(gelu_th, 1)
                done(act, f"ux_{c}")
                if c:
                    act.wait_ge(xc_ready, c)
                free(act.activation(halves(upad[:, 3:TM + 3]), job_pair(f"ux_{c}", 264), ACT.Copy), f"ux_{c}")
                if c:
                    lru_decay(c - 1)
            lru_decay(7)
            normed_and_turned(3, 2, (4, 0, 1, 2, 3))

            def xet_copy(E, par, first=False):
                act.wait_ge(xe_used, E + 1)
                if not first:
                    act.wait_ge(up_ready, E - 1)
                act.activation(xeT[par], ps[:, 0:2, :].rearrange("p a (b c) -> p (a b) c", c=P), ACT.Copy).then_inc(xet_copied, 1)

            def expert(l, e, par, with_next=True):
                E = NE * l + e
                early = isinstance(E, int) and E < 2
                act.wait_ge(gate_ready, E + 1)
                if not early:
                    act.wait_ge(hb_ready, E * 2 - 2)
                act.activation(zg[par], ps[:, 2 + 2 * par, :], ACT.Tanh, scale=0.5).then_inc(tanh_ready, 1)
                if with_next:
                    xet_copy(E + 1, 1 - par, first=isinstance(E, int) and E + 1 < 2)
                act.wait_ge(y_ready, E + 1)
                if not early:
                    act.wait_ge(yo_sent[par], (E - par) * 8)
                act.activation(halves(yo[par]), ps[:, 6:8, :], ACT.Copy).then_inc(yo_ready, 1)

            def experts(l):
                xet_copy(NE * l, 0, first=l == 0)
                expert(l, 0, 0)
                expert(l, 1, 1)
                with act.Fori(1, NE // 2 - 1) as i:
                    expert(l, i * 2, 0)
                    expert(l, i * 2 + 1, 1)
                expert(l, NE - 2, 0)
                expert(l, NE - 1, 1, with_next=False)
                o = ov[l]
                act.wait_ge(route_ready, l + 1)
                n_over = act.value_load(over_i[0:1, 8:9], min_val=0, max_val=NOVER)
                for j in range(NOVER):
                    with act.If(n_over > j):
                        act.wait_ge(o["xt"], j + 1)
                        act.activation(xeT[0], ps[:, 0:2, :].rearrange("p a (b c) -> p (a b) c", c=P), ACT.Copy).then_inc(o["xc"], 1)
                        act.wait_ge(o["g"], 2 * j + 1)
                        act.activation(zg[0], ps[:, 2, :], ACT.Tanh, scale=0.5).then_inc(o["t"], 1)
                        act.wait_ge(o["y"], j + 1)
                        if j == 0:
                            act.wait_ge(yo_sent[0], 8 * NE * (l + 1))
                        else:
                            act.wait_ge(o["out"], 16 * j)
                        act.activation(halves(yo[0]), ps[:, 6:8, :], ACT.Copy).then_inc(o["yo"], 1)
                    with act.Else():
                        act.nop()

            def route(l):
                act.wait_ge(pg_in, l + 1)
                mark(act.activation(adr[:, :, 0:NG], adr[:, :, 0:NG], ACT.Exp))
                act.activation(sm[:, 5, :], sm[:, 4, :], ACT.Exp).then_inc(pg_exp, 1)

            route(0)
            experts(0)
            normed_and_turned(4, 3, (4, 0, 1, 2, 3), lag=2)
            for c in range(DC):
                done(act, f"cg_{c}")
                if c >= 2:
                    taken(act, f"cv_{c - 2}")
                free(act.activation(halves(cgs[c % 2]), job_pair(f"cg_{c}", 257), ACT.Copy), f"cg_{c}")
            normed_and_turned(5, 4, range(NT))
            route(1)
            experts(1)
            for t in range(NT):
                deviation(5, t)

        @block.vector
        def _(vec):
            own = [0]

            def mark(ins):
                own[0] += 1
                ins.then_inc(vec_own, 1)

            def settle():
                vec.wait_ge(vec_own, own[0])

            def step(ins):
                mark(ins)
                settle()

            def free(ins, name):
                ins.then_inc(proj_free[JOB[name] % 2], 1)

            done(vec, "params")
            free(vec.tensor_copy(cols[:, 0:NROWS], job_bank("params", NROWS)), "params")
            done(vec, "taps")
            free(vec.tensor_copy(cols[:, SC0:SC0 + 24], job_bank("taps", 24)), "taps")
            taken(vec, "params")
            taken(vec, "taps")
            lam = cols[:, PROWS["lam"]:PROWS["lam"] + DC]
            vec.scalar_tensor_tensor(lamc[:, 0, :], lam, -1.0, lam, ALU.mult, ALU.max).then_inc(lam_b, 1)
            mark(vec.tensor_scalar(lamc[:, 3, :], lam, -1.0, 0.0, ALU.mult, ALU.max))
            for i, n in enumerate(("b_a", "b_i")):
                mark(vec.tensor_scalar(half_b[:, i, :], cols[:, PROWS[n]:PROWS[n] + DC], 0.5, None, ALU.mult))
            vec.wait_ge(lam_a, 1)
            step(vec.scalar_tensor_tensor(csilu[:, 0, :], csilu[:, 0, :], 1.0, cols[:, PROWS["c"]:PROWS["c"] + DC], ALU.add, ALU.mult))
            vec.tensor_scalar(csilu[:, 1, :], csilu[:, 0, :], 0.5, None, ALU.mult).then_inc(csilu_ready, 1)
            vec.wait_ge(lam_a, 2)
            step(vec.tensor_tensor(lamc[:, 0, :], lamc[:, 3, :], lamc[:, 2, :], ALU.add))
            mark(vec.tensor_scalar(lamc[:, 1, :], lamc[:, 0, :], -4.0, None, ALU.mult))
            step(vec.tensor_scalar(lamc[:, 0, :], lamc[:, 0, :], -2.0, None, ALU.mult))

            def modulation_sum(l, s):
                turn = TURN[("ada", l, s)]
                w = shaped(turn, DC, 512)
                landed(vec, turn)
                step(vec.tensor_scalar(w[:, 0, :], w[:, 0, :], csilu[:, 1, 0:1], None, ALU.mult))
                for k in range(1, DC):
                    ins = vec.scalar_tensor_tensor(w[:, 0, :], w[:, k, :], csilu[:, 1, k:k + 1], w[:, 0, :], ALU.mult, ALU.add)
                    if k < DC - 1:
                        step(ins)
                ins.then_inc(mod_sum, 1)

            def modulation(l, s):
                name = f"mod{l}_{s}"
                done(vec, name)
                o = PROWS["ada_b"] + 24 * l + 4 * s
                free(vec.scalar_tensor_tensor(mod[:, l, 4 * s:4 * s + 4], job_bank(name, 4), 1.0 if s in (2, 3) else 0.0,
                                              cols[:, o:o + 4], ALU.add, ALU.add), name)

            def turn_copy(k, t):
                n = TURNED[(k, t)]
                r = rows_of(t)
                vec.wait_ge(turned, 2 * n + 2)
                src = turn_bank(n, 1)
                if k >= 2:
                    ins = vec.tensor_copy(HT[:, 4:8, tokens(t)], src[:, 0:4 * r].rearrange("p (c t) -> p c t", t=r))
                else:
                    for c in range(4):
                        ins = vec.tensor_scalar(HT[:, 4 + c, tokens(t)], src[:, P * c:P * (c + 1)], mod[:, k, 12 + c:13 + c],
                                                mod[:, k, 4 + c:5 + c], ALU.mult, ALU.add)
                        if c < 3:
                            mark(ins)
                ins.then_inc(turn_copied[1], 1)

            def finish_and_turn(k, order, finish, logits=None, lag=1):
                for i, t in enumerate(order):
                    finish(t)
                    if i >= lag:
                        turn_copy(k, order[i - lag])
                    if logits and i > 1:
                        logits(order[i - 2])
                if lag == 2:
                    turn_copy(k, order[-2])
                affine_last(k - 1, order[-1])
                turn_copy(k, order[-1])
                if logits:
                    logits(order[-2])
                    logits(order[-1])

            def logits(l):
                def tile(t):
                    r, name = rows_of(t), f"router{l}_{t}"
                    done(vec, name)
                    mark(vec.tensor_tensor(lg[0:r, t, 0:NG], job_bank(name)[0:r, 0:NG], rb[0:r, l, 0:NG], ALU.add))
                    free(vec.tensor_tensor(lg[0:r, t, 8:40], job_bank(name)[0:r, NG:36], rb[0:r, l, NG:36], ALU.add), name)
                return tile

            def clear_routing():
                vec.wait_ge(rw_in, 16 * 8)
                mark(vec.memset(lg, 0.0))
                mark(vec.memset(ohb, 0.0))
                mark(vec.memset(cnt[:, 3, :], 0.0))
                settle()
                step(vec.memset(lg[:, :, NG:8], NEG))

            def affine_last(l, t):
                n = LN[(l, t)]
                x = X[:, t, :]
                vec.wait_ge(normed, n + 1)
                vec.wait_ge(lnp_in, 32 * (l + 1))
                step(vec.tensor_tensor(x, x, lnp[:, 0, :], ALU.mult))
                vec.wait_ge(ln_done, n)
                vec.tensor_tensor(x, x, lnp[:, 1, :], ALU.add).then_inc(ln_done, 1)

            def gate_diagonals(l):
                for c in range(DC):
                    ins = vec.tensor_scalar(gate_b[:, P * c:P * (c + 1)], ident[:], mod[:, l, 16 + c:17 + c], None, ALU.mult)
                    if c < DC - 1:
                        mark(ins)
                ins.then_inc(diag_ready, 1)

            def gate_copy(l):
                done(vec, f"gateb{l}")
                free(vec.tensor_copy(halves(gate_b[:]), job_pair(f"gateb{l}")), f"gateb{l}")

            vec.wait_ge(csilu_ready, 1)
            for s in range(4):
                modulation_sum(0, s)
                if s:
                    modulation(0, s - 1)
                if s == 1:
                    for g in range(3):
                        done(vec, f"toep{g}")
                        free(vec.tensor_copy(brow[0:HPG, g, :], job_bank(f"toep{g}")[0:HPG, :]), f"toep{g}")
            modulation(0, 3)
            taken(vec, "mod0_2")
            taken(vec, "mod0_3")
            for t in range(NT):
                turn_copy(0, t)

            def scores_max_a(u):
                g, h, n = UNITS_A[u]
                vec.wait_ge(scores_ready, u + 1)
                if u == 0:
                    vec.wait_ge(toep_in, 16 * 3)
                if u >= 3:
                    vec.wait_ge(pt_ready, u - 2)
                b, sp = ps[:, 4 + u % 2, :], scores_sb[u % 3]
                if g == 0:
                    k0, k1 = max(0, n - 1), min(NT, n + 2)
                    w = P * (k1 - k0)
                    o = P * (k0 - n + 1)
                    vec.scalar_tensor_tensor(sp[:, 0:w], b[:, 0:w], HD ** -0.5, backwards(bias0[:, h, 384 - o - w:384 - o]), ALU.mult, ALU.add)\
                       .then_inc(scores_read, 1)
                    vec.wait_ge(scores_read, u + 1)
                    vec.tensor_reduce(negm[:, 0, n, h:h + 1], sp[:, 0:w], AX.X, ALU.max, negate=True).then_inc(max_ready, 1)
                else:
                    vec.scalar_tensor_tensor(tiles4(sp), tiles4(b), HD ** -0.5, spread(backwards(bias12[g - 1][:, h, :]), 1, NT),
                                             ALU.mult, ALU.add).then_inc(scores_read, 1)
                    vec.wait_ge(scores_read, u + 1)
                    vec.tensor_reduce(negm[:, g, :, h], tiles4(sp), AX.X, ALU.max, negate=True).then_inc(max_ready, 1)

            def o_copy_a(pair):
                vec.wait_ge(pv_done, O_LAST[pair] + 1)
                g = pair // 3
                src, dst = ps[:, (7, 3)[pair % 2], :], oT_a[:, pair, :]
                if g:
                    src, dst = tiles4(src), by_residue(dst)
                vec.tensor_copy(dst, src).then_inc(o_copied, 1)

            def silu_times(name, dst, k):
                vec.wait_ge(silu_ready, k + 1)
                free(vec.scalar_tensor_tensor(dst, dst, 1.0, job_bank(name), ALU.add, ALU.mult), name)

            def rows_copy(name):
                g = int(name[-1])
                done(vec, name)
                src, d = job_bank(name)[0:HPG, :], (rows_m if name[0] == "n" else rows_d)[0:HPG, g, :]
                if g:
                    src, d = tiles4(src), by_residue(d)
                free(vec.tensor_copy(d, src), name)

            def gate_o(cs):
                taken(vec, f"sgA_{cs[-1] - 1}")
                taken(vec, f"sgA_{cs[-1]}")
                vec.wait_ge(o_copied, cs[-1] + 1)
                for c in cs:
                    mark(vec.scalar_tensor_tensor(oT_a[:, c, :], oT_a[:, c, :], 0.5, sg_a[:, c, :], ALU.mult, ALU.mult))

            for u in range(NUA + 2):
                if u < NUA:
                    scores_max_a(u)
                elif u == NUA:
                    gate_o((0, 1, 2))
                if u + 1 in MOD_AT:
                    modulation_sum(*LATE_MODS[MOD_AT.index(u + 1)])
                for name in FILL_A.get(u, []):
                    if name[:3] == "sgA":
                        c = int(name[4:])
                        silu_times(name, sg_a[:, c, :], c)
                    elif name[:3] == "mod":
                        modulation(int(name[3]), int(name[5:]))
                        if name == "mod0_5":
                            taken(vec, "mod0_4")
                            taken(vec, "mod0_5")
                            vec.wait_ge(pool_set, 3)
                            gate_diagonals(0)
                    elif name == "gateb0":
                        gate_copy(0)
                    elif name[:-1] in ("negmax", "den"):
                        rows_copy(name)
                if u >= 3 and (u - 3) in O_AT:
                    o_copy_a(O_AT[u - 3])
            for u in range(NUA - 1, NUA + 2):
                if u in O_AT and u >= NUA - 1:
                    o_copy_a(O_AT[u])

            rows_copy("negmax2")
            rows_copy("den2")
            taken(vec, "negmax1")
            taken(vec, "den1")
            taken(vec, "negmax2")
            taken(vec, "den2")
            m_, d_, t_, s_ = rows_m[0:HPG], rows_d[0:HPG], rows_t[0:HPG, :], rows_s[0:HPG, :]
            step(vec.tensor_tensor(t_, m_[:, 0, :], m_[:, 1, :], ALU.min))
            step(vec.tensor_tensor(t_, t_, m_[:, 2, :], ALU.min))
            vec.tensor_tensor(m_, spread(t_, 1, 3), m_, ALU.subtract).then_inc(fac_in, 1)
            gate_o((3, 4, 5))
            vec.wait_ge(fac_exp, 1)
            step(vec.tensor_tensor(d_, d_, m_, ALU.mult))
            step(vec.tensor_tensor(s_, d_[:, 0, :], d_[:, 1, :], ALU.add))
            step(vec.tensor_tensor(s_, s_, d_[:, 2, :], ALU.add))
            step(vec.reciprocal(s_, s_))
            vec.tensor_tensor(m_, m_, spread(s_, 1, 3), ALU.mult).then_inc(factors_ready, 1)
            for c in (7, 8):
                silu_times(f"sgA_{c}", sg_a[:, c, :], c)
            settle()
            for c in range(9):
                if c == 3:
                    gate_o((6, 7, 8))
                    settle()
                done(vec, f"fac_{c}")
                free(vec.tensor_tensor(oT_a[:, c, :], oT_a[:, c, :], job_bank(f"fac_{c}"), ALU.mult), f"fac_{c}")
            def normalise(l, t):
                n = LN[(l, t)]
                r, o = rows_of(t), 32 * (n % 2)
                x = X[0:r, t, :]
                for h in range(2):
                    mark(vec.bn_stats(spec[0:r, o + 6 * h:o + 6 * h + 6], x[:, 512 * h:512 * h + 512]))
                settle()
                step(vec.bn_aggr(spec[0:r, o + 12:o + 14], spec[0:r, o:o + 12]))
                vec.tensor_scalar(spec[0:r, o + 14:o + 15], spec[0:r, o + 13:o + 14], LN_EPS, None, ALU.add).then_inc(var_ready, 1)
                vec.wait_ge(sd_ready, n + 1)
                step(vec.reciprocal(spec[0:r, o + 16:o + 17], spec[0:r, o + 15:o + 16]))
                if l in (3, 5):
                    vec.scalar_tensor_tensor(spec[0:r, o + 17:o + 18], spec[0:r, o + 12:o + 13], -1.0, spec[0:r, o + 16:o + 17],
                                             ALU.mult, ALU.mult).then_inc(scale_ready, 1)
                    return
                vec.tensor_scalar(x, x, spec[0:r, o + 12:o + 13], spec[0:r, o + 16:o + 17], ALU.subtract, ALU.mult)\
                   .then_inc(normed, 1)

            def gated_residual(l, t, name):
                done(vec, name)
                free(vec.tensor_tensor(halves(ztmp), job_pair(name), halves(gate_b[:]), ALU.mult), name)
                taken(vec, name)
                step(vec.scalar_tensor_tensor(X[:, t, :], X[:, t, :], ALPHA, ztmp, ALU.mult, ALU.add))
                normalise(l, t)

            def residual(l, t, name):
                r = rows_of(t)
                done(vec, name)
                free(vec.scalar_tensor_tensor(halves(X[0:r, t, :]), halves(X[0:r, t, :]), ALPHA, job_pair(name)[0:r],
                                              ALU.mult, ALU.add), name)
                taken(vec, name)
                normalise(l, t)

            taken(vec, "gateb0")
            vec.wait_ge(x_back, 16)
            finish_and_turn(1, range(NT), lambda t: gated_residual(0, t, f"outA_{t}"))
            gate_diagonals(1)

            for c in range(3):
                name = f"lat_{c}"
                done(vec, name)
                vec.wait_ge(lat_sq, c + 1)
                free(vec.tensor_copy(latB[:, c, :], job_bank(name)), name)
            SWAP = [(i + 16) % 32 for i in range(32)]
            vec.wait_ge(rot_in, 16)
            done(vec, "lat_3")
            free(vec.tensor_copy(tmp_b[0][0:32, :], job_bank("lat_3")[0:32, :]), "lat_3")
            taken(vec, "lat_3")
            step(vec.stream_shuffle(tmp_b[1][0:32, :], tmp_b[0][0:32, :], SWAP))
            mark(vec.tensor_tensor(tmp_b[0][0:32, :], tmp_b[0][0:32, :], rot[0:32, 0, :], ALU.mult))
            step(vec.tensor_tensor(tmp_b[1][0:32, :], tmp_b[1][0:32, :], rot[0:32, 1, :], ALU.mult))
            vec.tensor_tensor(krB[0:32, :], tmp_b[0][0:32, :], tmp_b[1][0:32, :], ALU.add).then_inc(kr_ready, 1)
            vec.wait_ge(kr_ready, 1)
            for i, width in enumerate((QL, KVL)):
                done(vec, f"rms{i}")
                free(vec.tensor_scalar(tmp_b[i], job_bank(f"rms{i}"), 1.0 / width, RMS_EPS, ALU.mult, ALU.add), f"rms{i}")
            gate_copy(1)
            vec.wait_ge(rms_sd, 2)
            for i in range(2):
                mark(vec.reciprocal(tmp_b[i], tmp_b[i]))
            settle()
            for c, (gain, i) in enumerate(((col("qn", 0), 0), (col("qn", 1), 0), (col("kvn"), 1))):
                vec.scalar_tensor_tensor(latB[:, c, :], latB[:, c, :], gain, tmp_b[i], ALU.mult, ALU.mult).then_inc(lat_ready, 1)
            vec.wait_ge(lat_ready, 3)
            for c in range(2):
                silu_times(f"sgB_{c}", sgB[:, c, :], 9 + c)

            def swap_q(h):
                taken(vec, f"qn_{h}")
                if h:
                    vec.wait_ge(qr_ready, h)
                vec.stream_shuffle(q_swap[NOPE:QW, :], qB[h % 4][NOPE:QW, :], SWAP).then_inc(q_swapped, 1)

            def scores_max_b(U):
                vec.wait_ge(scores_ready, U + 1)
                step(vec.tensor_reduce(nmax[:, U % 4:U % 4 + 1], ps[:, 4 + U % 2, :], AX.X, ALU.max, negate=True))
                vec.tensor_scalar(nmax[:, 4 + U % 4:5 + U % 4], nmax[:, U % 4:U % 4 + 1], SCALE_B, None, ALU.mult).then_inc(max_ready, 1)

            def probs_b(U):
                vec.wait_ge(scores_read, U + 1)
                step(vec.reciprocal(dsum[:, 4 + U % 4:5 + U % 4], dsum[:, U % 4:U % 4 + 1]))
                vec.tensor_scalar(scores_sb[U % 3], scores_sb[U % 3], dsum[:, 4 + U % 4:5 + U % 4], None, ALU.mult).then_inc(probs_ready, 1)

            def o_copy_b(pair):
                vec.wait_ge(pv_done, O_LAST[pair] + 1)
                vec.scalar_tensor_tensor(oT_b[:, pair - 9, :], ps[:, (7, 3)[pair % 2], :], 0.5, sgB[:, pair - 9, :],
                                         ALU.mult, ALU.mult).then_inc(o_copied, 1)

            for h in range(3):
                swap_q(h)
            for c in range(2, DC):
                silu_times(f"sgB_{c}", sgB[:, c, :], 9 + c)
            taken(vec, "sgB_6")
            taken(vec, "sgB_7")

            for u in range(NUB + 1):
                if u < NUB:
                    scores_max_b(NUA + u)
                if u >= 1:
                    probs_b(NUA + u - 1)
                if u % 4 == 3 and u // 4 + 3 < HB:
                    swap_q(u // 4 + 3)
                if u >= 12 and (u - 12) % 8 == 0 and (u - 12) // 8 < 7:
                    o_copy_b(9 + (u - 12) // 8)
            o_copy_b(16)
            vec.wait_ge(x1_back, 16)
            turn_copy(2, 4)
            finish_and_turn(2, range(NT), lambda t: gated_residual(1, t, f"outB_{t}"))

            mark(vec.memset(upad[:, 0:3], 0.0))
            settle()

            def lru_scan(c):
                taken(vec, f"ri_{c}")
                step(vec.scalar_tensor_tensor(gx[:, c % 2, :], gx[:, c % 2, :], 1.0, xcs[c % 2], ALU.add, ALU.mult))
                vec.wait_ge(s_ready, c + 1)
                vec.wait_ge(root_ready, c + 1)
                step(vec.scalar_tensor_tensor(root[:, c % 2, :], sT[:, c % 2, :], 1.0, root[:, c % 2, :], ALU.add, ALU.mult))
                step(vec.tensor_tensor(gx[:, c % 2, :], gx[:, c % 2, :], root[:, c % 2, :], ALU.mult))
                step(vec.tensor_tensor_scan(sT[:, c % 2, :], sT[:, c % 2, :], gx[:, c % 2, :], 0.0, ALU.mult, ALU.add))
                vec.scalar_tensor_tensor(yT[:, c, :], sT[:, c % 2, :], 0.25, yT[:, c, :], ALU.mult, ALU.mult).then_inc(yT_ready, 1)

            for c in range(DC):
                name = f"uy_{c}"
                done(vec, name)
                vec.wait_ge(gelu_sq, c + 1)
                step(vec.tensor_scalar(tA, tA, 0.044715, 1.0, ALU.mult, ALU.add))
                vec.tensor_tensor(halves(tB), halves(tA), job_pair(name, 264), ALU.mult).then_inc(gelu_in, 1)
                vec.wait_ge(gelu_th, c + 1)
                free(vec.scalar_tensor_tensor(halves(yT[:, c, :]), halves(tB), 1.0, job_pair(name, 264), ALU.add, ALU.mult), name)
                taken(vec, f"ux_{c}")
                xc = xcs[c % 2]
                step(vec.tensor_scalar(xc, upad[:, 0:TM], col("conv_w", c), col("conv_b", c), ALU.mult, ALU.add))
                for k in range(1, 4):
                    ins = vec.scalar_tensor_tensor(xc, upad[:, k:TM + k], col("conv_w", 8 * k + c), xc, ALU.mult, ALU.add)
                    if k < 3:
                        step(ins)
                ins.then_inc(xc_ready, 1)
                vec.wait_ge(xc_ready, c + 1)
                if c:
                    lru_scan(c - 1)
            lru_scan(7)
            clear_routing()
            finish_and_turn(3, (4, 0, 1, 2, 3), lambda t: residual(2, t, f"outC_{t}"), logits(0))

            def route(l):
                tiles = range(5 if l == 0 else 4)
                taken(vec, f"router{l}_2")
                taken(vec, f"router{l}_3")
                settle()
                for t in range(5):
                    mark(vec.max(g8[:, t, :], lg[:, t, 0:8]))
                settle()
                for t in range(5):
                    mark(vec.max_index(gi8[:, t, :], g8[:, t, :], lg[:, t, 0:8]))
                mark(vec.tensor_tensor(adr[:, :, 0:NG], lg[:, :, 0:NG], spread(g8[:, :, 0], 2, NG), ALU.subtract))
                settle()
                step(vec.tensor_copy(sm[:, 1, :], gi8[:, :, 0]))
                for t in range(5):
                    mark(vec.tensor_scalar(tq[:, t, :], group_of[:], sm[:, 1, t:t + 1], None, ALU.is_equal))
                settle()
                step(vec.tensor_tensor(elm, lg[:, :, 8:40], tq, ALU.mult))
                step(vec.tensor_scalar(tq, tq, 1.0, -NEG, ALU.subtract, ALU.mult))
                step(vec.tensor_tensor(elm, elm, tq, ALU.add))
                for t in range(5):
                    mark(vec.max(e8[:, t, :], elm[:, t, :]))
                settle()
                for t in range(5):
                    mark(vec.max_index(ei8[:, t, :], e8[:, t, :], elm[:, t, :]))
                vec.tensor_tensor(sm[:, 4, :], e8[:, :, 1], e8[:, :, 0], ALU.subtract).then_inc(pg_in, 1)
                settle()
                for k in range(2):
                    mark(vec.tensor_copy(sm[:, 2 + k, :], ei8[:, :, k]))
                settle()
                for t in range(5):
                    mark(vec.tensor_scalar(oh1[:, t, :], expert_of[:], sm[:, 2, t:t + 1], None, ALU.is_equal))
                    mark(vec.tensor_scalar(oh2[:, t, :], expert_of[:], sm[:, 3, t:t + 1], None, ALU.is_equal))
                settle()
                if l == 0:
                    mark(vec.tensor_tensor(ohb[0:META, 4, :], oh1[0:META, 4, :], oh2[0:META, 4, :], ALU.add))
                vec.tensor_tensor(ohb[:, 0:4, :], oh1[:, 0:4, :], oh2[:, 0:4, :], ALU.add).then_inc(onehot_ready, 1)
                vec.wait_ge(pg_exp, l + 1)
                step(vec.tensor_reduce(sm[:, 6, :], adr[:, :, 0:NG], AX.X, ALU.add))
                step(vec.scalar_tensor_tensor(sm[:, 7, :], sm[:, 5, :], 1.0, sm[:, 6, :], ALU.add, ALU.mult))
                step(vec.reciprocal(gates[:, 0, :], sm[:, 7, :]))
                mark(vec.tensor_tensor(gates[:, 1, :], gates[:, 0, :], sm[:, 5, :], ALU.mult))
                name = f"ranks{l}"
                done(vec, name)
                b = job_bank(name)
                nt = 5 if l == 0 else 4
                c = b[:, 0:NE * nt].rearrange("p (t n) -> p t n", n=NE)
                A, T_ = adr[:, 0:nt, :], tq[:, 0:nt, :]
                mark(vec.tensor_copy(cnt[:, 0, :], b[:, 160:192]))
                mark(vec.tensor_copy(load_i, b[0:1, 160:192]))
                step(vec.tensor_scalar(T_, c, float(CAP), None, ALU.is_ge))
                for k in range(2, 5):
                    step(vec.scalar_tensor_tensor(T_, c, float(CAP * k), T_, ALU.is_ge, ALU.add))
                B = blk[:, 0:nt, :]
                mark(vec.scalar_tensor_tensor(A, T_, float(-CAP), c, ALU.mult, ALU.add))
                mark(vec.tensor_tensor(B, T_, spread(expert_of[:], 1, nt), ALU.add))
                step(vec.tensor_scalar(cnt[:, 1, :], cnt[:, 0, :], float(CAP), None, ALU.is_gt))
                for k in range(2, 5):
                    step(vec.scalar_tensor_tensor(cnt[:, 1, :], cnt[:, 0, :], float(CAP * k), cnt[:, 1, :], ALU.is_gt, ALU.add))
                step(vec.tensor_tensor_scan(cnt[:, 2, :], cnt[:, 1, :], cnt[:, 3, :], 0.0, ALU.add, ALU.add))
                step(vec.tensor_tensor(cnt[:, 0, :], cnt[:, 2, :], cnt[:, 1, :], ALU.subtract))
                step(vec.scalar_tensor_tensor(cnt[:, 0, :], cnt[:, 0, :], float(NE - 1), expert_of[:], ALU.add, ALU.subtract))
                free(vec.scalar_tensor_tensor(T_, c, float(CAP), spread(cnt[:, 0, :], 1, nt), ALU.is_ge, ALU.mult), name)
                taken(vec, name)
                step(vec.tensor_tensor(B, B, T_, ALU.add))
                for k, oh in enumerate((oh1, oh2)):
                    mark(vec.tensor_tensor(picked[:, k, 0:nt, :], oh[:, 0:nt, :], A, ALU.mult))
                    mark(vec.tensor_tensor(oh[:, 0:nt, :], oh[:, 0:nt, :], B, ALU.mult))
                settle()
                for k, oh in enumerate((oh1, oh2)):
                    mark(vec.tensor_reduce(row_of[:, 0:nt, k], picked[:, k, 0:nt, :], AX.X, ALU.add))
                    mark(vec.tensor_reduce(block_of[:, 0:nt, k], oh[:, 0:nt, :], AX.X, ALU.add))
                settle()
                vec.wait_ge(numbers_set, 2)
                for i in range(2 * nt):
                    t, k = i // 2, i % 2
                    mark(vec.tensor_scalar(row_hot[:, i, :], column_no, row_of[:, t, k:k + 1], None, ALU.is_equal))
                    vec.tensor_scalar(block_hot[:, i, :], column_no[:, 0:NBLK], block_of[:, t, k:k + 1], assign_no[:, i:i + 1],
                                      ALU.is_equal, ALU.mult).then_inc(hot_ready, 1)
                name = f"table{l}"
                done(vec, name)
                step(vec.tensor_scalar(emptied, job_bank(name, NBLK), 0.0, float(EMPTY), ALU.is_equal, ALU.mult))
                free(vec.scalar_tensor_tensor(slot_ids[:], job_bank(name, NBLK), -1.0, emptied, ALU.add, ALU.add), name)
                taken(vec, name)
                vec.tensor_scalar(slot_tok[:], slot_ids[:], 1, None, ALU.arith_shift_right).then_inc(tok_ready, 1)
                ovt = at(RT + 480, NOVER * NE)[0:1, :].rearrange("p (j e) -> p j e", e=NE)
                step(vec.tensor_tensor(ovt, spread(cnt[0:1, 2, :], 1, NOVER), spread(expert_of[0:1, 0:NOVER], 2, NE), ALU.is_le))
                mark(vec.tensor_copy(ovf[0:1, 8:9], cnt[0:1, 2, NE - 1:NE]))
                step(vec.tensor_reduce(ovf[0:1, 0:8], ovt, AX.X, ALU.add))
                step(vec.tensor_scalar(ovf[0:1, 0:8], ovf[0:1, 0:8], float(NE - 1), None, ALU.min))
                vec.tensor_copy(over_i[0:1, 0:9], ovf[0:1, 0:9]).then_inc(route_ready, 1)

            def expert(l, e, par):
                E = NE * l + e
                vec.wait_ge(tanh_ready, E + 1)
                vec.scalar_tensor_tensor(zg[par], zg[par], 1.0, ps[:, 2 + 2 * par, :], ALU.add, ALU.mult).then_inc(zg_ready, 1)
                vec.wait_ge(zg_ready, E + 1)
                vec.wait_ge(up_ready, E + 1)
                if not (isinstance(E, int) and E < 2):
                    vec.wait_ge(y_ready, E - 1)
                up = ps[:, 3 + 2 * par, :].rearrange("p (c t) -> p c t", t=P)
                z = zg[par].rearrange("p (c t) -> p c t", t=P)
                for h in range(2):
                    f = slice(2 * h, 2 * h + 2)
                    vec.scalar_tensor_tensor(hb[par][:, f, :], z[:, f, :], 0.5, up[:, f, :], ALU.mult, ALU.mult).then_inc(hb_ready, 1)

            def experts(l):
                expert(l, 0, 0)
                expert(l, 1, 1)
                alpha(l)
                with vec.Fori(1, NE // 2) as i:
                    expert(l, i * 2, 0)
                    expert(l, i * 2 + 1, 1)
                o = ov[l]
                n_over = vec.value_load(over_i[0:1, 8:9], min_val=0, max_val=NOVER)
                vec.wait_ge(y_ready, NE * (l + 1))
                for j in range(NOVER):
                    with vec.If(n_over > j):
                        vec.wait_ge(o["t"], j + 1)
                        vec.scalar_tensor_tensor(zg[0], zg[0], 1.0, ps[:, 2, :], ALU.add, ALU.mult).then_inc(o["z"], 1)
                        vec.wait_ge(o["z"], j + 1)
                        vec.wait_ge(o["g"], 2 * j + 2)
                        vec.scalar_tensor_tensor(hb[0], zg[0].rearrange("p (c t) -> p c t", t=P), 0.5,
                                                 ps[:, 3, :].rearrange("p (c t) -> p c t", t=P), ALU.mult, ALU.mult)\
                           .then_inc(o["h"], 1)
                    with vec.Else():
                        vec.nop()

            def alpha(l):
                vec.wait_ge(h_out, 16 * (5 if l == 0 else 9))
                for t in range(5 if l == 0 else 4):
                    r = rows_of(t)
                    vec.tensor_scalar(X[0:r, t, :], X[0:r, t, :], ALPHA, None, ALU.mult).then_inc(alpha_done, 1)

            def combine(l, t):
                n = COMBINED[(3 + 2 * l, t)]
                r = rows_of(t)
                x, y = X[0:r, t, :], yin[t][0:r]
                vec.wait_ge(alpha_done, 5 if l == 0 else 9)
                vec.wait_ge(yin_in[t], 16 * (l + 1))
                step(vec.scalar_tensor_tensor(x, y[:, 0, :], gates[0:r, 0, t:t + 1], x, ALU.mult, ALU.add))
                vec.scalar_tensor_tensor(x, y[:, 1, :], gates[0:r, 1, t:t + 1], x, ALU.mult, ALU.add).then_inc(comb_done, 1)
                vec.wait_ge(comb_done, n + 1)
                normalise(3 + 2 * l, t)

            route(0)
            experts(0)
            finish_and_turn(4, (4, 0, 1, 2, 3), lambda t: combine(0, t), lag=2)

            for c in range(DC):
                z = zpad[c % 2]
                taken(vec, f"cg_{c}")
                done(vec, f"cv_{c}")
                free(vec.tensor_tensor(halves(z), halves(cgs[c % 2]), job_pair(f"cv_{c}", 257), ALU.mult), f"cv_{c}")
                taken(vec, f"cv_{c}")
                y = zT[:, c, :]
                tap = lambda k: cols[:, SC0 + 8 * k + c:SC0 + 8 * k + c + 1]
                step(vec.tensor_scalar(y, z[:, 0:S], tap(0), None, ALU.mult))
                for k in (1, 2):
                    step(vec.scalar_tensor_tensor(y, z[:, k:S + k], tap(k), y, ALU.mult, ALU.add))
                done(vec, f"bg_{c}")
                free(vec.tensor_tensor(y, y, job_bank(f"bg_{c}"), ALU.mult), f"bg_{c}")
            clear_routing()
            finish_and_turn(5, range(NT), lambda t: residual(4, t, f"outD_{t}"), logits(1))
            route(1)
            experts(1)
            for t in range(NT):
                combine(1, t)
            affine_last(5, 3)

        @block.gpsimd
        def _(pool):
            own = [0]

            def mark(ins):
                own[0] += 1
                ins.then_inc(pool_own, 1)

            def settle():
                pool.wait_ge(pool_own, own[0])

            mark(pool.memset(ident[:], 0.0))
            mark(pool.memset(before[:], 1.0))
            mark(pool.memset(ones[:], 1.0))
            settle()
            pool.affine_select(out=ident[:], in_=ident[:], compare_op=ALU.not_equal, fill=1.0, base=0,
                               pattern=[[-1, P]], channel_multiplier=1).then_inc(pool_set, 1)
            pool.memset(ones_h[:], 1.0).then_inc(pool_set, 1)
            pool.affine_select(out=before[:], in_=before[:], compare_op=ALU.is_gt, fill=0.0, base=0,
                               pattern=[[1, P]], channel_multiplier=-1).then_inc(pool_set, 1)
            pool.wait_ge(pool_set, 3)
            pool.memset(relb[NB:NB + 1, :], NEG).then_inc(prow_set, 1)
            pool.wait_ge(prow_set, 1)
            mark(pool.iota(expert_of[:], pattern=[[1, NE]], base=0, channel_multiplier=0, allow_small_or_imprecise_dtypes=True))
            mark(pool.iota(group_of[:], pattern=[[1, NG], [0, EPG]], base=0, channel_multiplier=0, allow_small_or_imprecise_dtypes=True))
            settle()

            taken(pool, "toep1")
            taken(pool, "toep2")
            pool.dma_start(bvec, brow[0:HPG, :, :]).then_inc(bvec_out, 16)
            pool.wait_ge(bvec_out, 16)
            pool.dma_start(bias0, bass.AP(bvec.tensor, 0, [[1, P], [1536, HPG], [1, 384]])).then_inc(toep_in, 16)
            for g in (1, 2):
                pool.dma_start(bias12[g - 1], bass.AP(bvec.tensor, 512 * g + P, [[1, P], [1536, HPG], [1, P]])).then_inc(toep_in, 16)

            LNP = [(a["ln_g"][0], a["ln_b"][0]), (a["ln_g"][1], a["ln_b"][1])] + [
                (a["ln_g_2"][l, i], a["ln_b_2"][l, i]) for l in range(2) for i in range(2)]

            def load_lnp(l):
                for i in range(2):
                    v = LNP[l][i]
                    pool.dma_start(lnp[:, i, :], bass.AP(v.tensor, v.offset, [[0, P], [1, D]])).then_inc(lnp_in, 16)

            def affine(l, t):
                n = LN[(l, t)]
                if t == NT - 1:
                    pool.wait_ge(ln_done, n + 1)
                    return
                r = rows_of(t)
                x = X[0:r, t, :]
                pool.wait_ge(normed, n + 1)
                mark(pool.tensor_tensor(x, x, lnp[0:r, 0, :], ALU.mult))
                settle()
                pool.tensor_tensor(x, x, lnp[0:r, 1, :], ALU.add).then_inc(ln_done, 1)
                pool.wait_ge(ln_done, n + 1)

            done(pool, "fac_8")
            load_lnp(0)
            pool.wait_ge(pv_done, NUA)
            pool.dma_start(X[:, 0:NT, :], a["x"][0].rearrange("(t p) d -> p t d", p=P)).then_inc(x_back, 16)
            pool.wait_ge(factors_ready, 1)
            pool.wait_ge(lnp_in, 32)
            for t in range(NT):
                affine(0, t)
                pool.dma_start(x1_d[P * t:P * (t + 1), :], X[:, t, :]).then_inc(x1_out, 16)
            pool.dma_start(rot, a["rotary"]).then_inc(rot_in, 16)
            load_lnp(1)
            pool.wait_ge(rot_in, 16)
            for h in range(HB):
                q, other = qB[h % 4][NOPE:QW, :], q_swap[NOPE:QW, :]
                pool.wait_ge(q_swapped, h + 1)
                mark(pool.tensor_tensor(other, other, rot[NOPE:QW, 1, :], ALU.mult))
                mark(pool.tensor_tensor(q, q, rot[NOPE:QW, 0, :], ALU.mult))
                settle()
                pool.tensor_tensor(q, q, other, ALU.add).then_inc(qr_ready, 1)
            pool.wait_ge(pv_done, NUA + NUB)
            pool.wait_ge(x1_out, 64)
            pool.dma_start(X[:, 0:NT, :], x1_d.rearrange("(t p) d -> p t d", p=P)).then_inc(x1_back, 16)
            pool.dma_start(meta_x[0:META, :], a["meta_tokens_2"]).then_inc(meta_in, 16)

            def load_bd(c):
                if c >= 2:
                    done(pool, f"ri_{c - 2}")
                for i, w in enumerate((a["lru_w_a_2"], a["lru_w_i_2"])):
                    for h in range(2):
                        s = slice(64 * h, 64 * h + 64)
                        pool.dma_start(wa_bd[s, c % 2, i, s], w[0, 2 * c + h]).then_inc(bd_in[c % 2], 16)

            mark(pool.memset(wa_bd, 0.0))
            settle()
            load_bd(0)
            load_bd(1)
            pool.wait_ge(lnp_in, 64)
            for t in range(NT):
                affine(1, t)
            load_lnp(2)
            for c in range(2, DC):
                load_bd(c)
            pool.wait_ge(yT_ready, DC)
            pool.iota(column_no, pattern=[[1, CAP]], base=0, channel_multiplier=0, allow_small_or_imprecise_dtypes=True)\
                .then_inc(numbers_set, 1)
            pool.iota(assign_no, pattern=[[2 * P, 5], [1, 2]], base=1, channel_multiplier=2, allow_small_or_imprecise_dtypes=True)\
                .then_inc(numbers_set, 1)
            for l in range(2):
                pool.dma_start(rw[:, l, :, 0:NG], a["moe_w_group_2"][l].rearrange("(c p) n -> p c n", p=P)).then_inc(rw_in, 16)
                pool.dma_start(rw[:, l, :, NG:36], a["moe_w_expert_2"][l].rearrange("(c p) n -> p c n", p=P)).then_inc(rw_in, 16)
                vg, ve = a["moe_b_group_2"][l], a["moe_b_expert_2"][l]
                pool.dma_start(rb[:, l, 0:NG], bass.AP(vg.tensor, vg.offset, [[0, P], [1, NG]])).then_inc(rw_in, 16)
                pool.dma_start(rb[:, l, NG:36], bass.AP(ve.tensor, ve.offset, [[0, P], [1, NE]])).then_inc(rw_in, 16)

            def rows_out(l, t):
                r0 = P * t
                pool.dma_start(h_d[l][r0:r0 + rows_of(t), :], X[0:rows_of(t), t, :]).then_inc(h_out, 16)

            def by_load(e, rows):
                load = pool.value_load(load_i[0:1, e:e + 1], min_val=0, max_val=TM)
                with pool.If(load > CAP // 2):
                    rows(CAP)
                with pool.Else():
                    rows(CAP // 2)

            def gather(l, e):
                E = NE * l + e
                if E >= 2:
                    pool.wait_ge(xe_used, E - 1)
                def rows(n):
                    pool.indirect_dma_start(out=xe[e % 2][0:n], out_offset=None, in_=h_d[l],
                                            in_offset=bass.IndirectOffsetOnAxis(ap=slot_tok[0:n, e:e + 1], axis=0),
                                            bounds_check=(TM if l == 0 else S) - 1, oob_is_err=False).then_inc(xe_landed[e % 2], 16)
                by_load(e, rows)

            def scatter(l, e):
                pool.wait_ge(yo_ready, NE * l + e + 1)
                def rows(n):
                    pool.indirect_dma_start(out=ya_d[l], out_offset=bass.IndirectOffsetOnAxis(ap=slot_ids[0:n, e:e + 1], axis=0),
                                            in_=yo[e % 2][0:n], in_offset=None, bounds_check=2 * (TM if l == 0 else S) - 1,
                                            oob_is_err=False).then_inc(yo_sent[e % 2], 16)
                by_load(e, rows)

            def experts(l):
                tiles = range(5 if l == 0 else 4)
                pool.wait_ge(tok_ready, l + 1)
                pool.wait_ge(h_out, 16 * (5 if l == 0 else 9))
                gather(l, 0)
                for e in range(NE):
                    if e + 1 < NE:
                        gather(l, e + 1)
                    scatter(l, e)
                for par in range(2):
                    pool.wait_ge(yo_sent[par], 8 * NE * (l + 1))
                o = ov[l]
                pool.wait_ge(route_ready, l + 1)
                n_over = pool.value_load(over_i[0:1, 8:9], min_val=0, max_val=NOVER)
                for j in range(NOVER):
                    with pool.If(n_over > j):
                        b = NE + j
                        pool.indirect_dma_start(out=xe[0], out_offset=None, in_=h_d[l],
                                                in_offset=bass.IndirectOffsetOnAxis(ap=slot_tok[:, b:b + 1], axis=0),
                                                bounds_check=(TM if l == 0 else S) - 1, oob_is_err=False).then_inc(o["x"], 16)
                        pool.wait_ge(o["yo"], j + 1)
                        pool.indirect_dma_start(out=ya_d[l], out_offset=bass.IndirectOffsetOnAxis(ap=slot_ids[:, b:b + 1], axis=0),
                                                in_=yo[0], in_offset=None, bounds_check=2 * (TM if l == 0 else S) - 1,
                                                oob_is_err=False).then_inc(o["out"], 16)
                        pool.wait_ge(o["out"], 16 * (j + 1))
                    with pool.Else():
                        pool.nop()

            def combined(l, order):
                for t in order:
                    r = rows_of(t)
                    pool.dma_start(yin[t][0:r], ya_d[l][2 * P * t:2 * P * t + 2 * r, :].rearrange("(p k) d -> p k d", k=2))\
                        .then_inc(yin_in[t], 16)
                pool.wait_ge(lnp_in, 32 * (4 + 2 * l))
                for t in order:
                    affine(3 + 2 * l, t)
                    if l == 1:
                        pool.dma_start(out[0, P * t:P * (t + 1), :], X[:, t, :]).then_inc(out_sent, 16)

            pool.wait_ge(lnp_in, 96)
            for t in (4, 0, 1, 2, 3):
                affine(2, t)
                rows_out(0, t)
            load_lnp(3)
            experts(0)
            combined(0, (4, 0, 1, 2, 3))
            load_lnp(4)
            pool.wait_ge(lnp_in, 32 * 5)
            for t in range(NT):
                affine(4, t)
                rows_out(1, t)
            load_lnp(5)
            experts(1)
            combined(1, (0, 1, 2, 3))
            pool.wait_ge(out_sent, 64)


_INS = ["x", "c", "rel_bias", "ada_w", "ada_b", "ln_g", "ln_b", "a_w_in", "a_w_out", "b_w_in", "b_q_norm", "b_w_uq",
        "b_kv_norm", "b_w_ukv", "b_w_out", "meta_tokens_2", "lru_w_in_2", "lru_conv_w_2", "lru_conv_b_2", "lru_w_a_2",
        "lru_b_a_2", "lru_w_i_2", "lru_b_i_2", "lru_lambda_2", "lru_w_out_2", "sc_w_in_2", "sc_conv_w_2", "sc_w_out_2",
        "moe_w_group_2", "moe_b_group_2", "moe_w_expert_2", "moe_b_expert_2", "moe_w_gate_2", "moe_w_up_2",
        "moe_w_down_2", "ln_g_2", "ln_b_2"]


def kernel(**inputs):
    import numpy as _np
    import concourse.bacc as _bacc
    from concourse import mybir as _mybir
    from concourse.bass_utils import run_bass_kernel_spmd as _run

    nc = _bacc.Bacc("TRN2", target_bir_lowering=False, num_devices=1)
    arrays, aps = {}, {}
    given = {n: inputs[n] for n in _INS}
    given.update(constants())
    for name, value in given.items():
        v = _np.ascontiguousarray(value)
        arrays[f"in_{name}_dram"] = v
        aps[name] = nc.dram_tensor(f"in_{name}_dram", v.shape, _mybir.dt.from_np(v.dtype), kind="ExternalInput").ap()
    out = nc.dram_tensor("out_0_dram", (1, S, D), F32, kind="ExternalOutput").ap()
    build(nc, aps, out)
    r = _run(nc, [arrays], core_ids=[0])
    return r.results[0]["out_0_dram"]
```
